# Optimizing a Trainium2 kernel written in Bass

```python
import math
import jax
import jax.numpy as jnp
from jax import lax
import numpy as np

D_MODEL = 1024
BATCH = 1
SEQ = 512
DEPTH = 2
DEC_BATCH = 8
DEC_SEQ = 1
PAST_LEN = 2048
PAGE_SIZE = 128

HEAD_DIM = 64
N_HEADS_A = D_MODEL // 256
N_HEADS_B = D_MODEL // 256
N_HEADS_C = D_MODEL // 256
DK_B = 128
DV_B = 128
DIL_PATTERNS = ((128, 1), (512, 4), (2048, 16))
WIN_MAX = 2048
ROPE_THETA = 10000.0
CONV_K = 4
DELTA_CHUNK = 64
SB_BLOCK = 128
SB_QK_SCALE = 0.3
PEER_HEADS = 8
PEER_KEYS = 128
PEER_TOPK = 16
PEER_KEY_DIM = 128
PEER_EXPERTS = PEER_KEYS * PEER_KEYS
PEER_BLOCK = 128
RMS_EPS = 1e-6
A_W = N_HEADS_A * HEAD_DIM
B_QK = N_HEADS_B * DK_B
B_V = N_HEADS_B * DV_B
C_W = N_HEADS_C * HEAD_DIM
CONV_CH = 2 * B_QK + B_V
IN_SPLITS = (A_W, A_W, A_W, B_QK, B_QK, B_V, B_V, N_HEADS_B, N_HEADS_B, C_W, C_W, C_W)
N_IN = 3 * A_W + 2 * B_QK + 2 * B_V + 2 * N_HEADS_B + 3 * C_W

kernel_name = 'hybrid_dilated_delta_stickbreak_peer_step'

def rms_norm(x, g):
    xf = x.astype(jnp.float32)
    y = xf * lax.rsqrt(jnp.mean(xf * xf, axis=-1, keepdims=True) + RMS_EPS)
    return y.astype(x.dtype) * g

def l2_norm(x):
    return x * lax.rsqrt(jnp.sum(x * x, axis=-1, keepdims=True) + 1e-6)

def split_cols(a, sizes):
    out, start = [], 0
    for s in sizes:
        out.append(a[..., start:start + s])
        start += s
    return out

def rope(x, pos):
    half = x.shape[-1] // 2
    inv = ROPE_THETA ** (-jnp.arange(half, dtype=jnp.float32) / half)
    ang = pos.astype(jnp.float32)[:, None] * inv[None, :]
    cos = jnp.cos(ang)[None, :, None, :]
    sin = jnp.sin(ang)[None, :, None, :]
    xf = x.astype(jnp.float32)
    x1, x2 = xf[..., :half], xf[..., half:]
    return jnp.concatenate([x1 * cos - x2 * sin, x2 * cos + x1 * sin], axis=-1)

def dilated_window_prompt(q, k, v, window, dilation):
    B, S, H, Dh = q.shape
    reach = window // dilation
    n_sub = -(-S // dilation)
    nb = -(-n_sub // reach)
    pad = nb * reach * dilation - S

    def blocks(a):
        a = jnp.pad(a.astype(jnp.float32), ((0, 0), (0, pad), (0, 0), (0, 0)))
        return a.reshape(B, nb, reach, dilation, H, Dh)

    def with_prev(a):
        prev = jnp.pad(a, ((0, 0), (1, 0), (0, 0), (0, 0), (0, 0), (0, 0)))[:, :nb]
        return jnp.concatenate([prev, a], axis=2)

    qb = blocks(q)
    kk = with_prev(blocks(k))
    vv = with_prev(blocks(v))
    s = jnp.einsum('bnirhd,bnjrhd->bnrhij', qb, kk) * (Dh ** -0.5)
    qi = jnp.arange(reach)[:, None]
    kj = jnp.arange(2 * reach)[None, :]
    band = (kj >= qi) & (kj <= qi + reach)
    blk_id = jnp.arange(nb)[:, None, None]
    valid = band[None] & ((blk_id > 0) | (kj[None] >= reach))
    s = jnp.where(valid[None, :, None, None], s, -jnp.inf)
    m = jnp.max(s, axis=-1, keepdims=True)
    e = jnp.exp(s - m)
    den = jnp.sum(e, axis=-1)
    o = jnp.einsum('bnrhij,bnjrhd->bnirhd', e, vv)
    den_t = jnp.transpose(den, (0, 1, 4, 2, 3))
    o = o / den_t[..., None]
    lse = jnp.transpose(m[..., 0], (0, 1, 4, 2, 3)) + jnp.log(den_t)
    o = o.reshape(B, nb * reach * dilation, H, Dh)[:, :S]
    lse = lse.reshape(B, nb * reach * dilation, H)[:, :S]
    return o, lse

def dilated_window_decode(q, k_all, v_all, n_buf, window, dilation):
    B, T, H, Dh = q.shape
    steps = jnp.arange(window // dilation + 1)
    idx = n_buf + jnp.arange(T)[:, None] - dilation * steps[None, :]
    valid = idx >= 0
    idx = jnp.maximum(idx, 0)
    kg = k_all[:, idx].astype(jnp.float32)
    vg = v_all[:, idx].astype(jnp.float32)
    s = jnp.einsum('bthd,btjhd->bhtj', q.astype(jnp.float32), kg) * (Dh ** -0.5)
    s = jnp.where(valid[None, None], s, -jnp.inf)
    m = jnp.max(s, axis=-1, keepdims=True)
    e = jnp.exp(s - m)
    den = jnp.sum(e, axis=-1)
    den_t = jnp.transpose(den, (0, 2, 1))
    o = jnp.einsum('bhtj,btjhd->bthd', e, vg) / den_t[..., None]
    lse = jnp.transpose(m[..., 0], (0, 2, 1)) + jnp.log(den_t)
    return o, lse

def merge_by_denominator(branches):
    o = jnp.stack([b[0] for b in branches])
    lse = jnp.stack([b[1] for b in branches])
    w = jax.nn.softmax(lse, axis=0)
    return jnp.sum(w[..., None] * o, axis=0)

def causal_conv(u, prev, w):
    full = jnp.concatenate([prev.astype(jnp.float32), u.astype(jnp.float32)], axis=1)
    out = lax.conv_general_dilated(full, w.astype(jnp.float32)[:, None, :], window_strides=(1,),
                                   padding='VALID', dimension_numbers=('NWC', 'WIO', 'NWC'),
                                   feature_group_count=full.shape[-1])
    return out, full[:, full.shape[1] - (CONV_K - 1):]

def gated_delta_chunked(q, k, v, g, beta, state0):
    f32 = jnp.float32
    B, T, H, Dk = q.shape
    Dv = v.shape[-1]
    C = DELTA_CHUNK
    nc = -(-T // C)
    pad = nc * C - T
    q = l2_norm(q.astype(f32)) * (Dk ** -0.5)
    k = l2_norm(k.astype(f32))

    def to_chunks(a):
        a = jnp.pad(a.astype(f32), [(0, 0), (0, pad)] + [(0, 0)] * (a.ndim - 2))
        a = a.reshape((B, nc, C) + a.shape[2:])
        return jnp.moveaxis(a, 3, 1)

    qc, kc, vc, gch, bch = to_chunks(q), to_chunks(k), to_chunks(v), to_chunks(g), to_chunks(beta)
    gc = jnp.cumsum(gch, axis=-1)
    i = jnp.arange(C)
    lower = i[:, None] >= i[None, :]
    strict = i[:, None] > i[None, :]
    diff = gc[..., :, None] - gc[..., None, :]
    decay = jnp.where(lower, jnp.exp(jnp.where(lower, diff, 0.0)), 0.0)
    kb = kc * bch[..., None]
    vb = vc * bch[..., None]
    m_low = jnp.where(strict, jnp.einsum('bhncd,bhnsd->bhncs', kb, kc) * decay, 0.0)
    eye = jnp.eye(C, dtype=f32)
    t_inv = lax.linalg.triangular_solve(eye + m_low, jnp.broadcast_to(eye, m_low.shape),
                                        left_side=True, lower=True)
    u = t_inv @ vb
    w = t_inv @ (kb * jnp.exp(gc)[..., None])
    intra = jnp.where(lower, jnp.einsum('bhncd,bhnsd->bhncs', qc, kc) * decay, 0.0)
    xs = tuple(jnp.moveaxis(a, 2, 0) for a in (qc, kc, u, w, intra, gc))

    def step(S, inp):
        qn, kn, un, wn, an, gn = inp
        v_new = un - wn @ S
        o = (qn * jnp.exp(gn)[..., None]) @ S + an @ v_new
        gl = gn[..., -1]
        S = S * jnp.exp(gl)[..., None, None] + jnp.einsum(
            'bhcd,bhce->bhde', kn * jnp.exp(gl[..., None] - gn)[..., None], v_new)
        return S, o

    S, o = lax.scan(step, state0.astype(f32), xs)
    o = jnp.transpose(o, (1, 0, 3, 2, 4)).reshape(B, nc * C, H, Dv)[:, :T]
    return o, S

def stick_break_attend(q, k, v, q_pos, k_pos):
    z = jnp.einsum('bqhd,bkhd->bhqk', q, k).astype(jnp.float32) * (q.shape[-1] ** -0.5)
    causal = k_pos[None, :] < q_pos[:, None]
    log_keep = jnp.where(causal, jax.nn.log_sigmoid(-z), 0.0)
    between = lax.cumsum(log_keep, axis=3, reverse=True) - log_keep
    w = jnp.where(causal, jnp.exp(jax.nn.log_sigmoid(z) + between), 0.0)
    return jnp.einsum('bhqk,bkhd->bqhd', w, v.astype(jnp.float32))

def stick_breaking_prompt(q, k, v):
    B, S, H, Dh = q.shape
    nb = S // SB_BLOCK
    qb = jnp.moveaxis(q.reshape(B, nb, SB_BLOCK, H, Dh), 1, 0)
    k_pos = jnp.arange(S)

    def block(args):
        q_blk, blk_i = args
        return stick_break_attend(q_blk, k, v, blk_i * SB_BLOCK + jnp.arange(SB_BLOCK), k_pos)

    o = lax.map(block, (qb, jnp.arange(nb)))
    return jnp.moveaxis(o, 0, 1).reshape(B, S, H, Dh)

def peer_ffn(h, wq, sub_keys, u_tab, v_tab):
    B, T, D = h.shape
    n = B * T
    x = h.reshape(n, D)
    q = (x @ wq).reshape(n, PEER_HEADS, 2, PEER_KEY_DIM // 2)
    s = jnp.einsum('nhpk,hpek->nhpe', q, sub_keys).astype(jnp.float32)
    s1, i1 = lax.top_k(s[:, :, 0], PEER_TOPK)
    s2, i2 = lax.top_k(s[:, :, 1], PEER_TOPK)
    cand_s = (s1[..., :, None] + s2[..., None, :]).reshape(n, PEER_HEADS, PEER_TOPK * PEER_TOPK)
    cand_i = (i1[..., :, None] * PEER_KEYS + i2[..., None, :]).reshape(n, PEER_HEADS, PEER_TOPK * PEER_TOPK)
    top_s, pick = lax.top_k(cand_s, PEER_TOPK)
    idx = jnp.take_along_axis(cand_i, pick, axis=-1).reshape(n, PEER_HEADS * PEER_TOPK)
    gate = jax.nn.softmax(top_s, axis=-1).reshape(n, PEER_HEADS * PEER_TOPK)
    blk = min(PEER_BLOCK, n)
    nb = -(-n // blk)
    pad = nb * blk - n
    xb = jnp.pad(x, ((0, pad), (0, 0))).reshape(nb, blk, D)
    ib = jnp.pad(idx, ((0, pad), (0, 0))).reshape(nb, blk, -1)
    gb = jnp.pad(gate, ((0, pad), (0, 0))).reshape(nb, blk, -1)

    def expert_block(args):
        xk, ik, gk = args
        act = jax.nn.gelu(jnp.einsum('nd,ned->ne', xk, u_tab[ik]).astype(jnp.float32), approximate=False)
        return jnp.einsum('ne,ned->nd', (gk * act).astype(v_tab.dtype), v_tab[ik])

    y = lax.map(expert_block, (xb, ib, gb)).reshape(nb * blk, D)[:n]
    return y.reshape(B, T, D).astype(h.dtype)

def hybrid_layer(x, c, pos, state, w_ada, b_ada, norm1_g, norm2_g, w_in, b_q_c, b_k_c, qnorm_a,
                 knorm_a, conv_w, a_log, dt_bias, gnorm_b, w_out, peer_wq, peer_keys, peer_u, peer_v):
    f32 = jnp.float32
    B, T, _ = x.shape
    mod = (jax.nn.silu(c) @ w_ada + b_ada)[:, None, :]
    sh1, sc1, gt1, sh2, sc2, gt2 = jnp.split(mod, 6, axis=-1)
    h = rms_norm(x, norm1_g) * (1.0 + sc1) + sh1
    qa, ka, va, qb, kb, vb, zb, bb, ab, qc, kc, vc = split_cols(h @ w_in, IN_SPLITS)

    def heads(a, n_h):
        return a.reshape(B, T, n_h, -1)

    qa = rope(rms_norm(heads(qa, N_HEADS_A), qnorm_a), pos)
    ka = rope(rms_norm(heads(ka, N_HEADS_A), knorm_a), pos)
    va = heads(va, N_HEADS_A)
    if state is None:
        branches = [dilated_window_prompt(qa, ka, va, wnd, dil) for wnd, dil in DIL_PATTERNS]
        keep = min(WIN_MAX, T)
        new_wk, new_wv = ka[:, T - keep:], va[:, T - keep:]
        conv_prev = jnp.zeros((B, CONV_K - 1, CONV_CH), f32)
        delta_prev = jnp.zeros((B, N_HEADS_B, DK_B, DV_B), f32)
    else:
        win_k, win_v, sb_k_past, sb_v_past, conv_prev, delta_prev = state
        k_all = jnp.concatenate([win_k, ka], axis=1)
        v_all = jnp.concatenate([win_v, va], axis=1)
        branches = [dilated_window_decode(qa, k_all, v_all, win_k.shape[1], wnd, dil)
                    for wnd, dil in DIL_PATTERNS]
        new_wk, new_wv = ka, va
    o_a = merge_by_denominator(branches).reshape(B, T, A_W)

    conv_out, new_conv = causal_conv(jnp.concatenate([qb, kb, vb], axis=-1), conv_prev, conv_w)
    qd, kd, vd = split_cols(jax.nn.silu(conv_out), (B_QK, B_QK, B_V))
    beta = jax.nn.sigmoid(bb.astype(f32))
    g = -jnp.exp(a_log.astype(f32)) * jax.nn.softplus(ab.astype(f32) + dt_bias.astype(f32))
    o_b, new_delta = gated_delta_chunked(heads(qd, N_HEADS_B), heads(kd, N_HEADS_B),
                                         heads(vd, N_HEADS_B), g, beta, delta_prev)
    o_b = (rms_norm(o_b, gnorm_b) * jax.nn.silu(heads(zb, N_HEADS_B).astype(f32))).reshape(B, T, B_V)

    qc = heads(qc + b_q_c, N_HEADS_C)
    kc = heads(kc + b_k_c, N_HEADS_C)
    vc = heads(vc, N_HEADS_C)
    if state is None:
        o_c = stick_breaking_prompt(qc, kc, vc)
    else:
        k_all_c = jnp.concatenate([sb_k_past, kc], axis=1)
        v_all_c = jnp.concatenate([sb_v_past, vc], axis=1)
        o_c = stick_break_attend(qc, k_all_c, v_all_c, pos, jnp.arange(k_all_c.shape[1]))
    o_c = o_c.reshape(B, T, C_W)

    mixed = jnp.concatenate([o_a, o_b, o_c], axis=-1).astype(x.dtype) @ w_out
    x = x + gt1 * mixed
    h2 = rms_norm(x, norm2_g) * (1.0 + sc2) + sh2
    x = x + gt2 * peer_ffn(h2, peer_wq, peer_keys, peer_u, peer_v)
    return x, (new_wk, new_wv, kc, vc, new_conv, new_delta)

def setup_inputs(seed: int = 0) -> dict:
    key = jax.random.key(seed)
    ks = jax.random.split(key, 30)
    f32 = jnp.float32
    n_pages = PAST_LEN // PAGE_SIZE
    n_used = DEC_BATCH * n_pages
    n_phys = n_used + n_used // 4
    win_buf = min(WIN_MAX, PAST_LEN)

    def nrm(k, shape, scale=1.0):
        return jax.random.normal(k, shape, f32) * scale

    dt = jnp.exp(jax.random.uniform(ks[20], (DEPTH, N_HEADS_B), f32, math.log(1e-3), math.log(1e-1)))
    page_table = jax.random.permutation(ks[8], n_phys)[:n_used].reshape(DEC_BATCH, n_pages).astype(jnp.int32)
    u_dir = nrm(ks[27], (DEPTH, N_HEADS_C, HEAD_DIM))
    u_dir = u_dir * lax.rsqrt(jnp.sum(u_dir * u_dir, axis=-1, keepdims=True))
    offsets = 2.0 * (1.0 + jnp.arange(N_HEADS_C, dtype=f32))
    amp = jnp.sqrt(offsets * math.sqrt(HEAD_DIM))[None, :, None]
    b_q_c = (amp * u_dir).reshape(DEPTH, C_W)
    b_k_c = (-amp * u_dir + nrm(ks[28], (DEPTH, N_HEADS_C, HEAD_DIM), 0.02)).reshape(DEPTH, C_W)
    col_scale = jnp.ones((N_IN,), f32).at[N_IN - 3 * C_W:N_IN - C_W].set(SB_QK_SCALE)
    sb_shape = (DEPTH, n_phys, PAGE_SIZE, N_HEADS_C, HEAD_DIM)
    cache_sb_k = b_k_c.reshape(DEPTH, 1, 1, N_HEADS_C, HEAD_DIM) + nrm(ks[4], sb_shape, SB_QK_SCALE)
    return {
        'x_prompt': nrm(ks[0], (BATCH, SEQ, D_MODEL)),
        'x_sample': nrm(ks[1], (DEC_BATCH, DEC_SEQ, D_MODEL)),
        'cache_win_k': nrm(ks[2], (DEPTH, DEC_BATCH, win_buf, N_HEADS_A, HEAD_DIM)),
        'cache_win_v': nrm(ks[3], (DEPTH, DEC_BATCH, win_buf, N_HEADS_A, HEAD_DIM)),
        'cache_sb_k': cache_sb_k,
        'cache_sb_v': nrm(ks[5], sb_shape),
        'state_conv': nrm(ks[6], (DEPTH, DEC_BATCH, CONV_K - 1, CONV_CH)),
        'state_delta': nrm(ks[7], (DEPTH, DEC_BATCH, N_HEADS_B, DK_B, DV_B), 0.1),
        'page_table': page_table,
        'c_prompt': nrm(ks[9], (BATCH, D_MODEL)),
        'c_sample': nrm(ks[10], (DEC_BATCH, D_MODEL)),
        'w_ada': nrm(ks[11], (DEPTH, D_MODEL, 6 * D_MODEL), 0.5 * D_MODEL ** -0.5),
        'b_ada': nrm(ks[12], (DEPTH, 6 * D_MODEL), 0.02),
        'norm1_g': 1.0 + nrm(ks[13], (DEPTH, D_MODEL), 0.02),
        'norm2_g': 1.0 + nrm(ks[14], (DEPTH, D_MODEL), 0.02),
        'w_in': nrm(ks[15], (DEPTH, D_MODEL, N_IN), D_MODEL ** -0.5) * col_scale,
        'b_q_c': b_q_c,
        'b_k_c': b_k_c,
        'qnorm_a': 1.0 + nrm(ks[16], (DEPTH, HEAD_DIM), 0.02),
        'knorm_a': 1.0 + nrm(ks[17], (DEPTH, HEAD_DIM), 0.02),
        'conv_w': nrm(ks[18], (DEPTH, CONV_K, CONV_CH), CONV_K ** -0.5),
        'a_log': jnp.log(jax.random.uniform(ks[19], (DEPTH, N_HEADS_B), f32, 1.0, 16.0)),
        'dt_bias': dt + jnp.log(-jnp.expm1(-dt)),
        'gnorm_b': 1.0 + nrm(ks[21], (DEPTH, DV_B), 0.02),
        'w_out': nrm(ks[22], (DEPTH, D_MODEL, D_MODEL), D_MODEL ** -0.5),
        'peer_wq': nrm(ks[23], (DEPTH, D_MODEL, PEER_HEADS * PEER_KEY_DIM), D_MODEL ** -0.5),
        'peer_keys': nrm(ks[24], (DEPTH, PEER_HEADS, 2, PEER_KEYS, PEER_KEY_DIM // 2), (PEER_KEY_DIM // 2) ** -0.5),
        'peer_u': nrm(ks[25], (DEPTH, PEER_EXPERTS, D_MODEL), D_MODEL ** -0.5),
        'peer_v': nrm(ks[26], (DEPTH, PEER_EXPERTS, D_MODEL), 0.3),
    }

def reference(x_prompt, x_sample, cache_win_k, cache_win_v, cache_sb_k, cache_sb_v, state_conv,
              state_delta, page_table, c_prompt, c_sample, w_ada, b_ada, norm1_g, norm2_g, w_in,
              b_q_c, b_k_c, qnorm_a, knorm_a, conv_w, a_log, dt_bias, gnorm_b, w_out, peer_wq,
              peer_keys, peer_u, peer_v):
    dec_batch, n_pages = page_table.shape
    past_len = n_pages * cache_sb_k.shape[2]
    pos_prompt = jnp.arange(x_prompt.shape[1])
    pos_sample = past_len + jnp.arange(x_sample.shape[1])
    yp, ys = x_prompt, x_sample
    st_prompt, st_sample = [], []
    for l in range(DEPTH):
        weights = (w_ada[l], b_ada[l], norm1_g[l], norm2_g[l], w_in[l], b_q_c[l], b_k_c[l],
                   qnorm_a[l], knorm_a[l], conv_w[l], a_log[l], dt_bias[l], gnorm_b[l], w_out[l],
                   peer_wq[l], peer_keys[l], peer_u[l], peer_v[l])
        yp, sp = hybrid_layer(yp, c_prompt, pos_prompt, None, *weights)
        past_k = cache_sb_k[l][page_table].reshape(dec_batch, past_len, N_HEADS_C, HEAD_DIM)
        past_v = cache_sb_v[l][page_table].reshape(dec_batch, past_len, N_HEADS_C, HEAD_DIM)
        state = (cache_win_k[l], cache_win_v[l], past_k, past_v, state_conv[l], state_delta[l])
        ys, ss = hybrid_layer(ys, c_sample, pos_sample, state, *weights)
        st_prompt.append(sp)
        st_sample.append(ss)

    def stack_layers(states, i):
        return jnp.stack([s[i] for s in states])

    win_k_prompt = stack_layers(st_prompt, 0)
    win_v_prompt = stack_layers(st_prompt, 1)
    win_k_sample = stack_layers(st_sample, 0)
    win_v_sample = stack_layers(st_sample, 1)
    sb_k_prompt = stack_layers(st_prompt, 2)
    sb_v_prompt = stack_layers(st_prompt, 3)
    sb_k_sample = stack_layers(st_sample, 2)
    sb_v_sample = stack_layers(st_sample, 3)
    conv_prompt = stack_layers(st_prompt, 4)
    conv_sample = stack_layers(st_sample, 4)
    delta_prompt = stack_layers(st_prompt, 5)
    delta_sample = stack_layers(st_sample, 5)
    return (yp, ys, win_k_prompt, win_v_prompt, win_k_sample, win_v_sample, sb_k_prompt, sb_v_prompt,
            sb_k_sample, sb_v_sample, conv_prompt, conv_sample, delta_prompt, delta_sample)


_drawn_inputs = setup_inputs


def setup_inputs(seed=0):
    import zlib

    import numpy as np

    out = dict(_drawn_inputs(seed))
    spreads = {}
    factors = {'cache_win_k': 3.148, 'norm2_g': 5.528, 'qnorm_a': 8.0, 'knorm_a': 2.862, 'gnorm_b': 8.0}
    for name, (base, spread) in spreads.items():
        noise = np.random.default_rng([zlib.crc32(name.encode()), seed]).standard_normal(out[name].shape)
        drawn = base * np.exp(spread * noise) if base else spread * noise
        out[name] = jnp.asarray(drawn.astype(out[name].dtype))
    for name, factor in factors.items():
        out[name] = (out[name] * factor).astype(out[name].dtype)
    return out
```

```python
from contextlib import ExitStack

import numpy as np

import concourse.bass as bass
from concourse import mybir

P = 128
D = 1024
KD = D // P
SEQ = 512
NT = SEQ // P
TILES = NT + 1
NB = 8
DEPTH = 2
HD = 64
NH = 4
AW = NH * HD
DK = 128
CONV_CH = 3 * NH * DK
CC = CONV_CH // P
KW = 4
N_IN = 3592
PAST = 2048
PAGES = PAST // P
PH = 8
PK = 128
TOPK = 16
EXPERTS = PK * PK
SLOTS = PH * TOPK
RMS_EPS = 1e-6
NEG = -30000.0
LEVELS = 7
MOD = 6 * D
GBLK = 512

F32 = mybir.dt.float32
I32 = mybir.dt.int32
U32 = mybir.dt.uint32
ALU = mybir.AluOpType
ACT = mybir.ActivationFunctionType
AX = mybir.AxisListType.X

CONST_COLS = [("ident", P), ("upper", P), ("neg_lower", P), ("ones", P), ("neg_ones", P),
              ("neg_mask", P), ("strict_upper", P), ("strict_lower", P), ("levels", LEVELS * P),
              ("log_count", SEQ), ("rope", TILES * 64), ("iota16", 16), ("pick_row", NB * P),
              ("replicate", P), ("gather8", NB), ("head_diag", AW), ("place", NB * NB),
              ("own_mask", 16), ("slot_of_row", 16), ("row8", P), ("eps", 8)]
CONST_AT = {}
_at = 0
for _n, _w in CONST_COLS:
    CONST_AT[_n] = (_at, _at + _w)
    _at += _w
CONST_W = _at


def constants():
    c = np.zeros((P, CONST_W), np.float32)

    def put(name, a):
        lo, _ = CONST_AT[name]
        a = np.asarray(a, np.float32)
        c[:a.shape[0], lo:lo + a.shape[1]] = a

    r = np.arange(P)
    put("ident", np.eye(P))
    put("upper", r[:, None] <= r[None, :])
    put("neg_lower", -(r[:, None] >= r[None, :]).astype(np.float32))
    put("ones", np.ones((P, P)))
    put("neg_ones", -np.ones((P, P)))
    put("neg_mask", np.where(r[:, None] >= r[None, :], NEG, 0.0))
    put("strict_upper", r[:, None] < r[None, :])
    put("strict_lower", r[:, None] > r[None, :])
    lv = []
    for k in range(LEVELS):
        b = 1 << k
        lv.append((r[:, None] // (2 * b) == r[None, :] // (2 * b)) & (r[:, None] // b == r[None, :] // b + 1))
    put("levels", np.concatenate(lv, 1))
    dist = r[:, None] + 384 - np.arange(SEQ)[None, :]
    cnt = np.zeros(dist.shape)
    for window, dil in ((128, 1), (512, 4), (2048, 16)):
        cnt += (dist >= 0) & (dist <= window) & (dist % dil == 0)
    put("log_count", np.where(cnt > 0, np.log(np.maximum(cnt, 1)), NEG))
    half = HD // 2
    inv = np.float32(10000.0) ** (-np.arange(half, dtype=np.float32) / np.float32(half))
    rope = np.zeros((P, TILES, 2, half), np.float32)
    for t in range(TILES):
        pos = (t * P + r if t < NT else np.full(P, PAST)).astype(np.float32)
        ang = (pos[:, None] * inv[None, :]).astype(np.float32)
        rope[:, t, 0] = np.cos(ang)
        rope[:, t, 1] = np.sin(ang)
    put("rope", rope.reshape(P, -1))
    put("iota16", np.tile(np.arange(16), (P, 1)))
    pick = np.zeros((NB, NB, P))
    for b in range(NB):
        pick[b, b] = 1
    put("pick_row", pick.reshape(NB, -1))
    put("replicate", (r[None, :] % NB) == np.arange(NB)[:, None])
    put("gather8", (r[:, None] % NB) == np.arange(NB)[None, :])
    put("head_diag", (np.arange(AW)[None, :] // HD) == np.arange(NH)[:, None])
    place = np.zeros((NH, NB, NB))
    for b in range(NB):
        place[:, b, b] = 1
    put("place", place.reshape(NH, -1))
    own = np.zeros((P, 4, NH))
    own[3:, 3, :] = NEG
    put("own_mask", own.reshape(P, 16))
    put("slot_of_row", (r[:, None] // NB) == np.arange(16)[None, :])
    row8 = np.zeros((NB + 1, P))
    row8[NB] = 1
    put("row8", row8)
    put("eps", np.full((P, 8), RMS_EPS))
    return c


class Arena:

    def __init__(self, sbuf, cols):
        self.sbuf, self.cols, self.at = sbuf, cols, 0

    def room(self, *dims, rows=P):
        n = int(np.prod(dims))
        lo = self.at
        self.at += (n + 7) // 8 * 8
        assert self.at <= self.cols, (self.at, self.cols)
        v = self.sbuf[0:rows, lo:lo + n]
        if len(dims) == 2:
            v = v.rearrange("p (a b) -> p a b", a=dims[0])
        if len(dims) == 3:
            v = v.rearrange("p (a b c) -> p a b c", a=dims[0], b=dims[1])
        return v


def bc(ap, axis, n):
    u = ap.unsqueeze(axis)
    return u.broadcast_to([n if i == axis else s for i, s in enumerate(u.shape)])


def build(nc, ins, outs):
    x_prompt, x_sample = ins["x_prompt"], ins["x_sample"]
    with ExitStack() as ctx:
        def sem(name):
            return ctx.enter_context(nc.semaphore(name))

        arena_cols = 52800
        AR = Arena(ctx.enter_context(nc.sbuf_tensor("arena", [P, arena_cols], F32)), arena_cols)
        ps = [ctx.enter_context(nc.psum_tensor(f"bank{i}", [P, GBLK], F32)) for i in range(8)]

        loaded = sem("loaded")
        loaded2 = sem("loaded2")
        w_landed = [sem(f"w_landed{i}") for i in range(3)]
        w_used = sem("w_used")
        w_used_act = sem("w_used_act")
        stored = sem("stored")
        dve_own = sem("dve_own")
        act_own = sem("act_own")
        pool_own = sem("pool_own")
        pe2dve = sem("pe2dve")
        pe2act = sem("pe2act")
        dve2pe = sem("dve2pe")
        act2pe = sem("act2pe")
        dve2act = sem("dve2act")
        act2dve = sem("act2dve")
        act_free = sem("act_free")
        dve_free = sem("dve_free")
        dve2sp = sem("dve2sp")
        act2sp = sem("act2sp")
        dve2pool = sem("dve2pool")
        pool2dve = sem("pool2dve")
        pool2pe = sem("pool2pe")
        ring_free = sem("ring_free")
        GR = 16
        LOT = 4
        gathered = [sem(f"gathered{i}") for i in range(GR)]

        def rsqrt(out, in_, scale):
            act_.activation(out, in_, ACT.Ln, scale=scale, bias=cst("eps")[0:in_.shape[0], 0:1]).then_inc(act_own, 1)
            act_.wait_ge(act_own, 1).then_inc(act_own, -1)
            return act_.activation(out, out, ACT.Exp, scale=-0.5)

        X = AR.room(TILES, D)
        CN = AR.room(CONST_W)
        MOD9 = AR.room(MOD)
        O = AR.room(TILES, D)
        CT = AR.room(KD, NB + 1)
        LB = AR.room(8)

        def cst(name, rows=P):
            lo, hi = CONST_AT[name]
            return CN[0:rows, lo:hi]

        ident = cst("ident")
        vec, act_, pe_ = nc.vector, nc.scalar, nc.tensor
        base_mark = AR.at

        C9 = AR.room(D)
        with nc.Block() as block:
            @block.sync
            def _(sp):
                sp.dma_start(CN, ins["consts"]).then_inc(loaded, 16)
                sp.dma_start(C9[0:NB, :], ins["c_sample"]).then_inc(loaded, 16)
                sp.dma_start(C9[NB:NB + 1, :], ins["c_prompt"]).then_inc(loaded, 16)
                sp.dma_start(X[:, 0:NT, :], x_prompt[0].rearrange("(t p) d -> p t d", p=P)).then_inc(loaded2, 16)
                sp.dma_start(X[0:NB, NT, :], x_sample.rearrange("b s d -> (b s) d")).then_inc(loaded2, 16)
                sp.wait_ge(loaded2, 32).then_inc(loaded2, -32)

            @block.vector
            def _(dve):
                vec.memset(LB, 0.0)

            @block.scalar
            def _(act):
                act.wait_ge(loaded, 48).then_inc(loaded, -48)
                act_.activation(C9[0:NB + 1, :], C9[0:NB + 1, :], ACT.Silu).then_inc(act2pe, 1)
                act.wait_ge(pe2act, 1).then_inc(pe2act, -1)
                act_.copy(CT, ps[0][:, 0:KD * (NB + 1)].rearrange("p (k n) -> p k n", k=KD))

            @block.tensor
            def _(pe):
                pe.wait_ge(act2pe, 1).then_inc(act2pe, -1)
                for k in range(KD):
                    last = pe_.transpose(ps[0][:, k * 9:k * 9 + 9], C9[0:9, k * P:(k + 1) * P], ident[0:9, 0:9])
                last.then_inc(pe2act, 1)
        AR.at = base_mark

        def modulation(l):
            mark = AR.at
            W = [AR.room(KD, GBLK) for _ in range(3)]
            BA = AR.room(MOD, rows=NB + 1)
            NG = AR.room(2, D, rows=NB + 1)
            wa = ins["w_ada"][l].rearrange("(k p) n -> p k n", p=P)
            R9 = NB + 1
            with nc.Block() as block:
                @block.sync
                def _(sp):
                    sp.dma_start(BA, ins["b_ada"][l].partition_broadcast(R9)).then_inc(loaded, 16)
                    sp.dma_start(NG[:, 0, :], ins["norm1_g"][l].partition_broadcast(R9)).then_inc(loaded, 16)
                    sp.dma_start(NG[:, 1, :], ins["norm2_g"][l].partition_broadcast(R9)).then_inc(loaded, 16)
                    for n in range(MOD // GBLK):
                        if n >= 3:
                            sp.wait_ge(w_used, 1).then_inc(w_used, -1)
                        sp.dma_start(W[n % 3], wa[:, :, n * GBLK:(n + 1) * GBLK]).then_inc(w_landed[n % 3], 16)
                    sp.wait_ge(w_used, 3).then_inc(w_used, -3)

                @block.tensor
                def _(pe):
                    for n in range(MOD // GBLK):
                        pe.wait_ge(w_landed[n % 3], 16).then_inc(w_landed[n % 3], -16)
                        if n >= 2:
                            pe.wait_ge(dve_free, 1).then_inc(dve_free, -1)
                        for k in range(KD):
                            last = pe_.matmul(ps[n % 2][0:R9, :], CT[:, k, :], W[n % 3][:, k, :],
                                              start=(k == 0), stop=(k == KD - 1))
                        last.then_inc(pe2dve, 1)
                    pe.wait_ge(dve_free, 2).then_inc(dve_free, -2)

                @block.vector
                def _(dve):
                    dve.wait_ge(loaded, 48).then_inc(loaded, -48)
                    for n in range(MOD // GBLK):
                        c = slice(n * GBLK, (n + 1) * GBLK)
                        dve.wait_ge(pe2dve, 1).then_inc(pe2dve, -1)
                        dve.sem_inc(w_used, 1)
                        vec.tensor_tensor(MOD9[0:R9, c], ps[n % 2][0:R9, :], BA[:, c], ALU.add).then_inc(dve_free, 1)
                    vec.memset(BA[:, 0:1], 0.0).then_inc(dve_own, 1)
                    vec.wait_ge(dve_own, 1).then_inc(dve_own, -1)
                    for i, s in enumerate((1, 4)):
                        seg = MOD9[0:R9, s * D:(s + 1) * D]
                        vec.scalar_tensor_tensor(seg, seg, 1.0, NG[:, i, :], ALU.add, ALU.mult)
            AR.at = mark

        def norm(shift, HT):
            mark = AR.at
            SEG = AR.room(2, D)
            SQ = AR.room(D)
            SS = AR.room(TILES)
            RS = AR.room(TILES)
            with nc.Block() as block:
                @block.tensor
                def _(pe):
                    for i in range(4):
                        c = (shift + i // 2) * D + (i % 2) * GBLK
                        last = pe_.matmul(ps[i][:, :], cst("row8", NB + 1), MOD9[0:NB + 1, c:c + GBLK], start=True, stop=True)
                    last.then_inc(pe2act, 1)
                    for t in range(TILES):
                        rows = P if t < NT else NB
                        pe.wait_ge(dve2pe, 1).then_inc(dve2pe, -1)
                        for half in range(2):
                            g = 2 * t + half
                            if g >= 4:
                                pe.wait_ge(act_free, 1).then_inc(act_free, -1)
                            bank = ps[4 + g % 4]
                            for j in range(4):
                                k = half * 4 + j
                                last = pe_.transpose(bank[:, j * P:j * P + rows], O[0:rows, t, k * P:(k + 1) * P], ident[0:rows, 0:rows])
                            last.then_inc(pe2act, 1)
                    pe.wait_ge(act_free, 4).then_inc(act_free, -4)

                @block.scalar
                def _(act):
                    for t in range(TILES):
                        rows = P if t < NT else NB
                        act_.activation(SQ[0:rows, :], X[0:rows, t, :], ACT.Square, accum_out=SS[0:rows, t:t + 1]).then_inc(act_own, 1)
                        act_.wait_ge(act_own, 1).then_inc(act_own, -1)
                    rsqrt(RS[:, 0:NT], SS[:, 0:NT], 1.0 / D)
                    rsqrt(RS[0:NB, NT:TILES], SS[0:NB, NT:TILES], 1.0 / D).then_inc(act2dve, 1)
                    act.wait_ge(pe2act, 1).then_inc(pe2act, -1)
                    for i in range(4):
                        last = act_.copy(SEG[:, i // 2, (i % 2) * GBLK:(i % 2 + 1) * GBLK], ps[i][:, :])
                    last.then_inc(act2dve, 1)
                    for t in range(TILES):
                        rows = P if t < NT else NB
                        for half in range(2):
                            g = 2 * t + half
                            act.wait_ge(pe2act, 1).then_inc(pe2act, -1)
                            act_.copy(HT[:, half * 4:half * 4 + 4, t * P:t * P + rows],
                                      ps[4 + g % 4][:, :].rearrange("p (j n) -> p j n", j=4)[:, :, 0:rows]).then_inc(act_free, 1)

                @block.vector
                def _(dve):
                    dve.wait_ge(act2dve, 2).then_inc(act2dve, -2)
                    for t in range(TILES):
                        rows = P if t < NT else NB
                        sh = SEG[:, 0, :] if t < NT else MOD9[0:NB, shift * D:(shift + 1) * D]
                        gn = SEG[:, 1, :] if t < NT else MOD9[0:NB, (shift + 1) * D:(shift + 2) * D]
                        h = O[0:rows, t, :]
                        vec.scalar_tensor_tensor(h, X[0:rows, t, :], RS[0:rows, t:t + 1], gn, ALU.mult, ALU.mult).then_inc(dve_own, 1)
                        vec.wait_ge(dve_own, 1).then_inc(dve_own, -1)
                        vec.tensor_tensor(h, h, sh, ALU.add).then_inc(dve2pe, 1)
            AR.at = mark

        def project(l, HT, PA, PC, PZ, BA, BT, DB):
            mark = AR.at
            W = [AR.room(KD, GBLK) for _ in range(2)]
            wi = ins["w_in"][l].rearrange("(k p) n -> p k n", p=P)
            chunks = [(0, 512, "a"), (512, 768, "a"), (768, 1280, "b"), (1280, 1792, "b"), (1792, 2304, "b"),
                      (2304, 2816, "z"), (2816, 3080, "g"), (3080, 3592, "c")]
            groups = []
            for n, (lo, hi, kind) in enumerate(chunks):
                mine = []
                if kind == "b":
                    mine += [(n, "feature", c, lo, hi) for c in range((lo - 768) // P, (hi - 768) // P)]
                    mine += [(n, "b", NT, lo, hi)]
                else:
                    mine += [(n, kind, t, lo, hi) for t in range(TILES)]
                groups += [g + (i == len(mine) - 1,) for i, g in enumerate(mine)]
            freed = [w_used_act if i % 2 == 0 else w_used for i, g in enumerate(groups) if g[5]]

            def result(g):
                _, kind, t, lo, hi, _ = g
                rows = P if kind == "feature" or t < NT else NB
                if kind == "feature":
                    return [(BT[:, t, 3:3 + SEQ], P, 0, SEQ)]
                if kind == "a":
                    return [(PA[0:rows, t, lo:hi], rows, 0, hi - lo)]
                if kind == "b":
                    return [(DB[0:NB, lo - 768:hi - 768], rows, 0, hi - lo)]
                if kind == "z":
                    return [(PZ[0:rows, t, :], rows, 0, GBLK)]
                if kind == "g":
                    return [(BA[0:rows, t, :], rows, 0, 8), (PC[0:rows, t, 0:AW], rows, 8, 8 + AW)]
                return [(PC[0:rows, t, AW:3 * AW], rows, 0, 2 * AW)]

            with nc.Block() as block:
                @block.sync
                def _(sp):
                    for n, (lo, hi, _) in enumerate(chunks):
                        if n >= 2:
                            sp.wait_ge(freed[n - 2], 1).then_inc(freed[n - 2], -1)
                        sp.dma_start(W[n % 2][:, :, 0:hi - lo], wi[:, :, lo:hi]).then_inc(w_landed[n % 2], 16)
                    sp.wait_ge(freed[-2], 1).then_inc(freed[-2], -1)
                    sp.wait_ge(freed[-1], 1).then_inc(freed[-1], -1)

                @block.tensor
                def _(pe):
                    for i, (n, kind, t, lo, hi, last) in enumerate(groups):
                        if i == 0 or groups[i - 1][0] != n:
                            pe.wait_ge(w_landed[n % 2], 16).then_inc(w_landed[n % 2], -16)
                        if i >= 8:
                            pe.wait_ge(act_free if i % 2 == 0 else dve_free, 1).then_inc(act_free if i % 2 == 0 else dve_free, -1)
                        for k in range(KD):
                            if kind == "feature":
                                off = t * P - (lo - 768)
                                mm = pe_.matmul(ps[i % 8][:, :], W[n % 2][:, k, off:off + P], HT[:, k, 0:SEQ],
                                                start=(k == 0), stop=(k == KD - 1))
                            else:
                                rows = P if t < NT else NB
                                mm = pe_.matmul(ps[i % 8][0:rows, 0:hi - lo], HT[:, k, t * P:t * P + rows],
                                                W[n % 2][:, k, 0:hi - lo], start=(k == 0), stop=(k == KD - 1))
                        mm.then_inc(pe2act if i % 2 == 0 else pe2dve, 1)
                    pe.wait_ge(act_free, 4).then_inc(act_free, -4)
                    pe.wait_ge(dve_free, 4).then_inc(dve_free, -4)

                @block.scalar
                def _(act):
                    for i, g in enumerate(groups):
                        if i % 2 == 0:
                            act.wait_ge(pe2act, 1).then_inc(pe2act, -1)
                            if g[5]:
                                act.sem_inc(w_used_act, 1)
                            for dst, rows, lo, hi in result(g):
                                last = act_.copy(dst, ps[i % 8][0:rows, lo:hi])
                            last.then_inc(act_free, 1)

                @block.vector
                def _(dve):
                    for i, g in enumerate(groups):
                        if i % 2 == 1:
                            dve.wait_ge(pe2dve, 1).then_inc(pe2dve, -1)
                            if g[5]:
                                dve.sem_inc(w_used, 1)
                            for dst, rows, lo, hi in result(g):
                                last = vec.tensor_copy(dst, ps[i % 8][0:rows, lo:hi])
                            last.then_inc(dve_free, 1)

                @block.gpsimd
                def _(pool):
                    nc.gpsimd.memset(BT[:, :, 0:3], 0.0)
            AR.at = mark

        def heads_of_a_and_c(l, PA, PC):
            mark = AR.at
            GA = AR.room(8, HD)
            BC = AR.room(2 * AW)
            SQ = AR.room(TILES, 8, HD)
            SS = AR.room(TILES, 8)
            T1 = AR.room(TILES, 8, HD // 2)
            T2 = AR.room(TILES, 8, HD // 2)
            T3 = AR.room(TILES, 8, HD // 2)
            qk = PA[:, :, 0:2 * AW].rearrange("p t (h e) -> p t h e", e=HD)
            rope = cst("rope").rearrange("p (t c e) -> p t c e", t=TILES, c=2)
            cos, sin = (bc(rope[:, :, c, :], 2, 8) for c in range(2))
            with nc.Block() as block:
                @block.scalar
                def _(act):
                    act.wait_ge(dve2act, 1).then_inc(dve2act, -1)
                    rsqrt(SS, SS, 1.0 / HD).then_inc(act2dve, 1)

                @block.sync
                def _(sp):
                    for h in range(8):
                        g = ins["qnorm_a"] if h < NH else ins["knorm_a"]
                        sp.dma_start(GA[:, h, :], g[l].partition_broadcast(P)).then_inc(loaded, 16)
                    sp.dma_start(BC[:, 0:AW], ins["b_q_c"][l].partition_broadcast(P)).then_inc(loaded, 16)
                    sp.dma_start(BC[:, AW:2 * AW], ins["b_k_c"][l].partition_broadcast(P)).then_inc(loaded, 16)
                    sp.wait_ge(dve2sp, 1).then_inc(dve2sp, -1)
                    n = 0
                    for i, src in ((0, PC), (1, PA)):
                        if i == 1:
                            sp.wait_ge(dve2sp, 1).then_inc(dve2sp, -1)
                        names = ("sb_k", "sb_v") if i == 0 else ("win_k", "win_v")
                        for name, lo in zip(names, (AW, 2 * AW)):
                            sp.dma_start(outs[name + "_prompt"][l, 0].rearrange("(t p) h e -> p t (h e)", p=P),
                                         src[:, 0:NT, lo:lo + AW]).then_inc(stored, 16)
                            sp.dma_start(outs[name + "_sample"][l, :, 0].rearrange("b h e -> b (h e)"),
                                         src[0:NB, NT, lo:lo + AW]).then_inc(stored, 16)
                            n += 2
                    sp.wait_ge(stored, 16 * n).then_inc(stored, -(16 * n))

                @block.vector
                def _(dve):
                    dve.wait_ge(loaded, 160).then_inc(loaded, -160)
                    qkc = PC[:, :, 0:2 * AW]
                    vec.tensor_tensor(qkc, qkc, bc(BC, 1, TILES), ALU.add).then_inc(dve2sp, 1)
                    for t in range(TILES):
                        vec.tensor_tensor(SQ[:, t], qk[:, t], qk[:, t], ALU.mult)
                    vec.engine_nop().then_inc(dve_own, 1)
                    vec.wait_ge(dve_own, 1).then_inc(dve_own, -1)
                    vec.tensor_reduce(SS, SQ, AX, ALU.add).then_inc(dve2act, 1)
                    dve.wait_ge(act2dve, 1).then_inc(act2dve, -1)
                    vec.tensor_tensor(qk, qk, bc(SS, 3, HD), ALU.mult).then_inc(dve_own, 1)
                    vec.wait_ge(dve_own, 1).then_inc(dve_own, -1)
                    vec.tensor_tensor(qk, qk, bc(GA, 1, TILES), ALU.mult).then_inc(dve_own, 1)
                    vec.wait_ge(dve_own, 1).then_inc(dve_own, -1)
                    x1, x2 = qk[:, :, :, 0:HD // 2], qk[:, :, :, HD // 2:HD]
                    vec.tensor_tensor(T1, x1, sin, ALU.mult)
                    vec.tensor_tensor(T2, x2, sin, ALU.mult)
                    vec.tensor_tensor(T3, x1, cos, ALU.mult)
                    vec.tensor_tensor(SQ[:, :, :, 0:HD // 2], x2, cos, ALU.mult).then_inc(dve_own, 1)
                    vec.wait_ge(dve_own, 1).then_inc(dve_own, -1)
                    vec.tensor_tensor(x1, T3, T2, ALU.subtract)
                    vec.tensor_tensor(x2, SQ[:, :, :, 0:HD // 2], T1, ALU.add).then_inc(dve2sp, 1)
            AR.at = mark

        def transpose_heads(PA, PC, QT):
            with nc.Block() as block:
                @block.tensor
                def _(pe):
                    for i in range(8):
                        src, lo = (PA, PC)[i // 4], (i % 4) * P
                        for t in range(NT):
                            last = pe_.transpose(ps[i][:, t * P:(t + 1) * P], src[:, t, lo:lo + P], ident)
                        last.then_inc(pe2act if i % 4 < 2 else pe2dve, 1)

                @block.scalar
                def _(act):
                    for i in (0, 1, 4, 5):
                        act.wait_ge(pe2act, 1).then_inc(pe2act, -1)
                        act_.mul(QT[:, i, :], ps[i][:, :], HD ** -0.5)

                @block.vector
                def _(dve):
                    for i in (2, 3, 6, 7):
                        dve.wait_ge(pe2dve, 1).then_inc(pe2dve, -1)
                        vec.tensor_copy(QT[:, i, :], ps[i][:, :])

        def head_rows(QT, which, h):
            r = (h % 2) * HD
            return QT[r:r + HD, which + h // 2, :]

        def attend_a(QT, PA):
            mark = AR.at
            SM = [AR.room(SEQ) for _ in range(2)]
            PR = [AR.room(SEQ) for _ in range(2)]
            PT = [AR.room(NT, P) for _ in range(2)]
            NM = AR.room(NT * NH)
            DEN = AR.room(NT * NH)
            items = [(i, h) for i in range(NT) for h in range(NH)]
            with nc.Block() as block:
                def scores(n):
                    i, h = items[n]
                    w = (i + 1) * P
                    pe_.matmul(ps[n % 2][:, 0:w], head_rows(QT, 0, h)[:, i * P:(i + 1) * P],
                               head_rows(QT, 2, h)[:, 0:w], start=True, stop=True).then_inc(pe2dve, 1)

                @block.tensor
                def _(pe):
                    scores(0)
                    for n, (i, h) in enumerate(items):
                        if n + 1 < len(items):
                            scores(n + 1)
                        pe.wait_ge(act2pe, 1).then_inc(act2pe, -1)
                        for j in range(i + 1):
                            last = pe_.transpose(ps[2 + n % 2][:, j * P:(j + 1) * P], PR[n % 2][:, j * P:(j + 1) * P], ident)
                        last.then_inc(pe2act, 1)
                        pe.wait_ge(act2pe, 1).then_inc(act2pe, -1)
                        for j in range(i + 1):
                            last = pe_.matmul(ps[4 + n % 2][:, 0:HD], PT[n % 2][:, j, :],
                                              PA[:, j, 2 * AW + h * HD:2 * AW + (h + 1) * HD], start=(j == 0), stop=(j == i))
                        last.then_inc(pe2dve, 1)

                @block.vector
                def _(dve):
                    def finish(n):
                        i, h = items[n]
                        dve.wait_ge(pe2dve, 1).then_inc(pe2dve, -1)
                        vec.reciprocal(DEN[:, n:n + 1], DEN[:, n:n + 1]).then_inc(dve_own, 1)
                        vec.wait_ge(dve_own, 1).then_inc(dve_own, -1)
                        vec.tensor_scalar(O[:, i, h * HD:(h + 1) * HD], ps[4 + n % 2][:, 0:HD], DEN[:, n:n + 1], None, ALU.mult)

                    def mask(n):
                        i, h = items[n]
                        w = (i + 1) * P
                        dve.wait_ge(pe2dve, 1).then_inc(pe2dve, -1)
                        vec.tensor_tensor(SM[n % 2][:, 0:w], ps[n % 2][:, 0:w], cst("log_count")[:, SEQ - w:SEQ], ALU.add).then_inc(dve_own, 1)
                        vec.wait_ge(dve_own, 1).then_inc(dve_own, -1)
                        vec.tensor_reduce(NM[:, n:n + 1], SM[n % 2][:, 0:w], AX, ALU.max, negate=True).then_inc(dve2act, 1)

                    mask(0)
                    for n in range(len(items)):
                        if n + 1 < len(items):
                            mask(n + 1)
                        finish(n)

                @block.scalar
                def _(act):
                    for n, (i, h) in enumerate(items):
                        w = (i + 1) * P
                        act.wait_ge(dve2act, 1).then_inc(dve2act, -1)
                        act_.activation(PR[n % 2][:, 0:w], SM[n % 2][:, 0:w], ACT.Exp, bias=NM[:, n:n + 1],
                                        accum_out=DEN[:, n:n + 1]).then_inc(act2pe, 1)
                        act.wait_ge(pe2act, 1).then_inc(pe2act, -1)
                        act_.copy(PT[n % 2][:, 0:i + 1, :], ps[2 + n % 2][:, 0:w].rearrange("p (j k) -> p j k", k=P)).then_inc(act2pe, 1)
            AR.at = mark

        def attend_c(QT, PC):
            mark = AR.at
            SP = [[AR.room(SEQ) for _ in range(NT)] for _ in range(2)]
            W = [[AR.room(SEQ) for _ in range(NT)] for _ in range(2)]
            E1 = [AR.room(SEQ) for _ in range(2)]
            items = [(h, ks) for h in range(NH) for ks in reversed(range(NT))]
            with nc.Block() as block:
                def scores(n, bank, start, stop):
                    h, ks = items[n]
                    return pe_.matmul(bank[:, 0:SEQ - ks * P], head_rows(QT, 6, h)[:, ks * P:(ks + 1) * P],
                                      head_rows(QT, 4, h)[:, ks * P:SEQ], start=start, stop=stop)

                @block.tensor
                def _(pe):
                    scores(0, ps[0], True, True).then_inc(pe2act, 1)
                    for n, (h, ks) in enumerate(items):
                        if n + 1 < len(items):
                            scores(n + 1, ps[(n + 1) % 2], True, True).then_inc(pe2act, 1)
                        pe.wait_ge(dve2pe, 1).then_inc(dve2pe, -1)
                        arg = ps[2 + n % 2]
                        w = SEQ - ks * P
                        scores(n, arg, True, False)
                        pe_.matmul(arg[:, 0:P], ident, cst("neg_mask"), start=False, stop=False)
                        last = pe_.matmul(arg[:, 0:w], cst("neg_lower"), SP[h % 2][ks][:, 0:w], start=False, stop=(ks == NT - 1))
                        for k2 in range(ks + 1, NT):
                            off = (k2 - ks) * P
                            last = pe_.matmul(arg[:, off:w], cst("neg_ones"), SP[h % 2][k2][:, 0:SEQ - k2 * P],
                                              start=False, stop=(k2 == NT - 1))
                        last.then_inc(pe2act, 1)
                        pe.wait_ge(act2pe, 1).then_inc(act2pe, -1)
                        if ks == 0:
                            out = ps[4 + h % 2]
                            for t in range(NT):
                                for k2 in range(t + 1):
                                    last = pe_.matmul(out[:, t * HD:(t + 1) * HD], W[h % 2][k2][:, (t - k2) * P:(t - k2 + 1) * P],
                                                      PC[:, k2, 2 * AW + h * HD:2 * AW + (h + 1) * HD], start=(k2 == 0), stop=(k2 == t))
                            last.then_inc(pe2dve, 1)

                @block.scalar
                def _(act):
                    act_.preload_act_table_set("natural_log_exp_and_others")

                    def log_part(n):
                        h, ks = items[n]
                        w = SEQ - ks * P
                        act.wait_ge(pe2act, 1).then_inc(pe2act, -1)
                        act_.activation(E1[n % 2][:, 0:w], ps[n % 2][:, 0:w], ACT.Abs).then_inc(act_own, 1)
                        act_.wait_ge(act_own, 1).then_inc(act_own, -1)
                        act_.activation(E1[n % 2][:, 0:w], E1[n % 2][:, 0:w], ACT.Exp, scale=-1.0).then_inc(act_own, 1)
                        act_.wait_ge(act_own, 1).then_inc(act_own, -1)
                        act_.activation(E1[n % 2][:, 0:w], E1[n % 2][:, 0:w], ACT.Ln, bias=1.0).then_inc(act2dve, 1)

                    log_part(0)
                    for n, (h, ks) in enumerate(items):
                        if n + 1 < len(items):
                            log_part(n + 1)
                        w = SEQ - ks * P
                        act.wait_ge(pe2act, 1).then_inc(pe2act, -1)
                        act_.activation(W[h % 2][ks][:, 0:w], ps[2 + n % 2][:, 0:w], ACT.Exp).then_inc(act2pe, 1)

                @block.vector
                def _(dve):
                    def softplus(n):
                        h, ks = items[n]
                        w = SEQ - ks * P
                        dve.wait_ge(act2dve, 1).then_inc(act2dve, -1)
                        sp_ = SP[h % 2][ks]
                        vec.scalar_tensor_tensor(sp_[:, 0:w], ps[n % 2][:, 0:w], 0.0, E1[n % 2][:, 0:w], ALU.max, ALU.add).then_inc(dve_own, 1)
                        vec.wait_ge(dve_own, 1).then_inc(dve_own, -1)
                        vec.tensor_tensor(sp_[:, 0:P], sp_[:, 0:P], cst("strict_upper"), ALU.mult).then_inc(dve2pe, 1)

                    for n, (h, ks) in enumerate(items):
                        softplus(n)
                        if ks == 0:
                            dve.wait_ge(pe2dve, 1).then_inc(pe2dve, -1)
                            out = ps[4 + h % 2][:, 0:NT * HD].rearrange("p (t e) -> p t e", e=HD)
                            vec.tensor_copy(O[:, 0:NT, 3 * AW + h * HD:3 * AW + (h + 1) * HD], out)
            AR.at = mark

        def convolve(l, BT):
            mark = AR.at
            CWR = AR.room(P, rows=KW * CC)
            CW = AR.room(KW, CC)
            LAST = AR.room(P, rows=(KW - 1) * CC)
            LC = AR.room(KW - 1, CC)
            TMP = [AR.room(SEQ) for _ in range(4)]
            RN = [AR.room(SEQ) for _ in range(2)]
            with nc.Block() as block:
                @block.sync
                def _(sp):
                    sp.dma_start(CWR, ins["conv_w"][l].rearrange("j (c p) -> (j c) p", p=P)).then_inc(loaded, 16)
                    sp.wait_ge(act2sp, 1).then_inc(act2sp, -1)
                    sp.dma_start(outs["conv_prompt"][l, 0].rearrange("j (c p) -> (j c) p", p=P), LAST).then_inc(stored, 16)
                    sp.wait_ge(stored, 16).then_inc(stored, -16)

                @block.tensor
                def _(pe):
                    pe.wait_ge(loaded, 16).then_inc(loaded, -16)
                    pe_.transpose(ps[0][:, 0:KW * CC], CWR, ident[0:KW * CC, 0:KW * CC]).then_inc(pe2dve, 1)
                    pe.wait_ge(act2pe, 1).then_inc(act2pe, -1)
                    pe_.transpose(ps[1][0:(KW - 1) * CC, 0:P], LC.rearrange("p j c -> p (j c)"), ident).then_inc(pe2act, 1)
                    for c in range(8):
                        pe.wait_ge(dve2pe, 1).then_inc(dve2pe, -1)
                        pe_.matmul(ps[2 + c % 2][:, :], cst("ones"), TMP[2 + c % 2], start=True, stop=True).then_inc(pe2act, 1)

                @block.scalar
                def _(act):
                    act_.copy(LC, BT[:, :, SEQ:SEQ + KW - 1].rearrange("p c j -> p j c")).then_inc(act2pe, 1)
                    act.wait_ge(pe2act, 1).then_inc(pe2act, -1)
                    act_.copy(LAST, ps[1][0:(KW - 1) * CC, 0:P]).then_inc(act2sp, 1)
                    for c in range(CC):
                        act.wait_ge(dve2act, 1).then_inc(dve2act, -1)
                        act_.activation(BT[:, c, 3:3 + SEQ], TMP[c % 2], ACT.Silu).then_inc(act2dve, 1)
                    act_.preload_act_table_set("natural_log_exp_and_others")
                    for c in range(8):
                        act.wait_ge(pe2act, 1).then_inc(pe2act, -1)
                        rsqrt(RN[c % 2], ps[2 + c % 2][:, :], 1.0).then_inc(act2dve, 1)

                @block.vector
                def _(dve):
                    dve.wait_ge(pe2dve, 1).then_inc(pe2dve, -1)
                    vec.tensor_copy(CW, ps[0][:, 0:KW * CC].rearrange("p (j c) -> p j c", j=KW)).then_inc(dve_own, 1)
                    vec.wait_ge(dve_own, 1).then_inc(dve_own, -1)
                    for c in range(CC):
                        if c >= 2:
                            dve.wait_ge(act2dve, 1).then_inc(act2dve, -1)
                        t = TMP[c % 2]
                        vec.tensor_scalar(t, BT[:, c, 0:SEQ], CW[:, 0, c:c + 1], None, ALU.mult).then_inc(dve_own, 1)
                        vec.wait_ge(dve_own, 1).then_inc(dve_own, -1)
                        for j in range(1, KW):
                            i_ = vec.scalar_tensor_tensor(t, BT[:, c, j:j + SEQ], CW[:, j, c:c + 1], t, ALU.mult, ALU.add)
                            if j < KW - 1:
                                i_.then_inc(dve_own, 1)
                                vec.wait_ge(dve_own, 1).then_inc(dve_own, -1)
                        i_.then_inc(dve2act, 1)
                    dve.wait_ge(act2dve, 2).then_inc(act2dve, -2)
                    for c in range(8 + 1):
                        if c < 8:
                            u = BT[:, c, 3:3 + SEQ]
                            vec.tensor_tensor(TMP[2 + c % 2], u, u, ALU.mult).then_inc(dve2pe, 1)
                        if c >= 1:
                            k = c - 1
                            u = BT[:, k, 3:3 + SEQ]
                            dve.wait_ge(act2dve, 1).then_inc(act2dve, -1)
                            vec.scalar_tensor_tensor(u, u, DK ** -0.5 if k < NH else 1.0, RN[k % 2], ALU.mult, ALU.mult)
            AR.at = mark

        def gates(l, BA, G):
            mark = AR.at
            AL = AR.room(NH)
            DT = AR.room(NH)
            A = AR.room(TILES, NH)
            E = AR.room(TILES, NH)
            with nc.Block() as block:
                @block.sync
                def _(sp):
                    sp.dma_start(AL, ins["a_log"][l].partition_broadcast(P)).then_inc(loaded, 16)
                    sp.dma_start(DT, ins["dt_bias"][l].partition_broadcast(P)).then_inc(loaded, 16)

                @block.scalar
                def _(act):
                    act_.activation(G[:, 0], BA[:, :, 0:NH], ACT.Sigmoid)
                    act.wait_ge(dve2act, 1).then_inc(dve2act, -1)
                    act_.activation(AL, AL, ACT.Exp).then_inc(act_own, 1)
                    act_.wait_ge(act_own, 1).then_inc(act_own, -1)
                    act_.activation(E, A, ACT.Abs).then_inc(act_own, 1)
                    act_.wait_ge(act_own, 1).then_inc(act_own, -1)
                    act_.activation(E, E, ACT.Exp, scale=-1.0).then_inc(act_own, 1)
                    act_.wait_ge(act_own, 1).then_inc(act_own, -1)
                    act_.activation(E, E, ACT.Ln, bias=1.0).then_inc(act2dve, 1)

                @block.vector
                def _(dve):
                    dve.wait_ge(loaded, 32).then_inc(loaded, -32)
                    vec.tensor_tensor(A, BA[:, :, NH:2 * NH], bc(DT, 1, TILES), ALU.add).then_inc(dve2act, 1)
                    dve.wait_ge(act2dve, 1).then_inc(act2dve, -1)
                    vec.scalar_tensor_tensor(E, A, 0.0, E, ALU.max, ALU.add).then_inc(dve_own, 1)
                    vec.wait_ge(dve_own, 1).then_inc(dve_own, -1)
                    vec.scalar_tensor_tensor(G[:, 1], E, -1.0, bc(AL, 1, TILES), ALU.mult, ALU.mult)
            AR.at = mark

        def delta_prompt(l, BT, G, PZ):
            mark = AR.at
            F = NH * P
            names = ("KN", "VB", "KBE", "KS", "L", "R", "T", "AT", "QE")
            KN, VB, KBE, KS, L, R, T, AT, QE = (AR.room(NT, F) for _ in names)
            YB = [AR.room(F) for _ in range(2)]
            LM = [AR.room(F) for _ in range(2)]
            TG, DF, DU = YB[0], LM[0], LM[1]
            S, VN = YB[1], LM[0]
            GC = AR.room(NT * NH)
            GE = AR.room(NT * NH)
            GK = AR.room(NT * NH)
            GL = AR.room(NT * NH)
            BE = AR.room(NT * NH)
            H4 = lambda a: a.rearrange("p (h e) -> p h e", h=NH)
            hs = lambda h: slice(h * P, (h + 1) * P)
            beta = G[:, 0, 0:NT, :].rearrange("p t h -> p (t h)")
            g16 = G[:, 1, 0:NT, :].rearrange("p t h -> p (t h)")
            chan = lambda c, t: BT[:, c, 3 + t * P:3 + (t + 1) * P]
            with nc.Block() as block:
                @block.tensor
                def _(pe):
                    pe_.matmul(ps[0][:, 0:16], cst("upper"), g16, start=True, stop=True)
                    pe_.matmul(ps[1][:, 0:16], cst("ones"), g16, start=True, stop=True).then_inc(pe2dve, 1)
                    for t in range(NT):
                        for i, b0 in ((0, 4), (1, 8)):
                            for h in range(NH):
                                last = pe_.transpose(ps[2 + i][:, hs(h)], chan(b0 + h, t), ident)
                        last.then_inc(pe2dve, 1)
                        pe.wait_ge(dve2pe, 1).then_inc(dve2pe, -1)
                        pe_.matmul(ps[4][:, :], cst("ones"), TG, start=True, stop=True).then_inc(pe2dve, 1)
                        for h in range(NH):
                            pe_.matmul(ps[5][:, hs(h)], chan(4 + h, t), chan(4 + h, t), start=True, stop=True)
                            last = pe_.matmul(ps[6][:, hs(h)], chan(4 + h, t), chan(h, t), start=True, stop=True)
                        last.then_inc(pe2dve, 1)
                        pe.wait_ge(dve2pe, 1).then_inc(dve2pe, -1)

                @block.vector
                def _(dve):
                    dve.wait_ge(pe2dve, 1).then_inc(pe2dve, -1)
                    vec.tensor_copy(GC, ps[0][:, 0:16])
                    vec.tensor_copy(GL, ps[1][:, 0:16]).then_inc(dve_own, 1)
                    vec.wait_ge(dve_own, 1).then_inc(dve_own, -1)
                    vec.tensor_tensor(GK, GL, GC, ALU.subtract).then_inc(dve2act, 1)
                    dve.wait_ge(act2dve, 1).then_inc(act2dve, -1)
                    vec.tensor_tensor(BE, beta, GE, ALU.mult).then_inc(dve_own, 1)
                    vec.wait_ge(dve_own, 1).then_inc(dve_own, -1)
                    for t in range(NT):
                        for h in range(NH):
                            last = vec.tensor_scalar(TG[:, hs(h)], cst("upper"), g16[:, t * NH + h:t * NH + h + 1], None, ALU.mult)
                        last.then_inc(dve2pe, 1)
                        dve.wait_ge(pe2dve, 1).then_inc(pe2dve, -1)
                        col = lambda a, h: a[:, t * NH + h:t * NH + h + 1]
                        for h in range(NH):
                            vec.tensor_copy(KN[:, t, hs(h)], ps[2][:, hs(h)])
                            vec.tensor_scalar(VB[:, t, hs(h)], ps[3][:, hs(h)], col(beta, h), None, ALU.mult)
                            vec.tensor_scalar(KBE[:, t, hs(h)], ps[2][:, hs(h)], col(BE, h), None, ALU.mult)
                            vec.tensor_scalar(KS[:, t, hs(h)], ps[2][:, hs(h)], col(GK, h), None, ALU.mult)
                        dve.wait_ge(pe2dve, 1).then_inc(pe2dve, -1)
                        for h in range(NH):
                            vec.tensor_scalar(DF[:, hs(h)], ps[4][:, hs(h)], col(GC, h), 0.0, ALU.subtract, ALU.max)
                            last = vec.tensor_scalar(DU[:, hs(h)], ps[4][:, hs(h)], col(GC, h), 0.0, ALU.subtract, ALU.min)
                        last.then_inc(dve2act, 1)
                        dve.wait_ge(act2dve, 1).then_inc(act2dve, -1)
                        dve.wait_ge(pe2dve, 1).then_inc(pe2dve, -1)
                        vec.tensor_tensor(H4(DF), H4(DF), bc(cst("strict_lower"), 1, NH), ALU.mult)
                        vec.tensor_tensor(H4(DU), H4(DU), bc(cst("upper"), 1, NH), ALU.mult).then_inc(dve_own, 1)
                        vec.wait_ge(dve_own, 1).then_inc(dve_own, -1)
                        for h in range(NH):
                            vec.scalar_tensor_tensor(L[:, t, hs(h)], ps[5][:, hs(h)], col(beta, h), DF[:, hs(h)], ALU.mult, ALU.mult)
                        vec.tensor_tensor(AT[:, t, :], ps[6][:, :], DU, ALU.mult)
                        q4 = BT[:, 0:NH, 3 + t * P:3 + (t + 1) * P]
                        vec.tensor_tensor(H4(QE[:, t, :]), H4(QE[:, t, :]), q4, ALU.mult)
                        vec.tensor_copy(H4(R[:, t, :]), bc(ident, 1, NH))
                        vec.tensor_copy(H4(T[:, t, :]), bc(ident, 1, NH)).then_inc(dve2pe, 1)

                @block.scalar
                def _(act):
                    act_.preload_act_table_set("natural_log_exp_and_others")
                    act.wait_ge(dve2act, 1).then_inc(dve2act, -1)
                    act_.activation(GE, GC, ACT.Exp)
                    act_.activation(GK, GK, ACT.Exp)
                    act_.activation(GL, GL, ACT.Exp).then_inc(act2dve, 1)
                    for t in range(NT):
                        act.wait_ge(dve2act, 1).then_inc(dve2act, -1)
                        act_.activation(DF, DF, ACT.Exp, scale=-1.0)
                        act_.activation(DU, DU, ACT.Exp)
                        act_.activation(QE[:, t, :], ps[4][:, :], ACT.Exp).then_inc(act2dve, 1)

            with nc.Block() as block:
                rounds = [(v, t) for v in range(LEVELS) for t in range(NT)]

                @block.gpsimd
                def _(pool):
                    for n, (v, t) in enumerate(rounds):
                        if n >= 2:
                            pool.wait_ge(dve2pool, 1).then_inc(dve2pool, -1)
                        m = cst("levels")[:, v * P:(v + 1) * P]
                        nc.gpsimd.tensor_tensor(H4(LM[n % 2]), H4(L[:, t, :]), bc(m, 1, NH), ALU.mult).then_inc(pool2pe, 1)
                    pool.wait_ge(dve2pool, 2).then_inc(dve2pool, -2)

                @block.tensor
                def _(pe):
                    def first(n):
                        v, t = rounds[n]
                        pe.wait_ge(pool2pe, 1).then_inc(pool2pe, -1)
                        if n >= 2:
                            pe.wait_ge(dve2pe, 1).then_inc(dve2pe, -1)
                        for h in range(NH):
                            last = pe_.matmul(ps[n % 2][:, hs(h)], LM[n % 2][:, hs(h)], R[:, t, hs(h)], start=True, stop=True)
                        last.then_inc(pe2act, 1)

                    first(0)
                    for n, (v, t) in enumerate(rounds):
                        if n + 1 < len(rounds):
                            first(n + 1)
                        pe.wait_ge(act2pe, 1).then_inc(act2pe, -1)
                        for h in range(NH):
                            pe_.matmul(ps[2 + n % 2][:, hs(h)], T[:, t, hs(h)], YB[n % 2][:, hs(h)], start=True, stop=True)
                            last = pe_.matmul(ps[4 + n % 2][:, hs(h)], YB[n % 2][:, hs(h)], T[:, t, hs(h)], start=True, stop=True)
                        last.then_inc(pe2dve, 1)
                    pe.wait_ge(dve2pe, 2).then_inc(dve2pe, -2)

                @block.scalar
                def _(act):
                    for n in range(len(rounds)):
                        act.wait_ge(pe2act, 1).then_inc(pe2act, -1)
                        act_.copy(YB[n % 2], ps[n % 2][:, :]).then_inc(act2pe, 1)

                @block.vector
                def _(dve):
                    for n, (v, t) in enumerate(rounds):
                        dve.wait_ge(pe2dve, 1).then_inc(pe2dve, -1)
                        dve.sem_inc(dve2pool, 1)
                        vec.tensor_tensor(R[:, t, :], R[:, t, :], ps[2 + n % 2][:, :], ALU.subtract)
                        vec.tensor_tensor(T[:, t, :], T[:, t, :], ps[4 + n % 2][:, :], ALU.subtract).then_inc(dve2pe, 1)

            U, WT = L, T
            with nc.Block() as block:
                @block.tensor
                def _(pe):
                    for t in range(NT):
                        for h in range(NH):
                            pe_.matmul(ps[2 * (t % 2)][:, hs(h)], R[:, t, hs(h)], VB[:, t, hs(h)], start=True, stop=True)
                            last = pe_.matmul(ps[2 * (t % 2) + 1][:, hs(h)], KBE[:, t, hs(h)], R[:, t, hs(h)], start=True, stop=True)
                        last.then_inc(pe2act, 1)
                        if t >= 1:
                            pe.wait_ge(act2pe, 1).then_inc(act2pe, -1)
                    pe.wait_ge(act2pe, 1).then_inc(act2pe, -1)
                    for t in range(NT):
                        pe.wait_ge(dve2pe, 1).then_inc(dve2pe, -1)
                        for h in range(NH):
                            last = pe_.matmul(ps[4][:, hs(h)], WT[:, t, hs(h)], S[:, hs(h)], start=True, stop=True)
                        last.then_inc(pe2dve, 1)
                        pe.wait_ge(dve2pe, 1).then_inc(dve2pe, -1)
                        for h in range(NH):
                            last = pe_.matmul(ps[5][:, hs(h)], KS[:, t, hs(h)], VN[:, hs(h)], start=True, stop=True)
                        last.then_inc(pe2dve, 1)
                        for h in range(NH):
                            pe_.matmul(ps[6][:, hs(h)], QE[:, t, hs(h)], S[:, hs(h)], start=True, stop=False)
                            last = pe_.matmul(ps[6][:, hs(h)], AT[:, t, hs(h)], VN[:, hs(h)], start=False, stop=True)
                        last.then_inc(pe2act, 1)

                @block.scalar
                def _(act):
                    for t in range(NT):
                        act.wait_ge(pe2act, 1).then_inc(pe2act, -1)
                        act_.copy(U[:, t, :], ps[2 * (t % 2)][:, :])
                        act_.copy(WT[:, t, :], ps[2 * (t % 2) + 1][:, :]).then_inc(act2pe, 1)
                    for t in range(NT):
                        act.wait_ge(pe2act, 1).then_inc(pe2act, -1)
                        act_.copy(O[:, t, AW:AW + F], ps[6][:, :]).then_inc(act2dve, 1)

                @block.vector
                def _(dve):
                    vec.memset(S, 0.0).then_inc(dve2pe, 1)
                    for t in range(NT):
                        dve.wait_ge(pe2dve, 1).then_inc(pe2dve, -1)
                        vec.tensor_tensor(VN, U[:, t, :], ps[4][:, :], ALU.subtract).then_inc(dve2pe, 1)
                        dve.wait_ge(pe2dve, 1).then_inc(pe2dve, -1)
                        dve.wait_ge(act2dve, 1).then_inc(act2dve, -1)
                        for h in range(NH):
                            last = vec.scalar_tensor_tensor(S[:, hs(h)], S[:, hs(h)], GL[:, t * NH + h:t * NH + h + 1],
                                                            ps[5][:, hs(h)], ALU.mult, ALU.add)
                        last.then_inc(dve2pe if t < NT - 1 else dve2sp, 1)

                @block.sync
                def _(sp):
                    sp.wait_ge(dve2sp, 1).then_inc(dve2sp, -1)
                    sp.dma_start(outs["delta_prompt"][l, 0].rearrange("h k v -> k h v"), H4(S)).then_inc(stored, 16)
                    sp.wait_ge(stored, 16).then_inc(stored, -16)
            AR.at = mark

        def gated_norm(l, PZ):
            mark = AR.at
            GN = AR.room(P)
            SQ = AR.room(TILES, NH * P)
            SS = AR.room(TILES * NH)
            o = O[:, :, AW:3 * AW]
            by_head = lambda a, t: a[:, t, :].rearrange("p (h e) -> p h e", h=NH)
            with nc.Block() as block:
                @block.sync
                def _(sp):
                    sp.dma_start(GN, ins["gnorm_b"][l].partition_broadcast(P)).then_inc(loaded, 16)

                @block.scalar
                def _(act):
                    act_.activation(PZ, PZ, ACT.Silu).then_inc(act2dve, 1)
                    act.wait_ge(dve2act, 1).then_inc(dve2act, -1)
                    rsqrt(SS, SS, 1.0 / DK).then_inc(act2dve, 1)

                @block.vector
                def _(dve):
                    vec.tensor_tensor(SQ, o, o, ALU.mult).then_inc(dve_own, 1)
                    vec.wait_ge(dve_own, 1).then_inc(dve_own, -1)
                    vec.tensor_reduce(SS, SQ.rearrange("p t (h e) -> p (t h) e", h=NH), AX, ALU.add).then_inc(dve2act, 1)
                    dve.wait_ge(loaded, 16).then_inc(loaded, -16)
                    dve.wait_ge(act2dve, 2).then_inc(act2dve, -2)
                    for t in range(TILES):
                        vec.tensor_tensor(by_head(SQ, t), by_head(PZ, t), bc(GN, 1, NH), ALU.mult)
                    vec.engine_nop().then_inc(dve_own, 1)
                    vec.wait_ge(dve_own, 1).then_inc(dve_own, -1)
                    for t in range(TILES):
                        vec.tensor_tensor(by_head(SQ, t), by_head(SQ, t), bc(SS[:, t * NH:(t + 1) * NH], 2, P), ALU.mult)
                    vec.engine_nop().then_inc(dve_own, 1)
                    vec.wait_ge(dve_own, 1).then_inc(dve_own, -1)
                    vec.tensor_tensor(o, o, SQ, ALU.mult)
            AR.at = mark

        def delta_sample(l, DB, G):
            mark = AR.at
            NP_ = NB * NH
            SC = AR.room(KW - 1, CONV_CH, rows=NB)
            CB = AR.room(KW, CONV_CH, rows=NB)
            ACC = AR.room(CONV_CH, rows=NB)
            TM = AR.room(CONV_CH, rows=NB)
            SS = AR.room(8, rows=NB)
            BE = AR.room(8, rows=NB)
            QKV = AR.room(CC, NB)
            KQ = AR.room(NP_, 2)
            VT = AR.room(NP_)
            QK = AR.room(NP_)
            BG = AR.room(NB, 8)
            SD = AR.room(NP_, P)
            VV = AR.room(NP_)
            OT = AR.room(NP_)
            T1 = AR.room(NP_)
            DG = [AR.room(4, P) for _ in range(2)]
            pair = lambda a: a.rearrange("p (b h) -> p b h", h=NH)
            beta, eg = BG[:, :, 0:NH], BG[:, :, NH:8]
            with nc.Block() as block:
                @block.sync
                def _(sp):
                    sp.dma_start(SC, ins["state_conv"][l]).then_inc(loaded, 16)
                    sp.dma_start(CB.rearrange("p j c -> p (j c)"), ins["conv_w"][l].rearrange("j c -> (j c)").partition_broadcast(NB)).then_inc(loaded, 16)
                    for b in range(0, NB, 2):
                        sp.dma_start(SD[:, b * NH:(b + 2) * NH, :], ins["state_delta"][l, b:b + 2].rearrange("b h k v -> k (b h) v")).then_inc(loaded2, 16)
                    sp.dma_start(outs["conv_sample"][l, :, 0:2], ins["state_conv"][l, :, 1:3]).then_inc(stored, 16)
                    sp.dma_start(outs["conv_sample"][l, :, 2], DB[0:NB, :]).then_inc(stored, 16)
                    sp.wait_ge(dve2sp, 1).then_inc(dve2sp, -1)
                    sp.dma_start(outs["delta_sample"][l].rearrange("b h k v -> k (b h) v"), SD).then_inc(stored, 16)
                    sp.wait_ge(stored, 48).then_inc(stored, -48)

                @block.scalar
                def _(act):
                    act.wait_ge(dve2act, 1).then_inc(dve2act, -1)
                    act_.activation(ACC, ACC, ACT.Silu).then_inc(act2dve, 1)
                    act.wait_ge(dve2act, 1).then_inc(dve2act, -1)
                    rsqrt(SS, SS, 1.0).then_inc(act2dve, 1)
                    act_.activation(BE[:, NH:8], G[0:NB, 1, NT, :], ACT.Exp)
                    act_.copy(BE[:, 0:NH], G[0:NB, 0, NT, :]).then_inc(act2pe, 1)

                @block.tensor
                def _(pe):
                    pe.wait_ge(act2pe, 1).then_inc(act2pe, -1)
                    for b in range(NB):
                        last = pe_.matmul(ps[0][:, b * 8:b * 8 + 8], cst("pick_row", NB)[:, b * P:(b + 1) * P], BE, start=True, stop=True)
                    pe.wait_ge(dve2pe, 1).then_inc(dve2pe, -1)
                    for c in range(CC):
                        last = pe_.transpose(ps[1][:, c * 8:c * 8 + 8], ACC[:, c * P:(c + 1) * P], ident[0:NB, 0:NB])
                    last.then_inc(pe2dve, 1)
                    pe.wait_ge(dve2pe, 1).then_inc(dve2pe, -1)
                    pe_.matmul(ps[2][:, 0:NP_], cst("ones"), QK, start=True, stop=True)
                    for n in range(NP_):
                        last = pe_.matmul(ps[3][:, 2 * n:2 * n + 2], SD[:, n, :], KQ[:, n, :], start=True, stop=True)
                    last.then_inc(pe2dve, 1)
                    pe.wait_ge(dve2pe, 1).then_inc(dve2pe, -1)
                    for h in range(NH):
                        last = pe_.transpose(ps[0][0:NB, h * P:(h + 1) * P], pair(OT)[:, :, h], ident)
                    last.then_inc(pe2dve, 1)
                    for m in range(8):
                        pe.wait_ge(dve2pe, 1).then_inc(dve2pe, -1)
                        pe_.matmul(ps[4 + m % 4][:, :], cst("ones"), DG[m % 2].rearrange("p a b -> p (a b)"), start=True, stop=True).then_inc(pe2dve, 1)

                @block.vector
                def _(dve):
                    dve.wait_ge(loaded, 32).then_inc(loaded, -32)
                    vec.tensor_tensor(ACC, DB[0:NB, :], CB[:, KW - 1, :], ALU.mult).then_inc(dve_own, 1)
                    vec.wait_ge(dve_own, 1).then_inc(dve_own, -1)
                    for j in range(KW - 1):
                        vec.tensor_tensor(TM, SC[:, j, :], CB[:, j, :], ALU.mult).then_inc(dve_own, 1)
                        vec.wait_ge(dve_own, 1).then_inc(dve_own, -1)
                        i_ = vec.tensor_tensor(ACC, ACC, TM, ALU.add)
                        if j < KW - 2:
                            i_.then_inc(dve_own, 1)
                            vec.wait_ge(dve_own, 1).then_inc(dve_own, -1)
                    i_.then_inc(dve2act, 1)
                    dve.wait_ge(act2dve, 1).then_inc(act2dve, -1)
                    qk8 = ACC[:, 0:8 * P]
                    vec.tensor_tensor(TM[:, 0:8 * P], qk8, qk8, ALU.mult).then_inc(dve_own, 1)
                    vec.wait_ge(dve_own, 1).then_inc(dve_own, -1)
                    vec.tensor_reduce(SS, TM[:, 0:8 * P].rearrange("p (h e) -> p h e", h=8), AX, ALU.add).then_inc(dve2act, 1)
                    dve.wait_ge(act2dve, 1).then_inc(act2dve, -1)
                    vec.tensor_scalar(SS[:, 0:NH], SS[:, 0:NH], DK ** -0.5, None, ALU.mult).then_inc(dve_own, 1)
                    vec.wait_ge(dve_own, 1).then_inc(dve_own, -1)
                    qk8 = qk8.rearrange("p (h e) -> p h e", h=8)
                    vec.tensor_tensor(qk8, qk8, bc(SS, 2, P), ALU.mult).then_inc(dve2pe, 1)
                    dve.wait_ge(pe2dve, 1).then_inc(pe2dve, -1)
                    vec.tensor_copy(BG, ps[0][:, 0:64].rearrange("p (b e) -> p b e", b=NB))
                    vec.tensor_copy(QKV, ps[1][:, 0:CC * NB].rearrange("p (c b) -> p c b", c=CC)).then_inc(dve_own, 1)
                    vec.wait_ge(dve_own, 1).then_inc(dve_own, -1)
                    qv, kv, vv = (QKV[:, i * NH:(i + 1) * NH, :].rearrange("p h b -> p b h") for i in range(3))
                    kq = KQ.rearrange("p (b h) c -> p b h c", h=NH)
                    vec.tensor_copy(kq[:, :, :, 0], kv)
                    vec.tensor_copy(kq[:, :, :, 1], qv)
                    vec.tensor_copy(pair(VT), vv)
                    dve.wait_ge(loaded2, 64).then_inc(loaded2, -64)
                    vec.tensor_tensor(pair(QK), qv, kv, ALU.mult).then_inc(dve2pe, 1)
                    dve.wait_ge(pe2dve, 1).then_inc(pe2dve, -1)
                    r = ps[3][:, 0:2 * NP_].rearrange("p (b h c) -> p b h c", b=NB, h=NH)
                    vec.tensor_tensor(pair(T1), r[:, :, :, 0], eg, ALU.mult).then_inc(dve_own, 1)
                    vec.wait_ge(dve_own, 1).then_inc(dve_own, -1)
                    vec.tensor_tensor(T1, VT, T1, ALU.subtract).then_inc(dve_own, 1)
                    vec.wait_ge(dve_own, 1).then_inc(dve_own, -1)
                    vec.tensor_tensor(pair(VV), pair(T1), beta, ALU.mult).then_inc(dve_own, 1)
                    vec.wait_ge(dve_own, 1).then_inc(dve_own, -1)
                    vec.tensor_tensor(pair(OT), r[:, :, :, 1], eg, ALU.mult)
                    vec.tensor_tensor(T1, VV, ps[2][:, 0:NP_], ALU.mult).then_inc(dve_own, 1)
                    vec.wait_ge(dve_own, 1).then_inc(dve_own, -1)
                    vec.tensor_tensor(OT, OT, T1, ALU.add).then_inc(dve2pe, 1)
                    sd4 = SD.rearrange("p (b h) v -> p b h v", h=NH)
                    for b in range(NB):
                        vec.tensor_tensor(sd4[:, b], sd4[:, b], bc(eg[:, b, :], 2, P), ALU.mult)
                    dve.wait_ge(pe2dve, 1).then_inc(pe2dve, -1)
                    vec.tensor_copy(O[0:NB, NT, AW:3 * AW], ps[0][0:NB, :])
                    for m in range(8 + 1):
                        if m < 8:
                            vec.tensor_tensor(DG[m % 2], bc(ident, 1, 4), bc(VV[:, 4 * m:4 * m + 4], 2, P), ALU.mult).then_inc(dve2pe, 1)
                        if m >= 1:
                            dve.wait_ge(pe2dve, 1).then_inc(pe2dve, -1)
                            for i in range(4):
                                n = 4 * (m - 1) + i
                                last = vec.scalar_tensor_tensor(SD[:, n, :], ps[4 + (m - 1) % 4][:, i * P:(i + 1) * P],
                                                                KQ[:, n, 0:1], SD[:, n, :], ALU.mult, ALU.add)
                    last.then_inc(dve2sp, 1)
            AR.at = mark

        def attend_sample(l, mixer, SRC):
            mark = AR.at
            ns = 4 if mixer == "a" else PAGES
            vw = AW + 1 if mixer == "a" else AW
            out_at = 0 if mixer == "a" else 3 * AW
            KB = [AR.room(ns, vw) for _ in range(2)]
            QB = AR.room(NB, AW)
            Z = AR.room(NB * ns * NH)
            W = AR.room(NB * ns * NH)
            SF = [AR.room(NB * ns * NH) for _ in range(2)]
            MX = AR.room(8)
            MR = AR.room(P, rows=1)
            MB = AR.room(NB * NH, rows=1)
            OD = [AR.room(AW, rows=NH) for _ in range(2)]
            PT = nc_page_table
            z4 = lambda a: a.rearrange("p (b s h) -> p b s h", b=NB, s=ns)

            def load(sp, dst, what, b, done):
                if mixer == "a":
                    cache = ins["cache_win_" + what][l, b].rearrange("s h e -> s (h e)")
                    for s_, dil in enumerate((1, 4, 16)):
                        rows = cache[PAST - P * dil:PAST, :].rearrange("(p d) e -> p d e", d=dil)[:, 0, :]
                        sp.dma_start(dst[:, s_, 0:AW], rows).then_inc(done, 16)
                    own = outs[f"win_{what}_sample"][l, b, 0].rearrange("h e -> (h e)").partition_broadcast(3)
                    sp.dma_start(dst[0:3, 3, 0:AW], own).then_inc(done, 16)
                else:
                    cache = ins["cache_sb_" + what][l]
                    for j in range(PAGES):
                        page = sp.value_load(PT[0:1, b * PAGES + j:b * PAGES + j + 1], min_val=0, max_val=cache.shape[0] - 1)
                        sp.dma_start(dst[:, j, 0:AW], cache[page].rearrange("s h e -> s (h e)")).then_inc(done, 16)

            per = 16 * (4 if mixer == "a" else PAGES)
            with nc.Block() as block:
                @block.gpsimd
                def _(pool):
                    if mixer == "a":
                        for kb in KB:
                            nc.gpsimd.memset(kb[:, 3, 0:AW], 0.0)
                            last = nc.gpsimd.memset(kb[:, :, AW:AW + 1], 1.0)
                        last.then_inc(pool2dve, 1)

                @block.sync
                def _(sp):
                    if mixer == "a":
                        sp.wait_ge(pool2dve, 1).then_inc(pool2dve, -1)
                    for n in range(2 * NB):
                        if n >= 2:
                            sp.wait_ge(ring_free, 1).then_inc(ring_free, -1)
                        load(sp, KB[n % 2], "k" if n < NB else "v", n % NB, w_landed[n % 2])
                    sp.wait_ge(ring_free, 2).then_inc(ring_free, -2)

                @block.tensor
                def _(pe):
                    for b in range(NB):
                        pe_.matmul(ps[b][:, 0:AW], cst("pick_row", NB)[:, b * P:(b + 1) * P], SRC[0:NB, NT, 0:AW],
                                   start=True, stop=True).then_inc(pe2act, 1)
                    pe.wait_ge(dve2pe, 1).then_inc(dve2pe, -1)
                    if mixer == "a":
                        pe_.transpose(ps[4][:, 0:P], Z, ident).then_inc(pe2dve, 1)
                        pe.wait_ge(dve2pe, 1).then_inc(dve2pe, -1)
                        pe_.matmul(ps[5][0:1, 0:P], MX[:, 0:1], ident, start=True, stop=True).then_inc(pe2dve, 1)
                        pe.wait_ge(dve2pe, 1).then_inc(dve2pe, -1)
                        pe_.matmul(ps[6][:, 0:NB * NH], cst("ones", 1), MB, start=True, stop=True).then_inc(pe2dve, 1)
                    else:
                        last = SF[0]
                        pe_.matmul(ps[4][:, :], ident, Z, start=True, stop=False)
                        pe_.matmul(ps[4][:, :], cst("neg_lower"), W, start=False, stop=False)
                        pe_.matmul(z4(ps[4][:, :])[:, :, 0:ns - 1, :].rearrange("p b s h -> p b (s h)"), cst("neg_ones"),
                                   z4(last)[:, :, 1:ns, :].rearrange("p b s h -> p b (s h)"), start=False, stop=True).then_inc(pe2act, 1)
                    pe.wait_ge(act2pe, 1).then_inc(act2pe, -1)
                    for b in range(NB):
                        pe.wait_ge(w_landed[b % 2], per).then_inc(w_landed[b % 2], -per)
                        for s_ in range(ns):
                            last = pe_.matmul(ps[b % 2][0:NH, 0:vw], z4(W)[:, b, s_, :], KB[b % 2][:, s_, :],
                                              start=(s_ == 0), stop=(s_ == ns - 1))
                        last.then_inc(pe2dve, 1)
                        pe.wait_ge(dve2pe, 1).then_inc(dve2pe, -1)
                        pe_.matmul(ps[7][0:NB, 0:AW], cst("place", NH)[:, b * NB:(b + 1) * NB], OD[b % 2],
                                   start=(b == 0), stop=(b == NB - 1)).then_inc(pe2act, 1)
                        pe.wait_ge(act2pe, 1).then_inc(act2pe, -1)

                @block.scalar
                def _(act):
                    for b in range(NB):
                        act.wait_ge(pe2act, 1).then_inc(pe2act, -1)
                        act_.mul(QB[:, b, :], ps[b][:, 0:AW], HD ** -0.5).then_inc(act2dve, 1)
                    act.wait_ge(dve2act, 1).then_inc(dve2act, -1)
                    if mixer == "a":
                        act_.activation(W, W, ACT.Exp).then_inc(act2pe, 1)
                    else:
                        act_.preload_act_table_set("natural_log_exp_and_others")
                        act_.activation(W, Z, ACT.Abs).then_inc(act_own, 1)
                        act_.wait_ge(act_own, 1).then_inc(act_own, -1)
                        act_.activation(W, W, ACT.Exp, scale=-1.0).then_inc(act_own, 1)
                        act_.wait_ge(act_own, 1).then_inc(act_own, -1)
                        act_.activation(W, W, ACT.Ln, bias=1.0).then_inc(act2dve, 1)
                        act.wait_ge(pe2act, 1).then_inc(pe2act, -1)
                        act_.activation(W, ps[4][:, :], ACT.Exp).then_inc(act2pe, 1)
                    for b in range(NB):
                        act.wait_ge(pe2act, 1).then_inc(pe2act, -1)
                        act.sem_inc(act2pe, 1)
                    act_.copy(O[0:NB, NT, out_at:out_at + AW], ps[7][0:NB, 0:AW])

                @block.vector
                def _(dve):
                    for b in range(NB):
                        dve.wait_ge(act2dve, 1).then_inc(act2dve, -1)
                        dve.wait_ge(w_landed[b % 2], per).then_inc(w_landed[b % 2], -per)
                        kb = KB[b % 2][:, :, 0:AW]
                        vec.tensor_tensor(kb, kb, bc(QB[:, b, :], 1, ns), ALU.mult).then_inc(dve_own, 1)
                        vec.wait_ge(dve_own, 1).then_inc(dve_own, -1)
                        zb = Z[:, b * ns * NH:(b + 1) * ns * NH]
                        vec.tensor_reduce(zb, kb.rearrange("p s (h e) -> p s h e", h=NH), AX, ALU.add).then_inc(dve_own, 1)
                        vec.wait_ge(dve_own, 1).then_inc(dve_own, -1)
                        dve.sem_inc(ring_free, 1)
                    if mixer == "a":
                        z3 = Z.rearrange("p (b m) -> p b m", b=NB)
                        vec.tensor_tensor(z3, z3, bc(cst("own_mask"), 1, NB), ALU.add).then_inc(dve2pe, 1)
                        dve.wait_ge(pe2dve, 1).then_inc(pe2dve, -1)
                        vec.tensor_reduce(MX[:, 0:1], ps[4][:, 0:P], AX, ALU.max).then_inc(dve2pe, 1)
                        dve.wait_ge(pe2dve, 1).then_inc(pe2dve, -1)
                        vec.tensor_reduce(MB.rearrange("p (b h) -> p b h", b=NB), ps[5][0:1, 0:P].rearrange("p (b s h) -> p b h s", b=NB, s=ns),
                                          AX, ALU.max).then_inc(dve2pe, 1)
                        dve.wait_ge(pe2dve, 1).then_inc(pe2dve, -1)
                        mb = ps[6][:, 0:NB * NH].rearrange("p (b h) -> p b h", b=NB)
                        vec.tensor_tensor(z4(W), z4(Z), bc(mb, 2, ns), ALU.subtract).then_inc(dve2act, 1)
                    else:
                        vec.engine_nop().then_inc(dve2act, 1)
                        dve.wait_ge(act2dve, 1).then_inc(act2dve, -1)
                        vec.scalar_tensor_tensor(W, Z, 0.0, W, ALU.max, ALU.add).then_inc(dve_own, 1)
                        vec.wait_ge(dve_own, 1).then_inc(dve_own, -1)
                        src = W
                        step, k = 1, 0
                        while step < ns:
                            dst = SF[(k + 1) % 2]
                            for b in range(NB):
                                vec.tensor_tensor(z4(dst)[:, b, 0:ns - step, :], z4(src)[:, b, 0:ns - step, :], z4(src)[:, b, step:ns, :], ALU.add)
                            last = vec.tensor_copy(z4(dst)[:, :, ns - step:ns, :], z4(src)[:, :, ns - step:ns, :])
                            step, k, src = 2 * step, k + 1, dst
                            if step < ns:
                                last.then_inc(dve_own, 1)
                                vec.wait_ge(dve_own, 1).then_inc(dve_own, -1)
                        assert src is SF[0]
                        last.then_inc(dve2pe, 1)
                    for b in range(NB):
                        dve.wait_ge(pe2dve, 1).then_inc(pe2dve, -1)
                        dve.sem_inc(ring_free, 1)
                        if mixer == "a":
                            vec.reciprocal(MX[0:NH, b:b + 1], ps[b % 2][0:NH, AW:AW + 1]).then_inc(dve_own, 1)
                            vec.wait_ge(dve_own, 1).then_inc(dve_own, -1)
                            vec.scalar_tensor_tensor(OD[b % 2], ps[b % 2][0:NH, 0:AW], MX[0:NH, b:b + 1], cst("head_diag", NH),
                                                     ALU.mult, ALU.mult).then_inc(dve2pe, 1)
                        else:
                            vec.tensor_tensor(OD[b % 2], ps[b % 2][0:NH, 0:AW], cst("head_diag", NH), ALU.mult).then_inc(dve2pe, 1)
            AR.at = mark

        def out_projection(l):
            mark = AR.at
            W = AR.room(KD, D)
            OT = AR.room(KD, SEQ + NB)
            GP = AR.room(D)
            TM = [AR.room(GBLK) for _ in range(2)]
            with nc.Block() as block:
                @block.sync
                def _(sp):
                    sp.dma_start(W, ins["w_out"][l].rearrange("(k p) n -> p k n", p=P)).then_inc(w_landed[0], 16)

                @block.tensor
                def _(pe):
                    for i in range(2):
                        last = pe_.matmul(ps[6 + i][:, :], cst("row8", NB + 1), MOD9[0:NB + 1, 2 * D + i * GBLK:2 * D + (i + 1) * GBLK],
                                          start=True, stop=True)
                    last.then_inc(pe2act, 1)
                    for g in range(2 * TILES):
                        t, half = g // 2, g % 2
                        rows = P if t < NT else NB
                        if g >= 2:
                            pe.wait_ge(act_free, 1).then_inc(act_free, -1)
                        for j in range(4):
                            k = half * 4 + j
                            last = pe_.transpose(ps[g % 2][:, j * P:j * P + rows], O[0:rows, t, k * P:(k + 1) * P], ident[0:rows, 0:rows])
                        last.then_inc(pe2act, 1)
                    pe.wait_ge(act_free, 2).then_inc(act_free, -2)
                    pe.wait_ge(w_landed[0], 16).then_inc(w_landed[0], -16)
                    for g in range(2 * TILES):
                        t, half = g // 2, g % 2
                        rows = P if t < NT else NB
                        if g >= 2:
                            pe.wait_ge(dve_free, 1).then_inc(dve_free, -1)
                        for k in range(KD):
                            last = pe_.matmul(ps[2 + g % 2][0:rows, :], OT[:, k, t * P:t * P + rows], W[:, k, half * GBLK:(half + 1) * GBLK],
                                              start=(k == 0), stop=(k == KD - 1))
                        last.then_inc(pe2dve, 1)
                    pe.wait_ge(dve_free, 2).then_inc(dve_free, -2)

                @block.scalar
                def _(act):
                    act.wait_ge(pe2act, 1).then_inc(pe2act, -1)
                    act_.copy(GP[:, 0:GBLK], ps[6][:, :])
                    act_.copy(GP[:, GBLK:D], ps[7][:, :]).then_inc(act2dve, 1)
                    for g in range(2 * TILES):
                        t, half = g // 2, g % 2
                        rows = P if t < NT else NB
                        act.wait_ge(pe2act, 1).then_inc(pe2act, -1)
                        act_.copy(OT[:, half * 4:half * 4 + 4, t * P:t * P + rows],
                                  ps[g % 2][:, :].rearrange("p (j n) -> p j n", j=4)[:, :, 0:rows]).then_inc(act_free, 1)

                @block.vector
                def _(dve):
                    dve.wait_ge(act2dve, 1).then_inc(act2dve, -1)
                    for g in range(2 * TILES):
                        t, half = g // 2, g % 2
                        rows = P if t < NT else NB
                        c = slice(half * GBLK, (half + 1) * GBLK)
                        gate = GP[:, c] if t < NT else MOD9[0:NB, 2 * D + half * GBLK:2 * D + (half + 1) * GBLK]
                        dve.wait_ge(pe2dve, 1).then_inc(pe2dve, -1)
                        vec.tensor_tensor(TM[g % 2][0:rows, :], ps[2 + g % 2][0:rows, :], gate, ALU.mult).then_inc(dve_own, 1)
                        vec.wait_ge(dve_own, 1).then_inc(dve_own, -1)
                        dve.sem_inc(dve_free, 1)
                        vec.tensor_tensor(X[0:rows, t, c], X[0:rows, t, c], TM[g % 2][0:rows, :], ALU.add)
            AR.at = mark

        def peer(l):
            mark = AR.at
            IDX = AR.room(TILES, SLOTS)
            IDI = AR.room(TILES, SLOTS).bitcast(I32)
            GT = AR.room(TILES, SLOTS)
            GP = AR.room(D)
            SS = AR.room(TILES * PH)
            mark2 = AR.at
            HT = AR.room(KD, SEQ + NB)
            norm(3, HT)
            W = AR.room(KD, D)
            KR = AR.room(PH, P)
            KBD = AR.room(PH, 2 * PK)
            QT = AR.room(PH, SEQ + NB)
            QT_end = AR.at
            keys = ins["peer_keys"][l]
            with nc.Block() as block:
                @block.sync
                def _(sp):
                    for h in range(PH):
                        sp.dma_start(KR[:, h, :].rearrange("p (x k) -> p x k", x=2), keys[h].rearrange("x e k -> e x k")).then_inc(loaded, 16)
                    sp.dma_start(W, ins["peer_wq"][l].rearrange("(k p) n -> p k n", p=P)).then_inc(w_landed[0], 16)

                @block.gpsimd
                def _(pool):
                    nc.gpsimd.memset(KBD, 0.0).then_inc(pool2dve, 1)

                @block.tensor
                def _(pe):
                    for i in range(2):
                        last = pe_.matmul(ps[6 + i][:, :], cst("row8", NB + 1), MOD9[0:NB + 1, 5 * D + i * GBLK:5 * D + (i + 1) * GBLK],
                                          start=True, stop=True)
                    last.then_inc(pe2act, 1)
                    pe.wait_ge(loaded, 16 * PH).then_inc(loaded, -(16 * PH))
                    for h in range(PH):
                        last = pe_.transpose(ps[h // 4][:, (h % 4) * P:(h % 4 + 1) * P], KR[:, h, :], ident)
                    last.then_inc(pe2dve, 1)
                    pe.wait_ge(w_landed[0], 16).then_inc(w_landed[0], -16)
                    for h in range(PH):
                        if h >= 2:
                            pe.wait_ge(act_free, 1).then_inc(act_free, -1)
                        for k in range(KD):
                            pe_.matmul(ps[2 + h % 2][:, :], W[:, k, h * P:(h + 1) * P], HT[:, k, 0:SEQ], start=(k == 0), stop=(k == KD - 1))
                        for k in range(KD):
                            last = pe_.matmul(ps[4 + h % 2][:, 0:NB], W[:, k, h * P:(h + 1) * P], HT[:, k, SEQ:SEQ + NB],
                                              start=(k == 0), stop=(k == KD - 1))
                        last.then_inc(pe2act, 1)
                    pe.wait_ge(act_free, 2).then_inc(act_free, -2)

                @block.scalar
                def _(act):
                    act.wait_ge(pe2act, 1).then_inc(pe2act, -1)
                    act_.copy(GP[:, 0:GBLK], ps[6][:, :])
                    act_.copy(GP[:, GBLK:D], ps[7][:, :])
                    for h in range(PH):
                        act.wait_ge(pe2act, 1).then_inc(pe2act, -1)
                        act_.copy(QT[:, h, 0:SEQ], ps[2 + h % 2][:, :])
                        act_.copy(QT[:, h, SEQ:SEQ + NB], ps[4 + h % 2][:, 0:NB]).then_inc(act_free, 1)

                @block.vector
                def _(dve):
                    dve.wait_ge(pool2dve, 1).then_inc(pool2dve, -1)
                    dve.wait_ge(pe2dve, 1).then_inc(pe2dve, -1)
                    for i in range(2):
                        src = ps[i][:, :].rearrange("p (h e) -> p h e", h=4)
                        vec.tensor_copy(KBD[0:HD, 4 * i:4 * i + 4, 0:PK], src[0:HD])
                        vec.tensor_copy(KBD[HD:P, 4 * i:4 * i + 4, PK:2 * PK], src[HD:P])

            AR.at = mark2
            assert QT_end <= arena_cols
            G_ = [MOD9[:, i * D:(i + 1) * D] for i in range(5)] + [AR.room(D) for _ in range(GR - 5)]
            IS = [AR.room(LOT).bitcast(I32) for _ in range(GR // LOT)]
            A8 = AR.room(GR)
            AV = AR.room(SLOTS)
            assert AR.at <= mark2 + KD * (SEQ + NB) + KD * D + PH * P
            AR.at = QT_end
            SC = AR.room(2 * PH, PK)
            SC2 = AR.room(2 * PH, PK)
            CA = SC.rearrange("p g e -> p (g e)").rearrange("p (h e) -> p h e", h=PH)
            SC3 = SC2.rearrange("p g e -> p (g e)").rearrange("p (h e) -> p h e", h=PH)
            EQ = SC2.rearrange("p g e -> p (g e)")
            TV = AR.room(2 * PH, TOPK)
            TI = AR.room(2 * PH, TOPK)
            TF = AR.room(2 * PH, TOPK)
            BV = AR.room(PH, TOPK)
            BI = AR.room(PH, TOPK)
            AF = AR.room(SLOTS)
            BF = AR.room(SLOTS)
            AI = AR.room(SLOTS)
            ACC = [AR.room(D) for _ in range(2)]
            JK = ACC[1]
            XD = SC.rearrange("p g e -> p (g e)")[:, 0:D]
            TM = SC2.rearrange("p g e -> p (g e)")[:, 0:GBLK]
            IW = AR.room(2 * PH)
            IWI = AR.room(PH).bitcast(I32)
            tables = [ins[n].rearrange("l e d -> (l e) d") for n in ("peer_u", "peer_v")]
            per_layer = [(2 * NT * (SLOTS // GR) + 1) * 16 for j in range(GR)]
            SEGS = 4
            PER = SLOTS // GR // SEGS

            with nc.Block() as block:
                @block.gpsimd
                def _(pool):
                    pool.sem_inc(ring_free, GR - 1)
                    for t in range(NT):
                        pool.wait_ge(dve2pool, 1).then_inc(dve2pool, -1)
                        for which in range(2):
                            with pool.Fori(0, SLOTS // GR) as i:
                                for lot in range(GR // LOT):
                                    pool.wait_ge(ring_free, LOT).then_inc(ring_free, -LOT)
                                    nc.gpsimd.tensor_copy(IS[lot], IDI[:, t, bass.ds(i * GR + lot * LOT, LOT)]).then_inc(pool_own, 1)
                                    pool.wait_ge(pool_own, 1).then_inc(pool_own, -1)
                                    for j in range(LOT):
                                        pool.indirect_dma_start(G_[lot * LOT + j], None, tables[which],
                                                                bass.IndirectOffsetOnAxis(ap=IS[lot][:, j:j + 1], axis=0)).then_inc(gathered[lot * LOT + j], 16)
                    pool.wait_ge(dve2pool, 1).then_inc(dve2pool, -1)
                    pool.wait_ge(ring_free, GR).then_inc(ring_free, -GR)
                    for which in range(2):
                        for j in range(PH):
                            pool.indirect_dma_start(G_[which * PH + j], None, tables[which],
                                                    bass.IndirectOffsetOnAxis(ap=IWI[:, j:j + 1], axis=0)).then_inc(gathered[which * PH + j], 16)

                @block.tensor
                def _(pe):
                    for t in range(TILES):
                        rows = P if t < NT else NB
                        if t >= 1:
                            pe.wait_ge(dve_free, 1).then_inc(dve_free, -1)
                        for h in range(PH):
                            last = pe_.matmul(ps[h // 2][0:rows, (h % 2) * 256:(h % 2) * 256 + 256], QT[:, h, t * P:t * P + rows],
                                              KBD[:, h, :], start=True, stop=True)
                        last.then_inc(pe2act, 1)
                    pe.wait_ge(dve_free, 1).then_inc(dve_free, -1)
                    pe.wait_ge(dve2pe, 1).then_inc(dve2pe, -1)
                    for i in range(2):
                        pe_.matmul(ps[i][:, :], cst("replicate", NB), O[0:NB, NT, i * GBLK:(i + 1) * GBLK], start=True, stop=True)
                    pe_.matmul(ps[2][:, 0:SLOTS], cst("replicate", NB), IDX[0:NB, NT, :], start=True, stop=True)
                    pe_.matmul(ps[3][:, 0:SLOTS], cst("replicate", NB), GT[0:NB, NT, :], start=True, stop=True).then_inc(pe2dve, 1)
                    pe.wait_ge(dve2pe, 1).then_inc(dve2pe, -1)
                    for i in range(2):
                        last = pe_.matmul(ps[4 + i][0:NB, :], cst("gather8"), ACC[0][:, i * GBLK:(i + 1) * GBLK], start=True, stop=True)
                    last.then_inc(pe2dve, 1)

                @block.scalar
                def _(act):
                    def scores(t):
                        rows = P if t < NT else NB
                        act.wait_ge(pe2act, 1).then_inc(pe2act, -1)
                        for i in range(4):
                            last = act_.copy(SC[0:rows, 4 * i:4 * i + 4, :], ps[i][0:rows, :].rearrange("p (a e) -> p a e", a=4))
                        last.then_inc(act2dve, 1)

                    def gate_exp(t):
                        rows = P if t < NT else NB
                        act.wait_ge(dve2act, 1).then_inc(dve2act, -1)
                        act_.activation(GT[0:rows, t, :], GT[0:rows, t, :], ACT.Exp).then_inc(act2dve, 1)

                    scores(0)
                    gate_exp(0)
                    for t in range(NT):
                        scores(t + 1)
                        act.wait_ge(dve2act, 1).then_inc(dve2act, -1)
                        act_.activation(AV, AV, ACT.Gelu).then_inc(act2dve, 1)
                        gate_exp(t + 1)
                    act.wait_ge(dve2act, 1).then_inc(dve2act, -1)
                    act_.activation(A8[:, 0:PH], A8[:, 0:PH], ACT.Gelu).then_inc(act2dve, 1)

                @block.vector
                def _(dve):
                    def choose(t):
                        r = slice(0, P if t < NT else NB)

                        def best(src, spare, val, idx, n):
                            for g in range(n):
                                i_ = vec.max(val[r, g, 0:8], src[r, g, :])
                            i_.then_inc(dve_own, 1)
                            vec.wait_ge(dve_own, 1).then_inc(dve_own, -1)
                            yield
                            for g in range(n):
                                i_ = vec.max_index(idx[r, g, 0:8].bitcast(U32), val[r, g, 0:8], src[r, g, :])
                            i_.then_inc(dve_own, 1)
                            vec.wait_ge(dve_own, 1).then_inc(dve_own, -1)
                            yield
                            for g in range(n):
                                i_ = vec.match_replace(spare[r, g, :], val[r, g, 0:8], src[r, g, :], -3.0e38)
                            i_.then_inc(dve_own, 1)
                            vec.wait_ge(dve_own, 1).then_inc(dve_own, -1)
                            yield
                            for g in range(n):
                                i_ = vec.max(val[r, g, 8:16], spare[r, g, :])
                            i_.then_inc(dve_own, 1)
                            vec.wait_ge(dve_own, 1).then_inc(dve_own, -1)
                            yield
                            for g in range(n):
                                i_ = vec.max_index(idx[r, g, 8:16].bitcast(U32), val[r, g, 8:16], spare[r, g, :])
                            i_.then_inc(dve_own, 1)
                            vec.wait_ge(dve_own, 1).then_inc(dve_own, -1)

                        dve.wait_ge(act2dve, 1).then_inc(act2dve, -1)
                        dve.sem_inc(dve_free, 1)
                        yield from best(SC, SC2, TV, TI, 2 * PH)
                        vec.tensor_copy(TF[r], TI[r].bitcast(U32)).then_inc(dve_own, 1)
                        vec.wait_ge(dve_own, 1).then_inc(dve_own, -1)
                        yield
                        for h in range(PH):
                            i_ = vec.tensor_tensor(CA[r, h, :].rearrange("p (a b) -> p a b", a=TOPK), bc(TV[r, 2 * h, :], 2, TOPK),
                                                   bc(TV[r, 2 * h + 1, :], 1, TOPK), ALU.add)
                        i_.then_inc(dve_own, 1)
                        vec.wait_ge(dve_own, 1).then_inc(dve_own, -1)
                        yield from best(CA, SC3, BV, BI, PH)
                        bi = BI[r].rearrange("p h k -> p (h k)").bitcast(U32)
                        vec.tensor_scalar(AI[r].bitcast(U32), bi, 4, None, ALU.logical_shift_right).then_inc(dve_own, 1)
                        vec.wait_ge(dve_own, 1).then_inc(dve_own, -1)
                        vec.tensor_copy(AF[r], AI[r].bitcast(U32)).then_inc(dve_own, 1)
                        vec.wait_ge(dve_own, 1).then_inc(dve_own, -1)
                        vec.tensor_scalar(AI[r].bitcast(U32), bi, 15, None, ALU.bitwise_and).then_inc(dve_own, 1)
                        vec.wait_ge(dve_own, 1).then_inc(dve_own, -1)
                        vec.tensor_copy(BF[r], AI[r].bitcast(U32)).then_inc(dve_own, 1)
                        vec.wait_ge(dve_own, 1).then_inc(dve_own, -1)
                        for i, pos in enumerate((AF, BF)):
                            yield
                            eq = EQ[r].rearrange("p (m j) -> p m j", j=TOPK)
                            vec.tensor_tensor(eq, bc(pos[r], 2, TOPK), bc(cst("iota16")[r], 1, SLOTS), ALU.is_equal).then_inc(dve_own, 1)
                            vec.wait_ge(dve_own, 1).then_inc(dve_own, -1)
                            for h in range(PH):
                                e_h = EQ[r, h * 256:(h + 1) * 256].rearrange("p (k j) -> p k j", j=TOPK)
                                i_ = vec.tensor_tensor(e_h, e_h, bc(TF[r, 2 * h + i, :], 1, TOPK), ALU.mult)
                            i_.then_inc(dve_own, 1)
                            vec.wait_ge(dve_own, 1).then_inc(dve_own, -1)
                            yield
                            vec.tensor_reduce(pos[r], eq, AX, ALU.add).then_inc(dve_own, 1)
                            vec.wait_ge(dve_own, 1).then_inc(dve_own, -1)
                        vec.scalar_tensor_tensor(IDX[r, t, :], AF[r], float(PK), BF[r], ALU.mult, ALU.add).then_inc(dve_own, 1)
                        vec.wait_ge(dve_own, 1).then_inc(dve_own, -1)
                        vec.tensor_scalar(IDX[r, t, :], IDX[r, t, :], LB[r, 0:1], None, ALU.add).then_inc(dve_own, 1)
                        vec.wait_ge(dve_own, 1).then_inc(dve_own, -1)
                        vec.tensor_copy(IDI[r, t, :], IDX[r, t, :])
                        gt = GT[r, t, :].rearrange("p (h k) -> p h k", h=PH)
                        vec.tensor_tensor(gt, BV[r], bc(BV[r, :, 0], 2, TOPK), ALU.subtract).then_inc(dve2act, 1)
                        yield
                        dve.wait_ge(act2dve, 1).then_inc(act2dve, -1)
                        vec.tensor_reduce(SS[r, 0:PH], gt, AX, ALU.add).then_inc(dve_own, 1)
                        vec.wait_ge(dve_own, 1).then_inc(dve_own, -1)
                        vec.reciprocal(SS[r, 0:PH], SS[r, 0:PH]).then_inc(dve_own, 1)
                        vec.wait_ge(dve_own, 1).then_inc(dve_own, -1)
                        vec.tensor_tensor(gt, gt, bc(SS[r, 0:PH], 2, TOPK), ALU.mult).then_inc(dve2pool if t < NT else dve2pe, 1)

                    for _ in choose(0):
                        pass
                    done = 0
                    for t in range(NT):
                        nxt = choose(t + 1)
                        for seg in range(SEGS):
                            with dve.Fori(seg * PER, (seg + 1) * PER) as i:
                                for j in range(GR):
                                    dve.wait_ge(gathered[j], l * per_layer[j] + (i * 16 + (done + 16)))
                                    vec.tensor_tensor_reduce(G_[j], G_[j], O[:, t, :], 1.0, 0.0, ALU.mult, ALU.add, A8[:, j:j + 1]).then_inc(ring_free, 1)
                                vec.engine_nop().then_inc(dve_own, 1)
                                vec.wait_ge(dve_own, 1).then_inc(dve_own, -1)
                                vec.tensor_copy(AV[:, bass.ds(i * GR, GR)], A8).then_inc(dve_own, 1)
                                vec.wait_ge(dve_own, 1).then_inc(dve_own, -1)
                            next(nxt, None)
                            next(nxt, None)
                        done += SLOTS // GR * 16
                        dve.sem_inc(dve2act, 1)
                        dve.wait_ge(act2dve, 1).then_inc(act2dve, -1)
                        vec.tensor_tensor(AV, AV, GT[:, t, :], ALU.mult)
                        vec.memset(ACC[1], 0.0)
                        vec.memset(ACC[0], 0.0).then_inc(dve_own, 1)
                        vec.wait_ge(dve_own, 1).then_inc(dve_own, -1)
                        for seg in range(SEGS):
                            dve.sem_inc(dve_own, 1)
                            with dve.Fori(seg * PER, (seg + 1) * PER) as i:
                                for j in range(GR):
                                    dve.wait_ge(gathered[j], l * per_layer[j] + (i * 16 + (done + 16)))
                                    a = ACC[j % 2]
                                    vec.scalar_tensor_tensor(a, G_[j], AV[:, bass.ds(i * GR + j, 1)], a, ALU.mult, ALU.add).then_inc(dve_own, 1)
                                    dve.wait_ge(dve_own, 1).then_inc(dve_own, -1)
                                    dve.sem_inc(ring_free, 1)
                            dve.wait_ge(dve_own, 1).then_inc(dve_own, -1)
                            next(nxt, None)
                            next(nxt, None)
                        done += SLOTS // GR * 16
                        vec.tensor_tensor(ACC[0], ACC[0], ACC[1], ALU.add).then_inc(dve_own, 1)
                        vec.wait_ge(dve_own, 1).then_inc(dve_own, -1)
                        vec.tensor_tensor(ACC[0], ACC[0], GP, ALU.mult).then_inc(dve_own, 1)
                        vec.wait_ge(dve_own, 1).then_inc(dve_own, -1)
                        vec.tensor_tensor(X[:, t, :], X[:, t, :], ACC[0], ALU.add).then_inc(dve_own, 1)
                        vec.wait_ge(dve_own, 1).then_inc(dve_own, -1)
                        for _ in nxt:
                            pass
                    dve.sem_inc(ring_free, 1)
                    dve.wait_ge(pe2dve, 1).then_inc(pe2dve, -1)
                    for i in range(2):
                        vec.tensor_copy(XD[:, i * GBLK:(i + 1) * GBLK], ps[i][:, :])
                    sel = bc(cst("slot_of_row"), 1, PH)
                    for i in range(2):
                        v = JK[:, i * SLOTS:(i + 1) * SLOTS].rearrange("p (h k) -> p h k", h=PH)
                        vec.tensor_tensor(v, ps[2 + i][:, 0:SLOTS].rearrange("p (h k) -> p h k", h=PH), sel, ALU.mult).then_inc(dve_own, 1)
                        vec.wait_ge(dve_own, 1).then_inc(dve_own, -1)
                        vec.tensor_reduce(IW[:, i * PH:(i + 1) * PH], v, AX, ALU.add).then_inc(dve_own, 1)
                        vec.wait_ge(dve_own, 1).then_inc(dve_own, -1)
                    vec.tensor_copy(IWI, IW[:, 0:PH]).then_inc(dve2pool, 1)
                    for j in range(PH):
                        dve.wait_ge(gathered[j], l * per_layer[j] + (done + 16))
                        i_ = vec.tensor_tensor_reduce(G_[j], G_[j], XD, 1.0, 0.0, ALU.mult, ALU.add, A8[:, j:j + 1])
                    i_.then_inc(dve2act, 1)
                    dve.wait_ge(act2dve, 1).then_inc(act2dve, -1)
                    vec.tensor_tensor(A8[:, 0:PH], A8[:, 0:PH], IW[:, PH:2 * PH], ALU.mult).then_inc(dve_own, 1)
                    vec.wait_ge(dve_own, 1).then_inc(dve_own, -1)
                    vec.memset(ACC[0], 0.0).then_inc(dve_own, 1)
                    vec.wait_ge(dve_own, 1).then_inc(dve_own, -1)
                    for j in range(PH):
                        dve.wait_ge(gathered[PH + j], l * per_layer[PH + j] + (done + 16))
                        vec.scalar_tensor_tensor(ACC[0], G_[PH + j], A8[:, j:j + 1], ACC[0], ALU.mult, ALU.add).then_inc(dve_own, 1)
                        vec.wait_ge(dve_own, 1).then_inc(dve_own, -1)
                    dve.sem_inc(dve2pe, 1)
                    dve.wait_ge(pe2dve, 1).then_inc(pe2dve, -1)
                    for i in range(2):
                        c = slice(i * GBLK, (i + 1) * GBLK)
                        vec.tensor_tensor(TM[0:NB, :], ps[4 + i][0:NB, :], MOD9[0:NB, 5 * D + i * GBLK:5 * D + (i + 1) * GBLK], ALU.mult).then_inc(dve_own, 1)
                        vec.wait_ge(dve_own, 1).then_inc(dve_own, -1)
                        vec.tensor_tensor(X[0:NB, NT, c], X[0:NB, NT, c], TM[0:NB, :], ALU.add).then_inc(dve_own, 1)
                        vec.wait_ge(dve_own, 1).then_inc(dve_own, -1)
                    vec.tensor_scalar(LB, LB, float(EXPERTS), None, ALU.add)
            AR.at = mark

        nc_page_table = AR.room(NB * PAGES, rows=1).bitcast(I32)
        with nc.Block() as block:
            @block.sync
            def _(sp):
                sp.dma_start(nc_page_table, ins["page_table"].rearrange("b j -> (b j)").unsqueeze(0)).then_inc(loaded, 16)
                sp.wait_ge(loaded, 16).then_inc(loaded, -16)

        with nc.Fori(0, DEPTH) as l:
            mark = AR.at
            modulation(l)
            G = AR.room(2 * TILES, NH).rearrange("p (c t) h -> p c t h", c=2)
            PZ = AR.room(TILES, NH * DK)
            BA = AR.room(TILES, 8)
            BT = AR.room(CC, SEQ + 3)
            DB = AR.room(CONV_CH)
            inner = AR.at
            PA = AR.room(TILES, 3 * AW)
            PC = AR.room(TILES, 3 * AW)
            inner2 = AR.at
            with nc.Block() as block:
                @block.gpsimd
                def _(pool):
                    for a in (PA, PC, PZ, BA, O):
                        nc.gpsimd.memset(a[:, NT, :], 0.0)
            HT = AR.room(KD, SEQ + NB)
            norm(0, HT)
            project(l, HT, PA, PC, PZ, BA, BT, DB)
            AR.at = inner2
            heads_of_a_and_c(l, PA, PC)
            QT = AR.room(8, SEQ)
            transpose_heads(PA, PC, QT)
            attend_a(QT, PA)
            attend_c(QT, PC)
            AR.at = inner2
            attend_sample(l, "a", PA)
            attend_sample(l, "c", PC)
            AR.at = inner
            convolve(l, BT)
            gates(l, BA, G)
            delta_sample(l, DB, G)
            delta_prompt(l, BT, G, PZ)
            gated_norm(l, PZ)
            AR.at = mark
            out_projection(l)
            peer(l)
            AR.at = mark

        with nc.Block() as block:
            @block.sync
            def _(sp):
                sp.dma_start(outs["y_prompt"][0].rearrange("(t p) d -> p t d", p=P), X[:, 0:NT, :]).then_inc(stored, 16)
                sp.dma_start(outs["y_sample"].rearrange("b s d -> (b s) d"), X[0:NB, NT, :]).then_inc(stored, 16)
                sp.wait_ge(stored, 32).then_inc(stored, -32)


_INS = ["x_prompt", "x_sample", "cache_win_k", "cache_win_v", "cache_sb_k", "cache_sb_v", "state_conv", "state_delta",
        "page_table", "c_prompt", "c_sample", "w_ada", "b_ada", "norm1_g", "norm2_g", "w_in", "b_q_c", "b_k_c",
        "qnorm_a", "knorm_a", "conv_w", "a_log", "dt_bias", "gnorm_b", "w_out", "peer_wq", "peer_keys", "peer_u", "peer_v"]
_OUTS = [("y_prompt", (1, SEQ, D)), ("y_sample", (NB, 1, D)),
         ("win_k_prompt", (DEPTH, 1, SEQ, NH, HD)), ("win_v_prompt", (DEPTH, 1, SEQ, NH, HD)),
         ("win_k_sample", (DEPTH, NB, 1, NH, HD)), ("win_v_sample", (DEPTH, NB, 1, NH, HD)),
         ("sb_k_prompt", (DEPTH, 1, SEQ, NH, HD)), ("sb_v_prompt", (DEPTH, 1, SEQ, NH, HD)),
         ("sb_k_sample", (DEPTH, NB, 1, NH, HD)), ("sb_v_sample", (DEPTH, NB, 1, NH, HD)),
         ("conv_prompt", (DEPTH, 1, KW - 1, CONV_CH)), ("conv_sample", (DEPTH, NB, KW - 1, CONV_CH)),
         ("delta_prompt", (DEPTH, 1, NH, DK, DK)), ("delta_sample", (DEPTH, NB, NH, DK, DK))]


def kernel(**inputs):
    import numpy as _np
    import concourse.bacc as _bacc
    from concourse import mybir as _mybir
    from concourse.bass_utils import run_bass_kernel_spmd as _run

    nc = _bacc.Bacc("TRN2", target_bir_lowering=False, num_devices=1)
    arrays, ins, outs = {}, {}, {}
    for name in _INS + ["consts"]:
        a = constants() if name == "consts" else _np.ascontiguousarray(inputs[name])
        arrays[f"in_{name}_dram"] = a
        ins[name] = nc.dram_tensor(f"in_{name}_dram", a.shape, _mybir.dt.from_np(a.dtype), kind="ExternalInput").ap()
    for name, shape in _OUTS:
        outs[name] = nc.dram_tensor(f"out_{name}_dram", shape, _mybir.dt.from_np(_np.dtype("float32")), kind="ExternalOutput").ap()
    build(nc, ins, outs)
    r = _run(nc, [arrays], core_ids=[0])
    return tuple(r.results[0][f"out_{name}_dram"] for name, _ in _OUTS)
```

```python
from contextlib import ExitStack

import numpy as np

import concourse.bass as bass
from concourse import mybir

P = 128
D = 1024
KD = D // P
SEQ = 512
NT = SEQ // P
TILES = NT + 1
NB = 8
DEPTH = 2
HD = 64
NH = 4
AW = NH * HD
DK = 128
CONV_CH = 3 * NH * DK
CC = CONV_CH // P
KW = 4
N_IN = 3592
PAST = 2048
PAGES = PAST // P
PH = 8
PK = 128
TOPK = 16
EXPERTS = PK * PK
SLOTS = PH * TOPK
RMS_EPS = 1e-6
NEG = -30000.0
LEVELS = 7
MOD = 6 * D
GBLK = 512

F32 = mybir.dt.float32
I32 = mybir.dt.int32
U32 = mybir.dt.uint32
ALU = mybir.AluOpType
ACT = mybir.ActivationFunctionType
AX = mybir.AxisListType.X

CONST_COLS = [("ident", P), ("upper", P), ("neg_lower", P), ("ones", P), ("neg_ones", P),
              ("neg_mask", P), ("strict_upper", P), ("strict_lower", P), ("levels", LEVELS * P),
              ("log_count", SEQ), ("rope", TILES * 64), ("iota16", 16), ("pick_row", NB * P),
              ("replicate", P), ("gather8", NB), ("head_diag", AW), ("place", NB * NB),
              ("own_mask", 16), ("slot_of_row", 16), ("row8", P), ("eps", 8)]
CONST_AT = {}
_at = 0
for _n, _w in CONST_COLS:
    CONST_AT[_n] = (_at, _at + _w)
    _at += _w
CONST_W = _at


def constants():
    c = np.zeros((P, CONST_W), np.float32)

    def put(name, a):
        lo, _ = CONST_AT[name]
        a = np.asarray(a, np.float32)
        c[:a.shape[0], lo:lo + a.shape[1]] = a

    r = np.arange(P)
    put("ident", np.eye(P))
    put("upper", r[:, None] <= r[None, :])
    put("neg_lower", -(r[:, None] >= r[None, :]).astype(np.float32))
    put("ones", np.ones((P, P)))
    put("neg_ones", -np.ones((P, P)))
    put("neg_mask", np.where(r[:, None] >= r[None, :], NEG, 0.0))
    put("strict_upper", r[:, None] < r[None, :])
    put("strict_lower", r[:, None] > r[None, :])
    lv = []
    for k in range(LEVELS):
        b = 1 << k
        lv.append((r[:, None] // (2 * b) == r[None, :] // (2 * b)) & (r[:, None] // b == r[None, :] // b + 1))
    put("levels", np.concatenate(lv, 1))
    dist = r[:, None] + 384 - np.arange(SEQ)[None, :]
    cnt = np.zeros(dist.shape)
    for window, dil in ((128, 1), (512, 4), (2048, 16)):
        cnt += (dist >= 0) & (dist <= window) & (dist % dil == 0)
    put("log_count", np.where(cnt > 0, np.log(np.maximum(cnt, 1)), NEG))
    half = HD // 2
    inv = np.float32(10000.0) ** (-np.arange(half, dtype=np.float32) / np.float32(half))
    rope = np.zeros((P, TILES, 2, half), np.float32)
    for t in range(TILES):
        pos = (t * P + r if t < NT else np.full(P, PAST)).astype(np.float32)
        ang = (pos[:, None] * inv[None, :]).astype(np.float32)
        rope[:, t, 0] = np.cos(ang)
        rope[:, t, 1] = np.sin(ang)
    put("rope", rope.reshape(P, -1))
    put("iota16", np.tile(np.arange(16), (P, 1)))
    pick = np.zeros((NB, NB, P))
    for b in range(NB):
        pick[b, b] = 1
    put("pick_row", pick.reshape(NB, -1))
    put("replicate", (r[None, :] % NB) == np.arange(NB)[:, None])
    put("gather8", (r[:, None] % NB) == np.arange(NB)[None, :])
    put("head_diag", (np.arange(AW)[None, :] // HD) == np.arange(NH)[:, None])
    place = np.zeros((NH, NB, NB))
    for b in range(NB):
        place[:, b, b] = 1
    put("place", place.reshape(NH, -1))
    own = np.zeros((P, 4, NH))
    own[3:, 3, :] = NEG
    put("own_mask", own.reshape(P, 16))
    put("slot_of_row", (r[:, None] // NB) == np.arange(16)[None, :])
    row8 = np.zeros((NB + 1, P))
    row8[NB] = 1
    put("row8", row8)
    put("eps", np.full((P, 8), RMS_EPS))
    return c


class Arena:

    def __init__(self, sbuf, cols):
        self.sbuf, self.cols, self.at = sbuf, cols, 0

    def room(self, *dims, rows=P):
        n = int(np.prod(dims))
        lo = self.at
        self.at += (n + 7) // 8 * 8
        assert self.at <= self.cols, (self.at, self.cols)
        v = self.sbuf[0:rows, lo:lo + n]
        if len(dims) == 2:
            v = v.rearrange("p (a b) -> p a b", a=dims[0])
        if len(dims) == 3:
            v = v.rearrange("p (a b c) -> p a b c", a=dims[0], b=dims[1])
        return v


def bc(ap, axis, n):
    u = ap.unsqueeze(axis)
    return u.broadcast_to([n if i == axis else s for i, s in enumerate(u.shape)])


def build(nc, ins, outs):
    x_prompt, x_sample = ins["x_prompt"], ins["x_sample"]
    with ExitStack() as ctx:
        def sem(name):
            return ctx.enter_context(nc.semaphore(name))

        arena_cols = 52800
        AR = Arena(ctx.enter_context(nc.sbuf_tensor("arena", [P, arena_cols], F32)), arena_cols)
        ps = [ctx.enter_context(nc.psum_tensor(f"bank{i}", [P, GBLK], F32)) for i in range(8)]

        loaded = sem("loaded")
        loaded2 = sem("loaded2")
        w_landed = [sem(f"w_landed{i}") for i in range(3)]
        w_used = sem("w_used")
        w_used_act = sem("w_used_act")
        v_landed = [sem(f"v_landed{i}") for i in range(4)]
        v_used = sem("v_used")
        stored = sem("stored")
        dve_own = sem("dve_own")
        act_own = sem("act_own")
        pool_own = sem("pool_own")
        pe2dve = sem("pe2dve")
        pe2act = sem("pe2act")
        dve2pe = sem("dve2pe")
        act2pe = sem("act2pe")
        dve2act = sem("dve2act")
        act2dve = sem("act2dve")
        act_free = sem("act_free")
        dve_free = sem("dve_free")
        dve2sp = sem("dve2sp")
        act2sp = sem("act2sp")
        dve2pool = sem("dve2pool")
        pool2dve = sem("pool2dve")
        pool2pe = sem("pool2pe")
        ring_free = sem("ring_free")
        GR = 16
        LOT = 4
        gathered = [sem(f"gathered{i}") for i in range(GR)]

        def rsqrt(out, in_, scale):
            act_.activation(out, in_, ACT.Ln, scale=scale, bias=cst("eps")[0:in_.shape[0], 0:1]).then_inc(act_own, 1)
            act_.wait_ge(act_own, 1).then_inc(act_own, -1)
            return act_.activation(out, out, ACT.Exp, scale=-0.5)

        X = AR.room(TILES, D)
        CN = AR.room(CONST_W)
        MOD9 = AR.room(MOD)
        O = AR.room(TILES, D)
        CT = AR.room(KD, NB + 1)
        LB = AR.room(8)

        def cst(name, rows=P):
            lo, hi = CONST_AT[name]
            return CN[0:rows, lo:hi]

        ident = cst("ident")
        vec, act_, pe_ = nc.vector, nc.scalar, nc.tensor
        base_mark = AR.at

        C9 = AR.room(D)
        with nc.Block() as block:
            @block.sync
            def _(sp):
                sp.dma_start(CN, ins["consts"]).then_inc(loaded, 16)
                sp.dma_start(C9[0:NB, :], ins["c_sample"]).then_inc(loaded, 16)
                sp.dma_start(C9[NB:NB + 1, :], ins["c_prompt"]).then_inc(loaded, 16)
                sp.dma_start(X[:, 0:NT, :], x_prompt[0].rearrange("(t p) d -> p t d", p=P)).then_inc(loaded2, 16)
                sp.dma_start(X[0:NB, NT, :], x_sample.rearrange("b s d -> (b s) d")).then_inc(loaded2, 16)
                sp.wait_ge(loaded2, 32).then_inc(loaded2, -32)

            @block.vector
            def _(dve):
                vec.memset(LB, 0.0)

            @block.scalar
            def _(act):
                act.wait_ge(loaded, 48).then_inc(loaded, -48)
                act_.activation(C9[0:NB + 1, :], C9[0:NB + 1, :], ACT.Silu).then_inc(act2pe, 1)
                act.wait_ge(pe2act, 1).then_inc(pe2act, -1)
                act_.copy(CT, ps[0][:, 0:KD * (NB + 1)].rearrange("p (k n) -> p k n", k=KD))

            @block.tensor
            def _(pe):
                pe.wait_ge(act2pe, 1).then_inc(act2pe, -1)
                for k in range(KD):
                    last = pe_.transpose(ps[0][:, k * 9:k * 9 + 9], C9[0:9, k * P:(k + 1) * P], ident[0:9, 0:9])
                last.then_inc(pe2act, 1)
        AR.at = base_mark

        def modulation(l):
            mark = AR.at
            W = [AR.room(KD, GBLK) for _ in range(3)]
            BA = AR.room(MOD, rows=NB + 1)
            NG = AR.room(2, D, rows=NB + 1)
            wa = ins["w_ada"][l].rearrange("(k p) n -> p k n", p=P)
            R9 = NB + 1
            with nc.Block() as block:
                @block.sync
                def _(sp):
                    sp.dma_start(BA, ins["b_ada"][l].partition_broadcast(R9)).then_inc(loaded, 16)
                    sp.dma_start(NG[:, 0, :], ins["norm1_g"][l].partition_broadcast(R9)).then_inc(loaded, 16)
                    sp.dma_start(NG[:, 1, :], ins["norm2_g"][l].partition_broadcast(R9)).then_inc(loaded, 16)
                    for n in range(MOD // GBLK):
                        if n >= 3:
                            sp.wait_ge(w_used, 1).then_inc(w_used, -1)
                        sp.dma_start(W[n % 3], wa[:, :, n * GBLK:(n + 1) * GBLK]).then_inc(w_landed[n % 3], 16)
                    sp.wait_ge(w_used, 3).then_inc(w_used, -3)

                @block.tensor
                def _(pe):
                    for n in range(MOD // GBLK):
                        pe.wait_ge(w_landed[n % 3], 16).then_inc(w_landed[n % 3], -16)
                        if n >= 2:
                            pe.wait_ge(dve_free, 1).then_inc(dve_free, -1)
                        for k in range(KD):
                            last = pe_.matmul(ps[n % 2][0:R9, :], CT[:, k, :], W[n % 3][:, k, :],
                                              start=(k == 0), stop=(k == KD - 1))
                        last.then_inc(pe2dve, 1)
                    pe.wait_ge(dve_free, 2).then_inc(dve_free, -2)

                @block.vector
                def _(dve):
                    dve.wait_ge(loaded, 48).then_inc(loaded, -48)
                    for n in range(MOD // GBLK):
                        c = slice(n * GBLK, (n + 1) * GBLK)
                        dve.wait_ge(pe2dve, 1).then_inc(pe2dve, -1)
                        dve.sem_inc(w_used, 1)
                        vec.tensor_tensor(MOD9[0:R9, c], ps[n % 2][0:R9, :], BA[:, c], ALU.add).then_inc(dve_free, 1)
                    vec.memset(BA[:, 0:1], 0.0).then_inc(dve_own, 1)
                    vec.wait_ge(dve_own, 1).then_inc(dve_own, -1)
                    for i, s in enumerate((1, 4)):
                        seg = MOD9[0:R9, s * D:(s + 1) * D]
                        vec.scalar_tensor_tensor(seg, seg, 1.0, NG[:, i, :], ALU.add, ALU.mult)
            AR.at = mark

        def norm(shift, HT, load_ahead, scratch):
            mark = AR.at
            AR.at = scratch
            SEG = AR.room(2, D)
            SQ = [AR.room(D) for _ in range(2)]
            SS = AR.room(TILES)
            RS = AR.room(TILES)
            with nc.Block() as block:
                @block.sync
                def _(sp):
                    load_ahead(sp)

                @block.tensor
                def _(pe):
                    for i in range(4):
                        c = (shift + i // 2) * D + (i % 2) * GBLK
                        last = pe_.matmul(ps[i][:, :], cst("row8", NB + 1), MOD9[0:NB + 1, c:c + GBLK], start=True, stop=True)
                    last.then_inc(pe2dve, 1)
                    for t in range(TILES):
                        rows = P if t < NT else NB
                        pe.wait_ge(dve2pe, 1).then_inc(dve2pe, -1)
                        for half in range(2):
                            g = 2 * t + half
                            if g >= 4:
                                pe.wait_ge(act_free, 1).then_inc(act_free, -1)
                            bank = ps[4 + g % 4]
                            for j in range(4):
                                k = half * 4 + j
                                last = pe_.transpose(bank[:, j * P:j * P + rows], O[0:rows, t, k * P:(k + 1) * P], ident[0:rows, 0:rows])
                            last.then_inc(pe2act, 1)
                    pe.wait_ge(act_free, 4).then_inc(act_free, -4)

                @block.scalar
                def _(act):
                    for t in range(0, TILES, 2):
                        rows = P if t < NT else NB
                        act_.activation(SQ[0][0:rows, :], X[0:rows, t, :], ACT.Square, accum_out=SS[0:rows, t:t + 1]).then_inc(act_own, 1)
                        act_.wait_ge(act_own, 1).then_inc(act_own, -1)
                    act.wait_ge(dve2act, 1).then_inc(dve2act, -1)
                    rsqrt(RS[:, 0:NT], SS[:, 0:NT], 1.0 / D)
                    rsqrt(RS[0:NB, NT:TILES], SS[0:NB, NT:TILES], 1.0 / D).then_inc(act2dve, 1)
                    for t in range(TILES):
                        rows = P if t < NT else NB
                        for half in range(2):
                            g = 2 * t + half
                            act.wait_ge(pe2act, 1).then_inc(pe2act, -1)
                            act_.copy(HT[:, half * 4:half * 4 + 4, t * P:t * P + rows],
                                      ps[4 + g % 4][:, :].rearrange("p (j n) -> p j n", j=4)[:, :, 0:rows]).then_inc(act_free, 1)

                @block.vector
                def _(dve):
                    for t in range(1, TILES, 2):
                        i_ = vec.tensor_tensor_reduce(SQ[1], X[:, t, :], X[:, t, :], 1.0, 0.0, ALU.mult, ALU.add, SS[:, t:t + 1])
                        if t + 2 < TILES:
                            i_.then_inc(dve_own, 1)
                            vec.wait_ge(dve_own, 1).then_inc(dve_own, -1)
                    i_.then_inc(dve2act, 1)
                    dve.wait_ge(pe2dve, 1).then_inc(pe2dve, -1)
                    for i in range(4):
                        i_ = vec.tensor_copy(SEG[:, i // 2, (i % 2) * GBLK:(i % 2 + 1) * GBLK], ps[i][:, :])
                    i_.then_inc(dve_own, 1)
                    vec.wait_ge(dve_own, 1).then_inc(dve_own, -1)
                    dve.wait_ge(act2dve, 1).then_inc(act2dve, -1)
                    for t in range(TILES):
                        rows = P if t < NT else NB
                        sh = SEG[:, 0, :] if t < NT else MOD9[0:NB, shift * D:(shift + 1) * D]
                        gn = SEG[:, 1, :] if t < NT else MOD9[0:NB, (shift + 1) * D:(shift + 2) * D]
                        h = O[0:rows, t, :]
                        vec.scalar_tensor_tensor(h, X[0:rows, t, :], RS[0:rows, t:t + 1], gn, ALU.mult, ALU.mult).then_inc(dve_own, 1)
                        vec.wait_ge(dve_own, 1).then_inc(dve_own, -1)
                        vec.tensor_tensor(h, h, sh, ALU.add).then_inc(dve2pe, 1)
            AR.at = mark

        CHUNKS = [(768, 1280, "b"), (1280, 1792, "b"), (1792, 2304, "b"), (0, 512, "a"), (512, 768, "a"),
                  (2304, 2816, "z"), (2816, 3080, "g"), (3080, 3592, "c")]

        def w_in_tile(l, W, n):
            lo, hi, _ = CHUNKS[n]
            return W[n % 2][:, :, 0:hi - lo], ins["w_in"][l].rearrange("(k p) n -> p k n", p=P)[:, :, lo:hi]

        def project(l, HT, W, PA, PC, PZ, BA, BT, DB):
            mark = AR.at
            CWR = AR.room(P, rows=KW * CC)
            CW = AR.room(KW, CC)
            LAST = AR.room(P, rows=(KW - 1) * CC)
            LC = AR.room(KW - 1, CC)
            TMP = [O[:, i // 2, (i % 2) * SEQ:(i % 2 + 1) * SEQ] for i in range(4)]
            RN = [O[:, 2, i * SEQ:(i + 1) * SEQ] for i in range(2)]
            groups = []
            for n, (lo, hi, kind) in enumerate(CHUNKS):
                mine = []
                if kind == "b":
                    mine += [(n, "feature", c, lo, hi) for c in range((lo - 768) // P, (hi - 768) // P)]
                    mine += [(n, "b", NT, lo, hi)]
                else:
                    mine += [(n, kind, t, lo, hi) for t in range(TILES)]
                groups += [g + (i == len(mine) - 1,) for i, g in enumerate(mine)]
            ends_b = sum(g[1] in ("feature", "b") for g in groups)
            BANKS = 6
            norms_from = ends_b + 9
            assert norms_from + 8 <= len(groups)
            by_act = lambda i: i % 2 == 0 or i >= ends_b
            freed = [w_used_act if by_act(i) else w_used for i, g in enumerate(groups) if g[5]]

            def result(g):
                _, kind, t, lo, hi, _ = g
                rows = P if kind == "feature" or t < NT else NB
                if kind == "feature":
                    return [(BT[:, t, 3:3 + SEQ], P, 0, SEQ)]
                if kind == "a":
                    return [(PA[0:rows, t, lo:hi], rows, 0, hi - lo)]
                if kind == "b":
                    return [(DB[0:NB, lo - 768:hi - 768], rows, 0, hi - lo)]
                if kind == "z":
                    return [(PZ[0:rows, t, :], rows, 0, GBLK)]
                if kind == "g":
                    return [(BA[0:rows, t, :], rows, 0, 8), (PC[0:rows, t, 0:AW], rows, 8, 8 + AW)]
                return [(PC[0:rows, t, AW:3 * AW], rows, 0, 2 * AW)]

            with nc.Block() as block:
                @block.sync
                def _(sp):
                    sp.dma_start(CWR, ins["conv_w"][l].rearrange("j (c p) -> (j c) p", p=P)).then_inc(loaded, 16)
                    for n in range(2, len(CHUNKS)):
                        sp.wait_ge(freed[n - 2], 1).then_inc(freed[n - 2], -1)
                        sp.dma_start(*w_in_tile(l, W, n)).then_inc(w_landed[n % 2], 16)
                    sp.wait_ge(act2sp, 1).then_inc(act2sp, -1)
                    sp.dma_start(outs["conv_prompt"][l, 0].rearrange("j (c p) -> (j c) p", p=P), LAST).then_inc(stored, 16)
                    sp.wait_ge(stored, 16).then_inc(stored, -16)
                    sp.wait_ge(freed[-2], 1).then_inc(freed[-2], -1)
                    sp.wait_ge(freed[-1], 1).then_inc(freed[-1], -1)

                @block.tensor
                def _(pe):
                    for i, (n, kind, t, lo, hi, last) in enumerate(groups):
                        if i == 0 or groups[i - 1][0] != n:
                            pe.wait_ge(w_landed[n % 2], 16).then_inc(w_landed[n % 2], -16)
                        if i >= BANKS:
                            pe.wait_ge(act_free if by_act(i - BANKS) else dve_free, 1).then_inc(act_free if by_act(i - BANKS) else dve_free, -1)
                        for k in range(KD):
                            if kind == "feature":
                                off = t * P - (lo - 768)
                                mm = pe_.matmul(ps[i % BANKS][:, :], W[n % 2][:, k, off:off + P], HT[:, k, 0:SEQ],
                                                start=(k == 0), stop=(k == KD - 1))
                            else:
                                rows = P if t < NT else NB
                                mm = pe_.matmul(ps[i % BANKS][0:rows, 0:hi - lo], HT[:, k, t * P:t * P + rows],
                                                W[n % 2][:, k, 0:hi - lo], start=(k == 0), stop=(k == KD - 1))
                        mm.then_inc(pe2act if by_act(i) else pe2dve, 1)
                        if i == ends_b - 1:
                            pe.wait_ge(loaded, 16).then_inc(loaded, -16)
                            pe_.transpose(ps[6][:, 0:KW * CC], CWR, ident[0:KW * CC, 0:KW * CC]).then_inc(pe2dve, 1)
                        if i == ends_b:
                            pe.wait_ge(dve2pe, 1).then_inc(dve2pe, -1)
                            pe_.transpose(ps[7][0:(KW - 1) * CC, 0:P], LC.rearrange("p j c -> p (j c)"), ident).then_inc(pe2act, 1)
                        c = i - norms_from
                        if 0 <= c < 8:
                            pe.wait_ge(dve2pe, 1).then_inc(dve2pe, -1)
                            pe_.matmul(ps[6 + c % 2][:, :], cst("ones"), TMP[2 + c % 2], start=True, stop=True).then_inc(pe2act, 1)
                    for i in range(len(groups) - BANKS, len(groups)):
                        pe.wait_ge(act_free if by_act(i) else dve_free, 1).then_inc(act_free if by_act(i) else dve_free, -1)

                @block.scalar
                def _(act):
                    for i, g in enumerate(groups):
                        if by_act(i):
                            act.wait_ge(pe2act, 1).then_inc(pe2act, -1)
                            if g[5]:
                                act.sem_inc(w_used_act, 1)
                            for dst, rows, lo, hi in result(g):
                                last = act_.copy(dst, ps[i % BANKS][0:rows, lo:hi])
                            last.then_inc(act_free, 1)
                        if i == ends_b - 1:
                            act_.copy(RN[0][0:1, 0:1], cst("ones")[0:1, 0:1]).then_inc(act2dve, 1)
                        if i == ends_b:
                            act.wait_ge(pe2act, 1).then_inc(pe2act, -1)
                            act_.copy(LAST, ps[7][0:(KW - 1) * CC, 0:P]).then_inc(act2sp, 1)
                        for c in (2 * (i - ends_b), 2 * (i - ends_b) + 1):
                            if 0 <= c < CC:
                                act.wait_ge(dve2act, 1).then_inc(dve2act, -1)
                                act_.activation(BT[:, c, 3:3 + SEQ], TMP[c % 2], ACT.Silu).then_inc(act2dve, 1)
                        if i == norms_from - 1:
                            act_.preload_act_table_set("natural_log_exp_and_others")
                        c = i - norms_from
                        if 0 <= c < 8:
                            act.wait_ge(pe2act, 1).then_inc(pe2act, -1)
                            rsqrt(RN[c % 2], ps[6 + c % 2][:, :], 1.0).then_inc(act2dve, 1)

                @block.vector
                def _(dve):
                    for i, g in enumerate(groups):
                        if not by_act(i):
                            dve.wait_ge(pe2dve, 1).then_inc(pe2dve, -1)
                            if g[5]:
                                dve.sem_inc(w_used, 1)
                            for dst, rows, lo, hi in result(g):
                                last = vec.tensor_copy(dst, ps[i % BANKS][0:rows, lo:hi])
                            last.then_inc(dve_free, 1)
                    dve.wait_ge(pe2dve, 1).then_inc(pe2dve, -1)
                    vec.tensor_copy(CW, ps[6][:, 0:KW * CC].rearrange("p (j c) -> p j c", j=KW)).then_inc(dve_own, 1)
                    vec.wait_ge(dve_own, 1).then_inc(dve_own, -1)
                    dve.wait_ge(act2dve, 1).then_inc(act2dve, -1)
                    dve.wait_ge(pool2dve, 1).then_inc(pool2dve, -1)
                    vec.tensor_copy(LC, BT[:, :, SEQ:SEQ + KW - 1].rearrange("p c j -> p j c")).then_inc(dve_own, 1)
                    vec.wait_ge(dve_own, 1).then_inc(dve_own, -1)
                    dve.sem_inc(dve2pe, 1)
                    for c in range(CC):
                        if c >= 2:
                            dve.wait_ge(act2dve, 1).then_inc(act2dve, -1)
                        t = TMP[c % 2]
                        vec.tensor_scalar(t, BT[:, c, 0:SEQ], CW[:, 0, c:c + 1], None, ALU.mult).then_inc(dve_own, 1)
                        vec.wait_ge(dve_own, 1).then_inc(dve_own, -1)
                        for j in range(1, KW):
                            i_ = vec.scalar_tensor_tensor(t, BT[:, c, j:j + SEQ], CW[:, j, c:c + 1], t, ALU.mult, ALU.add)
                            if j < KW - 1:
                                i_.then_inc(dve_own, 1)
                                vec.wait_ge(dve_own, 1).then_inc(dve_own, -1)
                        i_.then_inc(dve2act, 1)
                    dve.wait_ge(act2dve, 2).then_inc(act2dve, -2)
                    for c in range(8 + 1):
                        if c < 8:
                            u = BT[:, c, 3:3 + SEQ]
                            vec.tensor_tensor(TMP[2 + c % 2], u, u, ALU.mult).then_inc(dve2pe, 1)
                        if c >= 1:
                            k = c - 1
                            u = BT[:, k, 3:3 + SEQ]
                            dve.wait_ge(act2dve, 1).then_inc(act2dve, -1)
                            vec.scalar_tensor_tensor(u, u, DK ** -0.5 if k < NH else 1.0, RN[k % 2], ALU.mult, ALU.mult)

                @block.gpsimd
                def _(pool):
                    nc.gpsimd.memset(BT[:, :, 0:3], 0.0).then_inc(pool2dve, 1)
            AR.at = mark

        def heads_of_a_and_c(l, PA, PC):
            mark = AR.at
            GA = AR.room(8, HD)
            BC = AR.room(2 * AW)
            SQ = AR.room(TILES, 8, HD)
            SS = AR.room(TILES, 8)
            T1 = AR.room(TILES, 8, HD // 2)
            T2 = AR.room(TILES, 8, HD // 2)
            T3 = AR.room(TILES, 8, HD // 2)
            qk = PA[:, :, 0:2 * AW].rearrange("p t (h e) -> p t h e", e=HD)
            rope = cst("rope").rearrange("p (t c e) -> p t c e", t=TILES, c=2)
            cos, sin = (bc(rope[:, :, c, :], 2, 8) for c in range(2))
            with nc.Block() as block:
                @block.scalar
                def _(act):
                    act.wait_ge(dve2act, 1).then_inc(dve2act, -1)
                    rsqrt(SS, SS, 1.0 / HD).then_inc(act2dve, 1)

                @block.sync
                def _(sp):
                    for h in range(8):
                        g = ins["qnorm_a"] if h < NH else ins["knorm_a"]
                        sp.dma_start(GA[:, h, :], g[l].partition_broadcast(P)).then_inc(loaded, 16)
                    sp.dma_start(BC[:, 0:AW], ins["b_q_c"][l].partition_broadcast(P)).then_inc(loaded, 16)
                    sp.dma_start(BC[:, AW:2 * AW], ins["b_k_c"][l].partition_broadcast(P)).then_inc(loaded, 16)
                    sp.wait_ge(dve2sp, 1).then_inc(dve2sp, -1)
                    for i, src in ((0, PC), (1, PA)):
                        if i == 1:
                            sp.wait_ge(dve2sp, 1).then_inc(dve2sp, -1)
                        names = ("sb_k", "sb_v") if i == 0 else ("win_k", "win_v")
                        for name, lo in zip(names, (AW, 2 * AW)):
                            sp.dma_start(outs[name + "_prompt"][l, 0].rearrange("(t p) h e -> p t (h e)", p=P),
                                         src[:, 0:NT, lo:lo + AW]).then_inc(stored, 16)
                            sp.dma_start(outs[name + "_sample"][l, :, 0].rearrange("b h e -> b (h e)"),
                                         src[0:NB, NT, lo:lo + AW]).then_inc(stored, 16)

                @block.vector
                def _(dve):
                    dve.wait_ge(loaded, 160).then_inc(loaded, -160)
                    qkc = PC[:, :, 0:2 * AW]
                    vec.tensor_tensor(qkc, qkc, bc(BC, 1, TILES), ALU.add).then_inc(dve2sp, 1)
                    for t in range(TILES):
                        vec.tensor_tensor(SQ[:, t], qk[:, t], qk[:, t], ALU.mult)
                    vec.engine_nop().then_inc(dve_own, 1)
                    vec.wait_ge(dve_own, 1).then_inc(dve_own, -1)
                    vec.tensor_reduce(SS, SQ, AX, ALU.add).then_inc(dve2act, 1)
                    dve.wait_ge(act2dve, 1).then_inc(act2dve, -1)
                    vec.tensor_tensor(qk, qk, bc(SS, 3, HD), ALU.mult).then_inc(dve_own, 1)
                    vec.wait_ge(dve_own, 1).then_inc(dve_own, -1)
                    vec.tensor_tensor(qk, qk, bc(GA, 1, TILES), ALU.mult).then_inc(dve_own, 1)
                    vec.wait_ge(dve_own, 1).then_inc(dve_own, -1)
                    x1, x2 = qk[:, :, :, 0:HD // 2], qk[:, :, :, HD // 2:HD]
                    vec.tensor_tensor(T1, x1, sin, ALU.mult)
                    vec.tensor_tensor(T2, x2, sin, ALU.mult)
                    vec.tensor_tensor(T3, x1, cos, ALU.mult)
                    vec.tensor_tensor(SQ[:, :, :, 0:HD // 2], x2, cos, ALU.mult).then_inc(dve_own, 1)
                    vec.wait_ge(dve_own, 1).then_inc(dve_own, -1)
                    vec.tensor_tensor(x1, T3, T2, ALU.subtract)
                    vec.tensor_tensor(x2, SQ[:, :, :, 0:HD // 2], T1, ALU.add).then_inc(dve2sp, 1)
            AR.at = mark

        def transpose_heads(PA, PC, QT):
            with nc.Block() as block:
                @block.tensor
                def _(pe):
                    for i in range(8):
                        src, lo = (PA, PC)[i // 4], (i % 4) * P
                        for t in range(NT):
                            last = pe_.transpose(ps[i][:, t * P:(t + 1) * P], src[:, t, lo:lo + P], ident)
                        last.then_inc(pe2act if i % 4 < 2 else pe2dve, 1)

                @block.scalar
                def _(act):
                    for i in (0, 1, 4, 5):
                        act.wait_ge(pe2act, 1).then_inc(pe2act, -1)
                        act_.mul(QT[:, i, :], ps[i][:, :], HD ** -0.5)

                @block.vector
                def _(dve):
                    for i in (2, 3, 6, 7):
                        dve.wait_ge(pe2dve, 1).then_inc(pe2dve, -1)
                        vec.tensor_copy(QT[:, i, :], ps[i][:, :])

        def head_rows(QT, which, h):
            r = (h % 2) * HD
            return QT[r:r + HD, which + h // 2, :]

        def attend_a(QT, PA):
            mark = AR.at
            SM = [AR.room(SEQ) for _ in range(2)]
            PR = [AR.room(SEQ) for _ in range(2)]
            PT = [AR.room(NT, P) for _ in range(2)]
            NM = AR.room(NT * NH)
            DEN = AR.room(NT * NH)
            items = [(i, h) for i in range(NT) for h in range(NH)]
            with nc.Block() as block:
                def scores(n):
                    i, h = items[n]
                    w = (i + 1) * P
                    pe_.matmul(ps[n % 2][:, 0:w], head_rows(QT, 0, h)[:, i * P:(i + 1) * P],
                               head_rows(QT, 2, h)[:, 0:w], start=True, stop=True).then_inc(pe2dve, 1)

                @block.tensor
                def _(pe):
                    scores(0)
                    for n, (i, h) in enumerate(items):
                        if n + 1 < len(items):
                            scores(n + 1)
                        pe.wait_ge(act2pe, 1).then_inc(act2pe, -1)
                        for j in range(i + 1):
                            last = pe_.transpose(ps[2 + n % 2][:, j * P:(j + 1) * P], PR[n % 2][:, j * P:(j + 1) * P], ident)
                        last.then_inc(pe2act, 1)
                        pe.wait_ge(act2pe, 1).then_inc(act2pe, -1)
                        for j in range(i + 1):
                            last = pe_.matmul(ps[4 + n % 2][:, 0:HD], PT[n % 2][:, j, :],
                                              PA[:, j, 2 * AW + h * HD:2 * AW + (h + 1) * HD], start=(j == 0), stop=(j == i))
                        last.then_inc(pe2dve, 1)

                @block.vector
                def _(dve):
                    def finish(n):
                        i, h = items[n]
                        dve.wait_ge(pe2dve, 1).then_inc(pe2dve, -1)
                        vec.reciprocal(DEN[:, n:n + 1], DEN[:, n:n + 1]).then_inc(dve_own, 1)
                        vec.wait_ge(dve_own, 1).then_inc(dve_own, -1)
                        vec.tensor_scalar(O[:, i, h * HD:(h + 1) * HD], ps[4 + n % 2][:, 0:HD], DEN[:, n:n + 1], None, ALU.mult)

                    def mask(n):
                        i, h = items[n]
                        w = (i + 1) * P
                        dve.wait_ge(pe2dve, 1).then_inc(pe2dve, -1)
                        vec.tensor_tensor(SM[n % 2][:, 0:w], ps[n % 2][:, 0:w], cst("log_count")[:, SEQ - w:SEQ], ALU.add).then_inc(dve_own, 1)
                        vec.wait_ge(dve_own, 1).then_inc(dve_own, -1)
                        vec.tensor_reduce(NM[:, n:n + 1], SM[n % 2][:, 0:w], AX, ALU.max, negate=True).then_inc(dve2act, 1)

                    mask(0)
                    for n in range(len(items)):
                        if n + 1 < len(items):
                            mask(n + 1)
                        finish(n)

                @block.scalar
                def _(act):
                    for n, (i, h) in enumerate(items):
                        w = (i + 1) * P
                        act.wait_ge(dve2act, 1).then_inc(dve2act, -1)
                        act_.activation(PR[n % 2][:, 0:w], SM[n % 2][:, 0:w], ACT.Exp, bias=NM[:, n:n + 1],
                                        accum_out=DEN[:, n:n + 1]).then_inc(act2pe, 1)
                        act.wait_ge(pe2act, 1).then_inc(pe2act, -1)
                        act_.copy(PT[n % 2][:, 0:i + 1, :], ps[2 + n % 2][:, 0:w].rearrange("p (j k) -> p j k", k=P)).then_inc(act2pe, 1)
            AR.at = mark

        def attend_c(QT, PC):
            mark = AR.at
            SP = [[AR.room(SEQ) for _ in range(NT)] for _ in range(2)]
            W = [[AR.room(SEQ) for _ in range(NT)] for _ in range(2)]
            E1 = [AR.room(SEQ) for _ in range(2)]
            items = [(h, ks) for h in range(NH) for ks in reversed(range(NT))]
            with nc.Block() as block:
                def scores(n, bank, start, stop):
                    h, ks = items[n]
                    return pe_.matmul(bank[:, 0:SEQ - ks * P], head_rows(QT, 6, h)[:, ks * P:(ks + 1) * P],
                                      head_rows(QT, 4, h)[:, ks * P:SEQ], start=start, stop=stop)

                @block.sync
                def _(sp):
                    sp.wait_ge(stored, 16 * 8).then_inc(stored, -(16 * 8))

                @block.tensor
                def _(pe):
                    scores(0, ps[0], True, True).then_inc(pe2act, 1)
                    for n, (h, ks) in enumerate(items):
                        if n + 1 < len(items):
                            scores(n + 1, ps[(n + 1) % 2], True, True).then_inc(pe2act, 1)
                        pe.wait_ge(dve2pe, 1).then_inc(dve2pe, -1)
                        arg = ps[2 + n % 2]
                        w = SEQ - ks * P
                        scores(n, arg, True, False)
                        pe_.matmul(arg[:, 0:P], ident, cst("neg_mask"), start=False, stop=False)
                        last = pe_.matmul(arg[:, 0:w], cst("neg_lower"), SP[h % 2][ks][:, 0:w], start=False, stop=(ks == NT - 1))
                        for k2 in range(ks + 1, NT):
                            off = (k2 - ks) * P
                            last = pe_.matmul(arg[:, off:w], cst("neg_ones"), SP[h % 2][k2][:, 0:SEQ - k2 * P],
                                              start=False, stop=(k2 == NT - 1))
                        last.then_inc(pe2act, 1)
                        pe.wait_ge(act2pe, 1).then_inc(act2pe, -1)
                        if ks == 0:
                            out = ps[4 + h % 2]
                            for t in range(NT):
                                for k2 in range(t + 1):
                                    last = pe_.matmul(out[:, t * HD:(t + 1) * HD], W[h % 2][k2][:, (t - k2) * P:(t - k2 + 1) * P],
                                                      PC[:, k2, 2 * AW + h * HD:2 * AW + (h + 1) * HD], start=(k2 == 0), stop=(k2 == t))
                            last.then_inc(pe2dve, 1)

                @block.scalar
                def _(act):
                    act_.preload_act_table_set("natural_log_exp_and_others")

                    def log_part(n):
                        h, ks = items[n]
                        w = SEQ - ks * P
                        act.wait_ge(pe2act, 1).then_inc(pe2act, -1)
                        act_.activation(E1[n % 2][:, 0:w], ps[n % 2][:, 0:w], ACT.Abs).then_inc(act_own, 1)
                        act_.wait_ge(act_own, 1).then_inc(act_own, -1)
                        act_.activation(E1[n % 2][:, 0:w], E1[n % 2][:, 0:w], ACT.Exp, scale=-1.0).then_inc(act_own, 1)
                        act_.wait_ge(act_own, 1).then_inc(act_own, -1)
                        act_.activation(E1[n % 2][:, 0:w], E1[n % 2][:, 0:w], ACT.Ln, bias=1.0).then_inc(act2dve, 1)

                    log_part(0)
                    for n, (h, ks) in enumerate(items):
                        if n + 1 < len(items):
                            log_part(n + 1)
                        w = SEQ - ks * P
                        act.wait_ge(pe2act, 1).then_inc(pe2act, -1)
                        act_.activation(W[h % 2][ks][:, 0:w], ps[2 + n % 2][:, 0:w], ACT.Exp).then_inc(act2pe, 1)

                @block.vector
                def _(dve):
                    def softplus(n):
                        h, ks = items[n]
                        w = SEQ - ks * P
                        dve.wait_ge(act2dve, 1).then_inc(act2dve, -1)
                        sp_ = SP[h % 2][ks]
                        vec.scalar_tensor_tensor(sp_[:, 0:w], ps[n % 2][:, 0:w], 0.0, E1[n % 2][:, 0:w], ALU.max, ALU.add).then_inc(dve_own, 1)
                        vec.wait_ge(dve_own, 1).then_inc(dve_own, -1)
                        vec.tensor_tensor(sp_[:, 0:P], sp_[:, 0:P], cst("strict_upper"), ALU.mult).then_inc(dve2pe, 1)

                    for n, (h, ks) in enumerate(items):
                        softplus(n)
                        if ks == 0:
                            dve.wait_ge(pe2dve, 1).then_inc(pe2dve, -1)
                            out = ps[4 + h % 2][:, 0:NT * HD].rearrange("p (t e) -> p t e", e=HD)
                            vec.tensor_copy(O[:, 0:NT, 3 * AW + h * HD:3 * AW + (h + 1) * HD], out)
            AR.at = mark

        def gates(l, BA, G):
            mark = AR.at
            AL = AR.room(NH)
            DT = AR.room(NH)
            A = AR.room(TILES, NH)
            E = AR.room(TILES, NH)
            with nc.Block() as block:
                @block.sync
                def _(sp):
                    sp.dma_start(AL, ins["a_log"][l].partition_broadcast(P)).then_inc(loaded, 16)
                    sp.dma_start(DT, ins["dt_bias"][l].partition_broadcast(P)).then_inc(loaded, 16)

                @block.scalar
                def _(act):
                    act_.activation(G[:, 0], BA[:, :, 0:NH], ACT.Sigmoid)
                    act.wait_ge(dve2act, 1).then_inc(dve2act, -1)
                    act_.activation(AL, AL, ACT.Exp).then_inc(act_own, 1)
                    act_.wait_ge(act_own, 1).then_inc(act_own, -1)
                    act_.activation(E, A, ACT.Abs).then_inc(act_own, 1)
                    act_.wait_ge(act_own, 1).then_inc(act_own, -1)
                    act_.activation(E, E, ACT.Exp, scale=-1.0).then_inc(act_own, 1)
                    act_.wait_ge(act_own, 1).then_inc(act_own, -1)
                    act_.activation(E, E, ACT.Ln, bias=1.0).then_inc(act2dve, 1)

                @block.vector
                def _(dve):
                    dve.wait_ge(loaded, 32).then_inc(loaded, -32)
                    vec.tensor_tensor(A, BA[:, :, NH:2 * NH], bc(DT, 1, TILES), ALU.add).then_inc(dve2act, 1)
                    dve.wait_ge(act2dve, 1).then_inc(act2dve, -1)
                    vec.scalar_tensor_tensor(E, A, 0.0, E, ALU.max, ALU.add).then_inc(dve_own, 1)
                    vec.wait_ge(dve_own, 1).then_inc(dve_own, -1)
                    vec.scalar_tensor_tensor(G[:, 1], E, -1.0, bc(AL, 1, TILES), ALU.mult, ALU.mult)
            AR.at = mark

        def delta_prompt(l, BT, G, PZ):
            mark = AR.at
            F = NH * P
            names = ("KN", "VB", "KBE", "KS", "L", "R", "T", "AT", "QE")
            KN, VB, KBE, KS, L, R, T, AT, QE = (AR.room(NT, F) for _ in names)
            YB = [AR.room(F) for _ in range(2)]
            LM = [AR.room(F) for _ in range(2)]
            TG, DF, DU = YB[0], LM[0], LM[1]
            S, VN = YB[1], LM[0]
            GC = AR.room(NT * NH)
            GE = AR.room(NT * NH)
            GK = AR.room(NT * NH)
            GL = AR.room(NT * NH)
            BE = AR.room(NT * NH)
            H4 = lambda a: a.rearrange("p (h e) -> p h e", h=NH)
            hs = lambda h: slice(h * P, (h + 1) * P)
            beta = G[:, 0, 0:NT, :].rearrange("p t h -> p (t h)")
            g16 = G[:, 1, 0:NT, :].rearrange("p t h -> p (t h)")
            chan = lambda c, t: BT[:, c, 3 + t * P:3 + (t + 1) * P]
            with nc.Block() as block:
                @block.tensor
                def _(pe):
                    pe_.matmul(ps[0][:, 0:16], cst("upper"), g16, start=True, stop=True)
                    pe_.matmul(ps[1][:, 0:16], cst("ones"), g16, start=True, stop=True).then_inc(pe2dve, 1)
                    for t in range(NT):
                        for i, b0 in ((0, 4), (1, 8)):
                            for h in range(NH):
                                last = pe_.transpose(ps[2 + i][:, hs(h)], chan(b0 + h, t), ident)
                        last.then_inc(pe2dve, 1)
                        pe.wait_ge(dve2pe, 1).then_inc(dve2pe, -1)
                        pe_.matmul(ps[4][:, :], cst("ones"), TG, start=True, stop=True).then_inc(pe2dve, 1)
                        for h in range(NH):
                            pe_.matmul(ps[5][:, hs(h)], chan(4 + h, t), chan(4 + h, t), start=True, stop=True)
                            last = pe_.matmul(ps[6][:, hs(h)], chan(4 + h, t), chan(h, t), start=True, stop=True)
                        last.then_inc(pe2dve, 1)
                        pe.wait_ge(dve2pe, 1).then_inc(dve2pe, -1)

                @block.vector
                def _(dve):
                    dve.wait_ge(pe2dve, 1).then_inc(pe2dve, -1)
                    vec.tensor_copy(GC, ps[0][:, 0:16])
                    vec.tensor_copy(GL, ps[1][:, 0:16]).then_inc(dve_own, 1)
                    vec.wait_ge(dve_own, 1).then_inc(dve_own, -1)
                    vec.tensor_tensor(GK, GL, GC, ALU.subtract).then_inc(dve2act, 1)
                    dve.wait_ge(act2dve, 1).then_inc(act2dve, -1)
                    vec.tensor_tensor(BE, beta, GE, ALU.mult).then_inc(dve_own, 1)
                    vec.wait_ge(dve_own, 1).then_inc(dve_own, -1)
                    for t in range(NT):
                        for h in range(NH):
                            last = vec.tensor_scalar(TG[:, hs(h)], cst("upper"), g16[:, t * NH + h:t * NH + h + 1], None, ALU.mult)
                        last.then_inc(dve2pe, 1)
                        dve.wait_ge(pe2dve, 1).then_inc(pe2dve, -1)
                        col = lambda a, h: a[:, t * NH + h:t * NH + h + 1]
                        for h in range(NH):
                            vec.tensor_copy(KN[:, t, hs(h)], ps[2][:, hs(h)])
                            vec.tensor_scalar(VB[:, t, hs(h)], ps[3][:, hs(h)], col(beta, h), None, ALU.mult)
                            vec.tensor_scalar(KBE[:, t, hs(h)], ps[2][:, hs(h)], col(BE, h), None, ALU.mult)
                            vec.tensor_scalar(KS[:, t, hs(h)], ps[2][:, hs(h)], col(GK, h), None, ALU.mult)
                        dve.wait_ge(pe2dve, 1).then_inc(pe2dve, -1)
                        for h in range(NH):
                            vec.tensor_scalar(DF[:, hs(h)], ps[4][:, hs(h)], col(GC, h), 0.0, ALU.subtract, ALU.max)
                            last = vec.tensor_scalar(DU[:, hs(h)], ps[4][:, hs(h)], col(GC, h), 0.0, ALU.subtract, ALU.min)
                        last.then_inc(dve2act, 1)
                        dve.wait_ge(act2dve, 1).then_inc(act2dve, -1)
                        dve.wait_ge(pe2dve, 1).then_inc(pe2dve, -1)
                        vec.tensor_tensor(H4(DF), H4(DF), bc(cst("strict_lower"), 1, NH), ALU.mult)
                        vec.tensor_tensor(H4(DU), H4(DU), bc(cst("upper"), 1, NH), ALU.mult).then_inc(dve_own, 1)
                        vec.wait_ge(dve_own, 1).then_inc(dve_own, -1)
                        for h in range(NH):
                            vec.scalar_tensor_tensor(L[:, t, hs(h)], ps[5][:, hs(h)], col(beta, h), DF[:, hs(h)], ALU.mult, ALU.mult)
                        vec.tensor_tensor(AT[:, t, :], ps[6][:, :], DU, ALU.mult)
                        q4 = BT[:, 0:NH, 3 + t * P:3 + (t + 1) * P]
                        vec.tensor_tensor(H4(QE[:, t, :]), H4(QE[:, t, :]), q4, ALU.mult)
                        vec.tensor_copy(H4(R[:, t, :]), bc(ident, 1, NH))
                        vec.tensor_copy(H4(T[:, t, :]), bc(ident, 1, NH)).then_inc(dve2pe, 1)

                @block.scalar
                def _(act):
                    act_.preload_act_table_set("natural_log_exp_and_others")
                    act.wait_ge(dve2act, 1).then_inc(dve2act, -1)
                    act_.activation(GE, GC, ACT.Exp)
                    act_.activation(GK, GK, ACT.Exp)
                    act_.activation(GL, GL, ACT.Exp).then_inc(act2dve, 1)
                    for t in range(NT):
                        act.wait_ge(dve2act, 1).then_inc(dve2act, -1)
                        act_.activation(DF, DF, ACT.Exp, scale=-1.0)
                        act_.activation(DU, DU, ACT.Exp)
                        act_.activation(QE[:, t, :], ps[4][:, :], ACT.Exp).then_inc(act2dve, 1)

            with nc.Block() as block:
                rounds = [(v, t) for v in range(LEVELS) for t in range(NT)]

                @block.gpsimd
                def _(pool):
                    for n, (v, t) in enumerate(rounds):
                        if n >= 2:
                            pool.wait_ge(dve2pool, 1).then_inc(dve2pool, -1)
                        m = cst("levels")[:, v * P:(v + 1) * P]
                        nc.gpsimd.tensor_tensor(H4(LM[n % 2]), H4(L[:, t, :]), bc(m, 1, NH), ALU.mult).then_inc(pool2pe, 1)
                    pool.wait_ge(dve2pool, 2).then_inc(dve2pool, -2)

                @block.tensor
                def _(pe):
                    def first(n):
                        v, t = rounds[n]
                        pe.wait_ge(pool2pe, 1).then_inc(pool2pe, -1)
                        if n >= 2:
                            pe.wait_ge(dve2pe, 1).then_inc(dve2pe, -1)
                        for h in range(NH):
                            last = pe_.matmul(ps[n % 2][:, hs(h)], LM[n % 2][:, hs(h)], R[:, t, hs(h)], start=True, stop=True)
                        last.then_inc(pe2act, 1)

                    first(0)
                    for n, (v, t) in enumerate(rounds):
                        if n + 1 < len(rounds):
                            first(n + 1)
                        pe.wait_ge(act2pe, 1).then_inc(act2pe, -1)
                        for h in range(NH):
                            pe_.matmul(ps[2 + n % 2][:, hs(h)], T[:, t, hs(h)], YB[n % 2][:, hs(h)], start=True, stop=True)
                            last = pe_.matmul(ps[4 + n % 2][:, hs(h)], YB[n % 2][:, hs(h)], T[:, t, hs(h)], start=True, stop=True)
                        last.then_inc(pe2dve, 1)
                    pe.wait_ge(dve2pe, 2).then_inc(dve2pe, -2)

                @block.scalar
                def _(act):
                    for n in range(len(rounds)):
                        act.wait_ge(pe2act, 1).then_inc(pe2act, -1)
                        act_.copy(YB[n % 2], ps[n % 2][:, :]).then_inc(act2pe, 1)

                @block.vector
                def _(dve):
                    for n, (v, t) in enumerate(rounds):
                        dve.wait_ge(pe2dve, 1).then_inc(pe2dve, -1)
                        dve.sem_inc(dve2pool, 1)
                        vec.tensor_tensor(R[:, t, :], R[:, t, :], ps[2 + n % 2][:, :], ALU.subtract)
                        vec.tensor_tensor(T[:, t, :], T[:, t, :], ps[4 + n % 2][:, :], ALU.subtract).then_inc(dve2pe, 1)

            U, WT = L, T
            with nc.Block() as block:
                @block.tensor
                def _(pe):
                    for t in range(NT):
                        for h in range(NH):
                            pe_.matmul(ps[2 * (t % 2)][:, hs(h)], R[:, t, hs(h)], VB[:, t, hs(h)], start=True, stop=True)
                            last = pe_.matmul(ps[2 * (t % 2) + 1][:, hs(h)], KBE[:, t, hs(h)], R[:, t, hs(h)], start=True, stop=True)
                        last.then_inc(pe2act, 1)
                        if t >= 1:
                            pe.wait_ge(act2pe, 1).then_inc(act2pe, -1)
                    pe.wait_ge(act2pe, 1).then_inc(act2pe, -1)
                    for t in range(NT):
                        pe.wait_ge(dve2pe, 1).then_inc(dve2pe, -1)
                        for h in range(NH):
                            last = pe_.matmul(ps[4][:, hs(h)], WT[:, t, hs(h)], S[:, hs(h)], start=True, stop=True)
                        last.then_inc(pe2dve, 1)
                        pe.wait_ge(dve2pe, 1).then_inc(dve2pe, -1)
                        for h in range(NH):
                            last = pe_.matmul(ps[5][:, hs(h)], KS[:, t, hs(h)], VN[:, hs(h)], start=True, stop=True)
                        last.then_inc(pe2dve, 1)
                        for h in range(NH):
                            pe_.matmul(ps[6][:, hs(h)], QE[:, t, hs(h)], S[:, hs(h)], start=True, stop=False)
                            last = pe_.matmul(ps[6][:, hs(h)], AT[:, t, hs(h)], VN[:, hs(h)], start=False, stop=True)
                        last.then_inc(pe2act, 1)

                @block.scalar
                def _(act):
                    for t in range(NT):
                        act.wait_ge(pe2act, 1).then_inc(pe2act, -1)
                        act_.copy(U[:, t, :], ps[2 * (t % 2)][:, :])
                        act_.copy(WT[:, t, :], ps[2 * (t % 2) + 1][:, :]).then_inc(act2pe, 1)
                    for t in range(NT):
                        act.wait_ge(pe2act, 1).then_inc(pe2act, -1)
                        act_.copy(O[:, t, AW:AW + F], ps[6][:, :]).then_inc(act2dve, 1)

                @block.vector
                def _(dve):
                    vec.memset(S, 0.0).then_inc(dve2pe, 1)
                    for t in range(NT):
                        dve.wait_ge(pe2dve, 1).then_inc(pe2dve, -1)
                        vec.tensor_tensor(VN, U[:, t, :], ps[4][:, :], ALU.subtract).then_inc(dve2pe, 1)
                        dve.wait_ge(pe2dve, 1).then_inc(pe2dve, -1)
                        dve.wait_ge(act2dve, 1).then_inc(act2dve, -1)
                        for h in range(NH):
                            last = vec.scalar_tensor_tensor(S[:, hs(h)], S[:, hs(h)], GL[:, t * NH + h:t * NH + h + 1],
                                                            ps[5][:, hs(h)], ALU.mult, ALU.add)
                        last.then_inc(dve2pe if t < NT - 1 else dve2sp, 1)

                @block.sync
                def _(sp):
                    sp.wait_ge(dve2sp, 1).then_inc(dve2sp, -1)
                    sp.dma_start(outs["delta_prompt"][l, 0].rearrange("h k v -> k h v"), H4(S)).then_inc(stored, 16)
                    sp.wait_ge(stored, 16).then_inc(stored, -16)
            AR.at = mark

        def gated_norm(l, PZ, W_OUT):
            mark = AR.at
            GN = AR.room(P)
            SQ = AR.room(TILES, NH * P)
            SS = AR.room(TILES * NH)
            o = O[:, :, AW:3 * AW]
            by_head = lambda a, t: a[:, t, :].rearrange("p (h e) -> p h e", h=NH)
            with nc.Block() as block:
                @block.sync
                def _(sp):
                    sp.dma_start(GN, ins["gnorm_b"][l].partition_broadcast(P)).then_inc(loaded, 16)
                    sp.dma_start(W_OUT, ins["w_out"][l].rearrange("(k p) n -> p k n", p=P)).then_inc(w_landed[0], 16)

                @block.scalar
                def _(act):
                    act_.activation(PZ, PZ, ACT.Silu).then_inc(act2dve, 1)
                    act.wait_ge(dve2act, 1).then_inc(dve2act, -1)
                    rsqrt(SS, SS, 1.0 / DK).then_inc(act2dve, 1)

                @block.vector
                def _(dve):
                    vec.tensor_tensor(SQ, o, o, ALU.mult).then_inc(dve_own, 1)
                    vec.wait_ge(dve_own, 1).then_inc(dve_own, -1)
                    vec.tensor_reduce(SS, SQ.rearrange("p t (h e) -> p (t h) e", h=NH), AX, ALU.add).then_inc(dve2act, 1)
                    dve.wait_ge(loaded, 16).then_inc(loaded, -16)
                    dve.wait_ge(act2dve, 2).then_inc(act2dve, -2)
                    for t in range(TILES):
                        vec.tensor_tensor(by_head(SQ, t), by_head(PZ, t), bc(GN, 1, NH), ALU.mult)
                    vec.engine_nop().then_inc(dve_own, 1)
                    vec.wait_ge(dve_own, 1).then_inc(dve_own, -1)
                    for t in range(TILES):
                        vec.tensor_tensor(by_head(SQ, t), by_head(SQ, t), bc(SS[:, t * NH:(t + 1) * NH], 2, P), ALU.mult)
                    vec.engine_nop().then_inc(dve_own, 1)
                    vec.wait_ge(dve_own, 1).then_inc(dve_own, -1)
                    vec.tensor_tensor(o, o, SQ, ALU.mult)
            AR.at = mark

        def delta_sample(l, DB, G):
            mark = AR.at
            NP_ = NB * NH
            SC = AR.room(KW - 1, CONV_CH, rows=NB)
            CB = AR.room(KW, CONV_CH, rows=NB)
            ACC = AR.room(CONV_CH, rows=NB)
            TM = AR.room(CONV_CH, rows=NB)
            SS = AR.room(8, rows=NB)
            BE = AR.room(8, rows=NB)
            QKV = AR.room(CC, NB)
            KQ = AR.room(NP_, 2)
            VT = AR.room(NP_)
            QK = AR.room(NP_)
            BG = AR.room(NB, 8)
            SD = AR.room(NP_, P)
            VV = AR.room(NP_)
            OT = AR.room(NP_)
            T1 = AR.room(NP_)
            DG = [AR.room(4, P) for _ in range(2)]
            pair = lambda a: a.rearrange("p (b h) -> p b h", h=NH)
            beta, eg = BG[:, :, 0:NH], BG[:, :, NH:8]
            with nc.Block() as block:
                @block.sync
                def _(sp):
                    sp.dma_start(SC, ins["state_conv"][l]).then_inc(loaded, 16)
                    sp.dma_start(CB.rearrange("p j c -> p (j c)"), ins["conv_w"][l].rearrange("j c -> (j c)").partition_broadcast(NB)).then_inc(loaded, 16)
                    for b in range(0, NB, 2):
                        sp.dma_start(SD[:, b * NH:(b + 2) * NH, :], ins["state_delta"][l, b:b + 2].rearrange("b h k v -> k (b h) v")).then_inc(loaded2, 16)
                    sp.dma_start(outs["conv_sample"][l, :, 0:2], ins["state_conv"][l, :, 1:3]).then_inc(stored, 16)
                    sp.dma_start(outs["conv_sample"][l, :, 2], DB[0:NB, :]).then_inc(stored, 16)
                    for b in range(NB):
                        sp.wait_ge(dve2sp, 1).then_inc(dve2sp, -1)
                        sp.dma_start(outs["delta_sample"][l, b].rearrange("h k v -> k h v"), SD[:, b * NH:(b + 1) * NH, :]).then_inc(stored, 16)
                    sp.wait_ge(stored, 16 * (2 + NB)).then_inc(stored, -(16 * (2 + NB)))

                @block.scalar
                def _(act):
                    act.wait_ge(dve2act, 1).then_inc(dve2act, -1)
                    act_.activation(ACC, ACC, ACT.Silu).then_inc(act2dve, 1)
                    act.wait_ge(dve2act, 1).then_inc(dve2act, -1)
                    rsqrt(SS, SS, 1.0).then_inc(act2dve, 1)
                    act_.activation(BE[:, NH:8], G[0:NB, 1, NT, :], ACT.Exp)
                    act_.copy(BE[:, 0:NH], G[0:NB, 0, NT, :]).then_inc(act2pe, 1)

                @block.tensor
                def _(pe):
                    pe.wait_ge(act2pe, 1).then_inc(act2pe, -1)
                    for b in range(NB):
                        last = pe_.matmul(ps[0][:, b * 8:b * 8 + 8], cst("pick_row", NB)[:, b * P:(b + 1) * P], BE, start=True, stop=True)
                    pe.wait_ge(dve2pe, 1).then_inc(dve2pe, -1)
                    for c in range(CC):
                        last = pe_.transpose(ps[1][:, c * 8:c * 8 + 8], ACC[:, c * P:(c + 1) * P], ident[0:NB, 0:NB])
                    last.then_inc(pe2dve, 1)
                    pe.wait_ge(dve2pe, 1).then_inc(dve2pe, -1)
                    pe_.matmul(ps[2][:, 0:NP_], cst("ones"), QK, start=True, stop=True)
                    for n in range(NP_):
                        last = pe_.matmul(ps[3][:, 2 * n:2 * n + 2], SD[:, n, :], KQ[:, n, :], start=True, stop=True)
                    last.then_inc(pe2dve, 1)
                    pe.wait_ge(dve2pe, 1).then_inc(dve2pe, -1)
                    for h in range(NH):
                        last = pe_.transpose(ps[0][0:NB, h * P:(h + 1) * P], pair(OT)[:, :, h], ident)
                    last.then_inc(pe2dve, 1)
                    for m in range(8):
                        pe.wait_ge(dve2pe, 1).then_inc(dve2pe, -1)
                        pe_.matmul(ps[4 + m % 4][:, :], cst("ones"), DG[m % 2].rearrange("p a b -> p (a b)"), start=True, stop=True).then_inc(pe2dve, 1)

                @block.vector
                def _(dve):
                    dve.wait_ge(loaded, 32).then_inc(loaded, -32)
                    vec.tensor_tensor(ACC, DB[0:NB, :], CB[:, KW - 1, :], ALU.mult).then_inc(dve_own, 1)
                    vec.wait_ge(dve_own, 1).then_inc(dve_own, -1)
                    for j in range(KW - 1):
                        vec.tensor_tensor(TM, SC[:, j, :], CB[:, j, :], ALU.mult).then_inc(dve_own, 1)
                        vec.wait_ge(dve_own, 1).then_inc(dve_own, -1)
                        i_ = vec.tensor_tensor(ACC, ACC, TM, ALU.add)
                        if j < KW - 2:
                            i_.then_inc(dve_own, 1)
                            vec.wait_ge(dve_own, 1).then_inc(dve_own, -1)
                    i_.then_inc(dve2act, 1)
                    dve.wait_ge(act2dve, 1).then_inc(act2dve, -1)
                    qk8 = ACC[:, 0:8 * P]
                    vec.tensor_tensor(TM[:, 0:8 * P], qk8, qk8, ALU.mult).then_inc(dve_own, 1)
                    vec.wait_ge(dve_own, 1).then_inc(dve_own, -1)
                    vec.tensor_reduce(SS, TM[:, 0:8 * P].rearrange("p (h e) -> p h e", h=8), AX, ALU.add).then_inc(dve2act, 1)
                    dve.wait_ge(act2dve, 1).then_inc(act2dve, -1)
                    vec.tensor_scalar(SS[:, 0:NH], SS[:, 0:NH], DK ** -0.5, None, ALU.mult).then_inc(dve_own, 1)
                    vec.wait_ge(dve_own, 1).then_inc(dve_own, -1)
                    qk8 = qk8.rearrange("p (h e) -> p h e", h=8)
                    vec.tensor_tensor(qk8, qk8, bc(SS, 2, P), ALU.mult).then_inc(dve2pe, 1)
                    dve.wait_ge(pe2dve, 1).then_inc(pe2dve, -1)
                    vec.tensor_copy(BG, ps[0][:, 0:64].rearrange("p (b e) -> p b e", b=NB))
                    vec.tensor_copy(QKV, ps[1][:, 0:CC * NB].rearrange("p (c b) -> p c b", c=CC)).then_inc(dve_own, 1)
                    vec.wait_ge(dve_own, 1).then_inc(dve_own, -1)
                    qv, kv, vv = (QKV[:, i * NH:(i + 1) * NH, :].rearrange("p h b -> p b h") for i in range(3))
                    kq = KQ.rearrange("p (b h) c -> p b h c", h=NH)
                    vec.tensor_copy(kq[:, :, :, 0], kv)
                    vec.tensor_copy(kq[:, :, :, 1], qv)
                    vec.tensor_copy(pair(VT), vv)
                    dve.wait_ge(loaded2, 64).then_inc(loaded2, -64)
                    vec.tensor_tensor(pair(QK), qv, kv, ALU.mult).then_inc(dve2pe, 1)
                    dve.wait_ge(pe2dve, 1).then_inc(pe2dve, -1)
                    r = ps[3][:, 0:2 * NP_].rearrange("p (b h c) -> p b h c", b=NB, h=NH)
                    vec.tensor_tensor(pair(T1), r[:, :, :, 0], eg, ALU.mult).then_inc(dve_own, 1)
                    vec.wait_ge(dve_own, 1).then_inc(dve_own, -1)
                    vec.tensor_tensor(T1, VT, T1, ALU.subtract).then_inc(dve_own, 1)
                    vec.wait_ge(dve_own, 1).then_inc(dve_own, -1)
                    vec.tensor_tensor(pair(VV), pair(T1), beta, ALU.mult).then_inc(dve_own, 1)
                    vec.wait_ge(dve_own, 1).then_inc(dve_own, -1)
                    vec.tensor_tensor(pair(OT), r[:, :, :, 1], eg, ALU.mult)
                    vec.tensor_tensor(T1, VV, ps[2][:, 0:NP_], ALU.mult).then_inc(dve_own, 1)
                    vec.wait_ge(dve_own, 1).then_inc(dve_own, -1)
                    vec.tensor_tensor(OT, OT, T1, ALU.add).then_inc(dve2pe, 1)
                    sd4 = SD.rearrange("p (b h) v -> p b h v", h=NH)
                    for b in range(NB):
                        vec.tensor_tensor(sd4[:, b], sd4[:, b], bc(eg[:, b, :], 2, P), ALU.mult)
                    dve.wait_ge(pe2dve, 1).then_inc(pe2dve, -1)
                    vec.tensor_copy(O[0:NB, NT, AW:3 * AW], ps[0][0:NB, :])
                    for m in range(8 + 1):
                        if m < 8:
                            vec.tensor_tensor(DG[m % 2], bc(ident, 1, 4), bc(VV[:, 4 * m:4 * m + 4], 2, P), ALU.mult).then_inc(dve2pe, 1)
                        if m >= 1:
                            dve.wait_ge(pe2dve, 1).then_inc(pe2dve, -1)
                            for i in range(4):
                                n = 4 * (m - 1) + i
                                last = vec.scalar_tensor_tensor(SD[:, n, :], ps[4 + (m - 1) % 4][:, i * P:(i + 1) * P],
                                                                KQ[:, n, 0:1], SD[:, n, :], ALU.mult, ALU.add)
                            last.then_inc(dve2sp, 1)
            AR.at = mark

        def windows_sample(l, SRC, PC):
            mark = AR.at
            ns = 4
            vw = AW + 1
            HB = NB // 2
            KB = AR.room(NB, ns * vw)
            VB = AR.room(HB, ns * vw)
            QB = PC[:, 0:NT, :].rearrange("p t e -> p (t e)")[:, 0:NB * AW].rearrange("p (b e) -> p b e", b=NB)
            slots = lambda a, b: a[:, b, :].rearrange("p (s e) -> p s e", s=ns)
            keys = lambda b: slots(KB, b)
            values = lambda b: slots(VB, b) if b < HB else slots(KB, b - HB)
            Z = AR.room(NB * ns * NH)
            W = AR.room(NB * ns * NH)
            MX = AR.room(8)
            MR = AR.room(P, rows=1)
            MB = AR.room(NB * NH, rows=1)
            OD = [AR.room(AW, rows=NH) for _ in range(2)]
            z4 = lambda a: a.rearrange("p (b s h) -> p b s h", b=NB, s=ns)

            def load(sp, dst, what, b0, done):
                cache = ins["cache_win_" + what][l, b0:b0 + HB]
                dst = dst.rearrange("p b (s e) -> p b s e", s=ns)
                for s_, dil in enumerate((1, 4, 16)):
                    rows = cache[:, PAST - P * dil:PAST].rearrange("b (p d) h e -> p b d (h e)", d=dil)[:, :, 0, :]
                    sp.dma_start(dst[:, :, s_, 0:AW], rows).then_inc(done, 16)
                own = outs[f"win_{what}_sample"][l, b0:b0 + HB, 0].rearrange("b h e -> b (h e)").partition_broadcast(3)
                sp.dma_start(dst[0:3, :, 3, 0:AW], own).then_inc(done, 16)

            per = 16 * ns
            with nc.Block() as block:
                @block.gpsimd
                def _(pool):
                    for kb in (KB, VB):
                        kb = kb.rearrange("p b (s e) -> p b s e", s=ns)
                        nc.gpsimd.memset(kb[:, :, 3, 0:AW], 0.0)
                        last = nc.gpsimd.memset(kb[:, :, :, AW:AW + 1], 1.0)
                    last.then_inc(pool2dve, 1)

                @block.sync
                def _(sp):
                    sp.wait_ge(pool2dve, 1).then_inc(pool2dve, -1)
                    load(sp, KB[:, 0:HB], "k", 0, w_landed[0])
                    load(sp, KB[:, HB:NB], "k", HB, w_landed[1])
                    load(sp, VB, "v", 0, v_landed[0])
                    sp.wait_ge(ring_free, 1).then_inc(ring_free, -1)
                    load(sp, KB[:, 0:HB], "v", HB, v_landed[1])

                @block.tensor
                def _(pe):
                    for b in range(NB):
                        pe_.matmul(ps[b][:, 0:AW], cst("pick_row", NB)[:, b * P:(b + 1) * P], SRC[0:NB, NT, 0:AW],
                                   start=True, stop=True).then_inc(pe2act, 1)
                    pe.wait_ge(dve2pe, 1).then_inc(dve2pe, -1)
                    pe_.transpose(ps[4][:, 0:P], Z, ident).then_inc(pe2dve, 1)
                    pe.wait_ge(dve2pe, 1).then_inc(dve2pe, -1)
                    pe_.matmul(ps[5][0:1, 0:P], MX[:, 0:1], ident, start=True, stop=True).then_inc(pe2dve, 1)
                    pe.wait_ge(dve2pe, 1).then_inc(dve2pe, -1)
                    pe_.matmul(ps[6][:, 0:NB * NH], cst("ones", 1), MB, start=True, stop=True).then_inc(pe2dve, 1)
                    pe.wait_ge(act2pe, 1).then_inc(act2pe, -1)
                    for b in range(NB + 1):
                        if b < NB:
                            if b % HB == 0:
                                pe.wait_ge(v_landed[b // HB], per).then_inc(v_landed[b // HB], -per)
                            for s_ in range(ns):
                                last = pe_.matmul(ps[b % 2][0:NH, 0:vw], z4(W)[:, b, s_, :], values(b)[:, s_, :],
                                                  start=(s_ == 0), stop=(s_ == ns - 1))
                            last.then_inc(pe2dve, 1)
                        if b >= 1:
                            pe.wait_ge(dve2pe, 1).then_inc(dve2pe, -1)
                            last = pe_.matmul(ps[7][0:NB, 0:AW], cst("place", NH)[:, (b - 1) * NB:b * NB], OD[(b - 1) % 2],
                                              start=(b == 1), stop=(b == NB))
                    last.then_inc(pe2act, 1)

                @block.scalar
                def _(act):
                    for b in range(NB):
                        act.wait_ge(pe2act, 1).then_inc(pe2act, -1)
                        act_.mul(QB[:, b, :], ps[b][:, 0:AW], HD ** -0.5).then_inc(act2dve, 1)
                    act.wait_ge(dve2act, 1).then_inc(dve2act, -1)
                    act_.activation(W, W, ACT.Exp).then_inc(act2pe, 1)
                    act.wait_ge(pe2act, 1).then_inc(pe2act, -1)
                    act_.copy(O[0:NB, NT, 0:AW], ps[7][0:NB, 0:AW])

                @block.vector
                def _(dve):
                    for b in range(NB):
                        dve.wait_ge(act2dve, 1).then_inc(act2dve, -1)
                        if b % HB == 0:
                            dve.wait_ge(w_landed[b // HB], per).then_inc(w_landed[b // HB], -per)
                        kb = keys(b)[:, :, 0:AW]
                        vec.tensor_tensor(kb, kb, bc(QB[:, b, :], 1, ns), ALU.mult).then_inc(dve_own, 1)
                        vec.wait_ge(dve_own, 1).then_inc(dve_own, -1)
                        zb = Z[:, b * ns * NH:(b + 1) * ns * NH]
                        vec.tensor_reduce(zb, kb.rearrange("p s (h e) -> p s h e", h=NH), AX, ALU.add).then_inc(dve_own, 1)
                        vec.wait_ge(dve_own, 1).then_inc(dve_own, -1)
                        if b == HB - 1:
                            dve.sem_inc(ring_free, 1)
                    z3 = Z.rearrange("p (b m) -> p b m", b=NB)
                    vec.tensor_tensor(z3, z3, bc(cst("own_mask"), 1, NB), ALU.add).then_inc(dve2pe, 1)
                    dve.wait_ge(pe2dve, 1).then_inc(pe2dve, -1)
                    vec.tensor_reduce(MX[:, 0:1], ps[4][:, 0:P], AX, ALU.max).then_inc(dve2pe, 1)
                    dve.wait_ge(pe2dve, 1).then_inc(pe2dve, -1)
                    vec.tensor_reduce(MB.rearrange("p (b h) -> p b h", b=NB), ps[5][0:1, 0:P].rearrange("p (b s h) -> p b h s", b=NB, s=ns),
                                      AX, ALU.max).then_inc(dve2pe, 1)
                    dve.wait_ge(pe2dve, 1).then_inc(pe2dve, -1)
                    mb = ps[6][:, 0:NB * NH].rearrange("p (b h) -> p b h", b=NB)
                    vec.tensor_tensor(z4(W), z4(Z), bc(mb, 2, ns), ALU.subtract).then_inc(dve2act, 1)
                    for b in range(NB):
                        dve.wait_ge(pe2dve, 1).then_inc(pe2dve, -1)
                        vec.reciprocal(MX[0:NH, b:b + 1], ps[b % 2][0:NH, AW:AW + 1]).then_inc(dve_own, 1)
                        vec.wait_ge(dve_own, 1).then_inc(dve_own, -1)
                        vec.scalar_tensor_tensor(OD[b % 2], ps[b % 2][0:NH, 0:AW], MX[0:NH, b:b + 1], cst("head_diag", NH),
                                                 ALU.mult, ALU.mult).then_inc(dve2pe, 1)
            AR.at = mark

        def sticks_sample(l, PC):
            mark = AR.at
            HP = PAGES // 2
            KB = [AR.room(HP, AW) for _ in range(2)]
            VB = [AR.room(HP, AW) for _ in range(4)]
            QB = AR.room(NB, AW)
            SW = PAGES * NH
            Z, W, SFA, SFB = (AR.room(NB * SW) for _ in range(4))
            OD = [AR.room(AW, rows=NH) for _ in range(2)]
            of = lambda a, b: a[:, b * SW:(b + 1) * SW]
            by_page = lambda a, b: of(a, b).rearrange("p (s h) -> p s h", h=NH)
            with nc.Block() as block:
                def pages(eng, dst, cache, b, half, done):
                    at = b * PAGES + half * HP
                    numbers = [eng.value_load(nc_page_table[0:1, at + j:at + j + 1], min_val=0, max_val=cache.shape[0] - 1)
                               for j in range(HP)]
                    for j, page in enumerate(numbers):
                        eng.dma_start(dst[:, j, :], cache[page].rearrange("s h e -> s (h e)")).then_inc(done, 16)

                @block.sync
                def _(sp):
                    for b in range(NB):
                        for half in range(2):
                            if b >= 1:
                                sp.wait_ge(ring_free, 1).then_inc(ring_free, -1)
                            pages(sp, KB[half], ins["cache_sb_k"][l], b, half, w_landed[half])
                    sp.wait_ge(ring_free, 2).then_inc(ring_free, -2)

                @block.tensor
                def _(pe):
                    for b in range(NB):
                        pe_.matmul(ps[b][:, 0:AW], cst("pick_row", NB)[:, b * P:(b + 1) * P], PC[0:NB, NT, 0:AW],
                                   start=True, stop=True).then_inc(pe2act, 1)
                    for s_ in range(1, NB + 2):
                        if s_ <= NB:
                            b = s_ - 1
                            pe.wait_ge(dve2pe, 1).then_inc(dve2pe, -1)
                            arg = ps[4 + b % 2][:, 0:SW]
                            pe_.matmul(arg, ident, of(Z, b), start=True, stop=False)
                            pe_.matmul(arg, cst("neg_lower"), of(W, b), start=False, stop=False)
                            pe_.matmul(arg[:, 0:SW - NH], cst("neg_ones"), of(SFA, b)[:, NH:SW], start=False, stop=True).then_inc(pe2act, 1)
                            pe.wait_ge(act2pe, 1).then_inc(act2pe, -1)
                            for j in range(PAGES):
                                i = 2 * (b % 2) + j // HP
                                if j % HP == 0:
                                    pe.wait_ge(v_landed[i], 16 * HP).then_inc(v_landed[i], -(16 * HP))
                                last = pe_.matmul(ps[b % 2][0:NH, 0:AW], by_page(SFB, b)[:, j, :], VB[i][:, j % HP, :],
                                                  start=(j == 0), stop=(j == PAGES - 1))
                            last.then_inc(pe2dve, 1)
                        if s_ >= 2:
                            b = s_ - 2
                            pe.wait_ge(dve2pe, 1).then_inc(dve2pe, -1)
                            last = pe_.matmul(ps[7][0:NB, 0:AW], cst("place", NH)[:, b * NB:(b + 1) * NB], OD[b % 2],
                                              start=(b == 0), stop=(b == NB - 1))
                    last.then_inc(pe2act, 1)

                @block.scalar
                def _(act):
                    act_.preload_act_table_set("natural_log_exp_and_others")
                    for b in range(NB):
                        act.wait_ge(pe2act, 1).then_inc(pe2act, -1)
                        act_.mul(QB[:, b, :], ps[b][:, 0:AW], HD ** -0.5).then_inc(act2dve, 1)

                    def log_part(b):
                        act.wait_ge(dve2act, 1).then_inc(dve2act, -1)
                        act_.activation(of(W, b), of(Z, b), ACT.Abs).then_inc(act_own, 1)
                        act_.wait_ge(act_own, 1).then_inc(act_own, -1)
                        act_.activation(of(W, b), of(W, b), ACT.Exp, scale=-1.0).then_inc(act_own, 1)
                        act_.wait_ge(act_own, 1).then_inc(act_own, -1)
                        act_.activation(of(W, b), of(W, b), ACT.Ln, bias=1.0).then_inc(act2dve, 1)

                    def values(b, half):
                        if b >= 2:
                            act.wait_ge(v_used, 1).then_inc(v_used, -1)
                        pages(act, VB[2 * (b % 2) + half], ins["cache_sb_v"][l], b, half, v_landed[2 * (b % 2) + half])

                    values(0, 0)
                    log_part(0)
                    values(0, 1)
                    for b in range(NB):
                        if b + 1 < NB:
                            log_part(b + 1)
                            values(b + 1, 0)
                        act.wait_ge(pe2act, 1).then_inc(pe2act, -1)
                        act_.activation(of(SFB, b), ps[4 + b % 2][:, 0:SW], ACT.Exp).then_inc(act2pe, 1)
                        if b + 1 < NB:
                            values(b + 1, 1)
                    act.wait_ge(v_used, 4).then_inc(v_used, -4)
                    act.wait_ge(pe2act, 1).then_inc(pe2act, -1)
                    act_.copy(O[0:NB, NT, 3 * AW:4 * AW], ps[7][0:NB, 0:AW])

                @block.vector
                def _(dve):
                    dve.wait_ge(act2dve, NB).then_inc(act2dve, -NB)
                    for s_ in range(NB + 2):
                        if s_ < NB:
                            b = s_
                            for half in range(2):
                                dve.wait_ge(w_landed[half], 16 * HP).then_inc(w_landed[half], -(16 * HP))
                                kb = KB[half]
                                vec.tensor_tensor(kb, kb, bc(QB[:, b, :], 1, HP), ALU.mult).then_inc(dve_own, 1)
                                vec.wait_ge(dve_own, 1).then_inc(dve_own, -1)
                                zb = of(Z, b)[:, half * HP * NH:(half + 1) * HP * NH]
                                vec.tensor_reduce(zb, kb.rearrange("p s (h e) -> p s h e", h=NH), AX, ALU.add).then_inc(dve_own, 1)
                                vec.wait_ge(dve_own, 1).then_inc(dve_own, -1)
                                dve.sem_inc(ring_free, 1)
                            dve.sem_inc(dve2act, 1)
                        if 1 <= s_ <= NB:
                            b = s_ - 1
                            dve.wait_ge(act2dve, 1).then_inc(act2dve, -1)
                            vec.scalar_tensor_tensor(of(W, b), of(Z, b), 0.0, of(W, b), ALU.max, ALU.add).then_inc(dve_own, 1)
                            vec.wait_ge(dve_own, 1).then_inc(dve_own, -1)
                            src, step = W, 1
                            while step < PAGES:
                                dst = SFA if src is not SFA and step != 1 else SFB
                                n = (PAGES - step) * NH
                                vec.tensor_tensor(of(dst, b)[:, 0:n], of(src, b)[:, 0:n], of(src, b)[:, SW - n:SW], ALU.add)
                                i_ = vec.tensor_copy(of(dst, b)[:, n:SW], of(src, b)[:, n:SW])
                                src, step = dst, 2 * step
                                if step < PAGES:
                                    i_.then_inc(dve_own, 1)
                                    vec.wait_ge(dve_own, 1).then_inc(dve_own, -1)
                            assert src is SFA
                            i_.then_inc(dve2pe, 1)
                        if s_ >= 2:
                            b = s_ - 2
                            dve.wait_ge(pe2dve, 1).then_inc(pe2dve, -1)
                            dve.sem_inc(v_used, 2)
                            vec.tensor_tensor(OD[b % 2], ps[b % 2][0:NH, 0:AW], cst("head_diag", NH), ALU.mult).then_inc(dve2pe, 1)
            AR.at = mark

        def out_projection(W):
            mark = AR.at
            OT = AR.room(KD, SEQ + NB)
            GP = AR.room(D)
            TM = [AR.room(GBLK) for _ in range(2)]
            assert AR.at <= inner
            with nc.Block() as block:
                @block.tensor
                def _(pe):
                    for i in range(2):
                        last = pe_.matmul(ps[6 + i][:, :], cst("row8", NB + 1), MOD9[0:NB + 1, 2 * D + i * GBLK:2 * D + (i + 1) * GBLK],
                                          start=True, stop=True)
                    last.then_inc(pe2act, 1)
                    for g in range(2 * TILES):
                        t, half = g // 2, g % 2
                        rows = P if t < NT else NB
                        if g >= 2:
                            pe.wait_ge(act_free, 1).then_inc(act_free, -1)
                        for j in range(4):
                            k = half * 4 + j
                            last = pe_.transpose(ps[g % 2][:, j * P:j * P + rows], O[0:rows, t, k * P:(k + 1) * P], ident[0:rows, 0:rows])
                        last.then_inc(pe2act, 1)
                    pe.wait_ge(act_free, 2).then_inc(act_free, -2)
                    pe.wait_ge(w_landed[0], 16).then_inc(w_landed[0], -16)
                    for g in range(2 * TILES):
                        t, half = g // 2, g % 2
                        rows = P if t < NT else NB
                        if g >= 2:
                            pe.wait_ge(dve_free, 1).then_inc(dve_free, -1)
                        for k in range(KD):
                            last = pe_.matmul(ps[2 + g % 2][0:rows, :], OT[:, k, t * P:t * P + rows], W[:, k, half * GBLK:(half + 1) * GBLK],
                                              start=(k == 0), stop=(k == KD - 1))
                        last.then_inc(pe2dve, 1)
                    pe.wait_ge(dve_free, 2).then_inc(dve_free, -2)

                @block.scalar
                def _(act):
                    act.wait_ge(pe2act, 1).then_inc(pe2act, -1)
                    act_.copy(GP[:, 0:GBLK], ps[6][:, :])
                    act_.copy(GP[:, GBLK:D], ps[7][:, :]).then_inc(act2dve, 1)
                    for g in range(2 * TILES):
                        t, half = g // 2, g % 2
                        rows = P if t < NT else NB
                        act.wait_ge(pe2act, 1).then_inc(pe2act, -1)
                        act_.copy(OT[:, half * 4:half * 4 + 4, t * P:t * P + rows],
                                  ps[g % 2][:, :].rearrange("p (j n) -> p j n", j=4)[:, :, 0:rows]).then_inc(act_free, 1)

                @block.vector
                def _(dve):
                    dve.wait_ge(act2dve, 1).then_inc(act2dve, -1)
                    for g in range(2 * TILES):
                        t, half = g // 2, g % 2
                        rows = P if t < NT else NB
                        c = slice(half * GBLK, (half + 1) * GBLK)
                        gate = GP[:, c] if t < NT else MOD9[0:NB, 2 * D + half * GBLK:2 * D + (half + 1) * GBLK]
                        dve.wait_ge(pe2dve, 1).then_inc(pe2dve, -1)
                        vec.tensor_tensor(TM[g % 2][0:rows, :], ps[2 + g % 2][0:rows, :], gate, ALU.mult).then_inc(dve_own, 1)
                        vec.wait_ge(dve_own, 1).then_inc(dve_own, -1)
                        dve.sem_inc(dve_free, 1)
                        vec.tensor_tensor(X[0:rows, t, c], X[0:rows, t, c], TM[g % 2][0:rows, :], ALU.add)
            AR.at = mark

        def peer(l):
            mark = AR.at
            IDX = AR.room(TILES, SLOTS)
            IDI = AR.room(TILES, SLOTS).bitcast(I32)
            GT = AR.room(TILES, SLOTS)
            GP = AR.room(D)
            SS = AR.room(TILES * PH)
            mark2 = AR.at
            HT = AR.room(KD, SEQ + NB)
            W = AR.room(KD, D)
            KR = AR.room(PH, P)
            KBD = AR.room(PH, 2 * PK)
            QT = AR.room(PH, SEQ + NB)
            QT_end = AR.at
            keys = ins["peer_keys"][l]

            def queries_weights(sp):
                for h in range(PH):
                    sp.dma_start(KR[:, h, :].rearrange("p (x k) -> p x k", x=2), keys[h].rearrange("x e k -> e x k")).then_inc(loaded, 16)
                sp.dma_start(W, ins["peer_wq"][l].rearrange("(k p) n -> p k n", p=P)).then_inc(w_landed[0], 16)

            norm(3, HT, queries_weights, AR.at)
            with nc.Block() as block:
                @block.gpsimd
                def _(pool):
                    nc.gpsimd.memset(KBD, 0.0).then_inc(pool2dve, 1)

                @block.tensor
                def _(pe):
                    for i in range(2):
                        last = pe_.matmul(ps[6 + i][:, :], cst("row8", NB + 1), MOD9[0:NB + 1, 5 * D + i * GBLK:5 * D + (i + 1) * GBLK],
                                          start=True, stop=True)
                    last.then_inc(pe2act, 1)
                    pe.wait_ge(loaded, 16 * PH).then_inc(loaded, -(16 * PH))
                    for h in range(PH):
                        last = pe_.transpose(ps[h // 4][:, (h % 4) * P:(h % 4 + 1) * P], KR[:, h, :], ident)
                    last.then_inc(pe2dve, 1)
                    pe.wait_ge(w_landed[0], 16).then_inc(w_landed[0], -16)
                    for h in range(PH):
                        if h >= 2:
                            pe.wait_ge(act_free, 1).then_inc(act_free, -1)
                        for k in range(KD):
                            pe_.matmul(ps[2 + h % 2][:, :], W[:, k, h * P:(h + 1) * P], HT[:, k, 0:SEQ], start=(k == 0), stop=(k == KD - 1))
                        for k in range(KD):
                            last = pe_.matmul(ps[4 + h % 2][:, 0:NB], W[:, k, h * P:(h + 1) * P], HT[:, k, SEQ:SEQ + NB],
                                              start=(k == 0), stop=(k == KD - 1))
                        last.then_inc(pe2act, 1)
                    pe.wait_ge(act_free, 2).then_inc(act_free, -2)

                @block.scalar
                def _(act):
                    act.wait_ge(pe2act, 1).then_inc(pe2act, -1)
                    act_.copy(GP[:, 0:GBLK], ps[6][:, :])
                    act_.copy(GP[:, GBLK:D], ps[7][:, :])
                    for h in range(PH):
                        act.wait_ge(pe2act, 1).then_inc(pe2act, -1)
                        act_.copy(QT[:, h, 0:SEQ], ps[2 + h % 2][:, :])
                        act_.copy(QT[:, h, SEQ:SEQ + NB], ps[4 + h % 2][:, 0:NB]).then_inc(act_free, 1)

                @block.vector
                def _(dve):
                    dve.wait_ge(pool2dve, 1).then_inc(pool2dve, -1)
                    dve.wait_ge(pe2dve, 1).then_inc(pe2dve, -1)
                    for i in range(2):
                        src = ps[i][:, :].rearrange("p (h e) -> p h e", h=4)
                        vec.tensor_copy(KBD[0:HD, 4 * i:4 * i + 4, 0:PK], src[0:HD])
                        vec.tensor_copy(KBD[HD:P, 4 * i:4 * i + 4, PK:2 * PK], src[HD:P])

            AR.at = mark2
            assert QT_end <= arena_cols
            G_ = [MOD9[:, i * D:(i + 1) * D] for i in range(5)] + [AR.room(D) for _ in range(GR - 5)]
            IS = [AR.room(LOT).bitcast(I32) for _ in range(GR // LOT)]
            A8 = AR.room(GR)
            AV = AR.room(SLOTS)
            assert AR.at <= mark2 + KD * (SEQ + NB) + KD * D + PH * P
            AR.at = QT_end
            SC = AR.room(2 * PH, PK)
            SC2 = AR.room(2 * PH, PK)
            CA = SC.rearrange("p g e -> p (g e)").rearrange("p (h e) -> p h e", h=PH)
            SC3 = SC2.rearrange("p g e -> p (g e)").rearrange("p (h e) -> p h e", h=PH)
            EQ = SC2.rearrange("p g e -> p (g e)")
            TV = AR.room(2 * PH, TOPK)
            TI = AR.room(2 * PH, TOPK)
            TF = AR.room(2 * PH, TOPK)
            BV = AR.room(PH, TOPK)
            BI = AR.room(PH, TOPK)
            AF = AR.room(SLOTS)
            BF = AR.room(SLOTS)
            AI = AR.room(SLOTS)
            ACC = [AR.room(D) for _ in range(2)]
            JK = ACC[1]
            XD = SC.rearrange("p g e -> p (g e)")[:, 0:D]
            TM = SC2.rearrange("p g e -> p (g e)")[:, 0:GBLK]
            IW = AR.room(2 * PH)
            IWI = AR.room(PH).bitcast(I32)
            tables = [ins[n].rearrange("l e d -> (l e) d") for n in ("peer_u", "peer_v")]
            per_layer = [(2 * NT * (SLOTS // GR) + 1) * 16 for j in range(GR)]
            SEGS = 4
            PER = SLOTS // GR // SEGS

            with nc.Block() as block:
                @block.gpsimd
                def _(pool):
                    pool.sem_inc(ring_free, GR - 1)
                    for t in range(NT):
                        pool.wait_ge(dve2pool, 1).then_inc(dve2pool, -1)
                        for which in range(2):
                            with pool.Fori(0, SLOTS // GR) as i:
                                for lot in range(GR // LOT):
                                    pool.wait_ge(ring_free, LOT).then_inc(ring_free, -LOT)
                                    nc.gpsimd.tensor_copy(IS[lot], IDI[:, t, bass.ds(i * GR + lot * LOT, LOT)]).then_inc(pool_own, 1)
                                    pool.wait_ge(pool_own, 1).then_inc(pool_own, -1)
                                    for j in range(LOT):
                                        pool.indirect_dma_start(G_[lot * LOT + j], None, tables[which],
                                                                bass.IndirectOffsetOnAxis(ap=IS[lot][:, j:j + 1], axis=0)).then_inc(gathered[lot * LOT + j], 16)
                    pool.wait_ge(dve2pool, 1).then_inc(dve2pool, -1)
                    pool.wait_ge(ring_free, GR).then_inc(ring_free, -GR)
                    for which in range(2):
                        for j in range(PH):
                            pool.indirect_dma_start(G_[which * PH + j], None, tables[which],
                                                    bass.IndirectOffsetOnAxis(ap=IWI[:, j:j + 1], axis=0)).then_inc(gathered[which * PH + j], 16)

                @block.tensor
                def _(pe):
                    for t in range(TILES):
                        rows = P if t < NT else NB
                        if t >= 1:
                            pe.wait_ge(dve_free, 1).then_inc(dve_free, -1)
                        for h in range(PH):
                            last = pe_.matmul(ps[h // 2][0:rows, (h % 2) * 256:(h % 2) * 256 + 256], QT[:, h, t * P:t * P + rows],
                                              KBD[:, h, :], start=True, stop=True)
                        last.then_inc(pe2act, 1)
                    pe.wait_ge(dve_free, 1).then_inc(dve_free, -1)
                    pe.wait_ge(dve2pe, 1).then_inc(dve2pe, -1)
                    for i in range(2):
                        pe_.matmul(ps[i][:, :], cst("replicate", NB), O[0:NB, NT, i * GBLK:(i + 1) * GBLK], start=True, stop=True)
                    pe_.matmul(ps[2][:, 0:SLOTS], cst("replicate", NB), IDX[0:NB, NT, :], start=True, stop=True)
                    pe_.matmul(ps[3][:, 0:SLOTS], cst("replicate", NB), GT[0:NB, NT, :], start=True, stop=True).then_inc(pe2dve, 1)
                    pe.wait_ge(dve2pe, 1).then_inc(dve2pe, -1)
                    for i in range(2):
                        last = pe_.matmul(ps[4 + i][0:NB, :], cst("gather8"), ACC[0][:, i * GBLK:(i + 1) * GBLK], start=True, stop=True)
                    last.then_inc(pe2dve, 1)

                @block.scalar
                def _(act):
                    def scores(t):
                        rows = P if t < NT else NB
                        act.wait_ge(pe2act, 1).then_inc(pe2act, -1)
                        for i in range(4):
                            last = act_.copy(SC[0:rows, 4 * i:4 * i + 4, :], ps[i][0:rows, :].rearrange("p (a e) -> p a e", a=4))
                        last.then_inc(act2dve, 1)

                    def gate_exp(t):
                        rows = P if t < NT else NB
                        act.wait_ge(dve2act, 1).then_inc(dve2act, -1)
                        act_.activation(GT[0:rows, t, :], GT[0:rows, t, :], ACT.Exp).then_inc(act2dve, 1)

                    scores(0)
                    gate_exp(0)
                    for t in range(NT):
                        scores(t + 1)
                        act.wait_ge(dve2act, 1).then_inc(dve2act, -1)
                        act_.activation(AV, AV, ACT.Gelu).then_inc(act2dve, 1)
                        gate_exp(t + 1)
                    act.wait_ge(dve2act, 1).then_inc(dve2act, -1)
                    act_.activation(A8[:, 0:PH], A8[:, 0:PH], ACT.Gelu).then_inc(act2dve, 1)

                @block.vector
                def _(dve):
                    def choose(t):
                        r = slice(0, P if t < NT else NB)

                        def best(src, spare, val, idx, n):
                            for g in range(n):
                                i_ = vec.max(val[r, g, 0:8], src[r, g, :])
                            i_.then_inc(dve_own, 1)
                            vec.wait_ge(dve_own, 1).then_inc(dve_own, -1)
                            yield
                            for g in range(n):
                                i_ = vec.max_index(idx[r, g, 0:8].bitcast(U32), val[r, g, 0:8], src[r, g, :])
                            i_.then_inc(dve_own, 1)
                            vec.wait_ge(dve_own, 1).then_inc(dve_own, -1)
                            yield
                            for g in range(n):
                                i_ = vec.match_replace(spare[r, g, :], val[r, g, 0:8], src[r, g, :], -3.0e38)
                            i_.then_inc(dve_own, 1)
                            vec.wait_ge(dve_own, 1).then_inc(dve_own, -1)
                            yield
                            for g in range(n):
                                i_ = vec.max(val[r, g, 8:16], spare[r, g, :])
                            i_.then_inc(dve_own, 1)
                            vec.wait_ge(dve_own, 1).then_inc(dve_own, -1)
                            yield
                            for g in range(n):
                                i_ = vec.max_index(idx[r, g, 8:16].bitcast(U32), val[r, g, 8:16], spare[r, g, :])
                            i_.then_inc(dve_own, 1)
                            vec.wait_ge(dve_own, 1).then_inc(dve_own, -1)

                        dve.wait_ge(act2dve, 1).then_inc(act2dve, -1)
                        dve.sem_inc(dve_free, 1)
                        yield from best(SC, SC2, TV, TI, 2 * PH)
                        vec.tensor_copy(TF[r], TI[r].bitcast(U32)).then_inc(dve_own, 1)
                        vec.wait_ge(dve_own, 1).then_inc(dve_own, -1)
                        yield
                        for h in range(PH):
                            i_ = vec.tensor_tensor(CA[r, h, :].rearrange("p (a b) -> p a b", a=TOPK), bc(TV[r, 2 * h, :], 2, TOPK),
                                                   bc(TV[r, 2 * h + 1, :], 1, TOPK), ALU.add)
                        i_.then_inc(dve_own, 1)
                        vec.wait_ge(dve_own, 1).then_inc(dve_own, -1)
                        yield from best(CA, SC3, BV, BI, PH)
                        bi = BI[r].rearrange("p h k -> p (h k)").bitcast(U32)
                        vec.tensor_scalar(AI[r].bitcast(U32), bi, 4, None, ALU.logical_shift_right).then_inc(dve_own, 1)
                        vec.wait_ge(dve_own, 1).then_inc(dve_own, -1)
                        vec.tensor_copy(AF[r], AI[r].bitcast(U32)).then_inc(dve_own, 1)
                        vec.wait_ge(dve_own, 1).then_inc(dve_own, -1)
                        vec.tensor_scalar(AI[r].bitcast(U32), bi, 15, None, ALU.bitwise_and).then_inc(dve_own, 1)
                        vec.wait_ge(dve_own, 1).then_inc(dve_own, -1)
                        vec.tensor_copy(BF[r], AI[r].bitcast(U32)).then_inc(dve_own, 1)
                        vec.wait_ge(dve_own, 1).then_inc(dve_own, -1)
                        for i, pos in enumerate((AF, BF)):
                            yield
                            eq = EQ[r].rearrange("p (m j) -> p m j", j=TOPK)
                            vec.tensor_tensor(eq, bc(pos[r], 2, TOPK), bc(cst("iota16")[r], 1, SLOTS), ALU.is_equal).then_inc(dve_own, 1)
                            vec.wait_ge(dve_own, 1).then_inc(dve_own, -1)
                            for h in range(PH):
                                e_h = EQ[r, h * 256:(h + 1) * 256].rearrange("p (k j) -> p k j", j=TOPK)
                                i_ = vec.tensor_tensor(e_h, e_h, bc(TF[r, 2 * h + i, :], 1, TOPK), ALU.mult)
                            i_.then_inc(dve_own, 1)
                            vec.wait_ge(dve_own, 1).then_inc(dve_own, -1)
                            yield
                            vec.tensor_reduce(pos[r], eq, AX, ALU.add).then_inc(dve_own, 1)
                            vec.wait_ge(dve_own, 1).then_inc(dve_own, -1)
                        vec.scalar_tensor_tensor(IDX[r, t, :], AF[r], float(PK), BF[r], ALU.mult, ALU.add).then_inc(dve_own, 1)
                        vec.wait_ge(dve_own, 1).then_inc(dve_own, -1)
                        vec.tensor_scalar(IDX[r, t, :], IDX[r, t, :], LB[r, 0:1], None, ALU.add).then_inc(dve_own, 1)
                        vec.wait_ge(dve_own, 1).then_inc(dve_own, -1)
                        vec.tensor_copy(IDI[r, t, :], IDX[r, t, :])
                        gt = GT[r, t, :].rearrange("p (h k) -> p h k", h=PH)
                        vec.tensor_tensor(gt, BV[r], bc(BV[r, :, 0], 2, TOPK), ALU.subtract).then_inc(dve2act, 1)
                        yield
                        dve.wait_ge(act2dve, 1).then_inc(act2dve, -1)
                        vec.tensor_reduce(SS[r, 0:PH], gt, AX, ALU.add).then_inc(dve_own, 1)
                        vec.wait_ge(dve_own, 1).then_inc(dve_own, -1)
                        vec.reciprocal(SS[r, 0:PH], SS[r, 0:PH]).then_inc(dve_own, 1)
                        vec.wait_ge(dve_own, 1).then_inc(dve_own, -1)
                        vec.tensor_tensor(gt, gt, bc(SS[r, 0:PH], 2, TOPK), ALU.mult).then_inc(dve2pool if t < NT else dve2pe, 1)

                    for _ in choose(0):
                        pass
                    done = 0
                    for t in range(NT):
                        nxt = choose(t + 1)
                        for seg in range(SEGS):
                            with dve.Fori(seg * PER, (seg + 1) * PER) as i:
                                for j in range(GR):
                                    dve.wait_ge(gathered[j], l * per_layer[j] + (i * 16 + (done + 16)))
                                    vec.tensor_tensor_reduce(G_[j], G_[j], O[:, t, :], 1.0, 0.0, ALU.mult, ALU.add, A8[:, j:j + 1]).then_inc(ring_free, 1)
                                vec.engine_nop().then_inc(dve_own, 1)
                                vec.wait_ge(dve_own, 1).then_inc(dve_own, -1)
                                vec.tensor_copy(AV[:, bass.ds(i * GR, GR)], A8).then_inc(dve_own, 1)
                                vec.wait_ge(dve_own, 1).then_inc(dve_own, -1)
                            next(nxt, None)
                            next(nxt, None)
                        done += SLOTS // GR * 16
                        dve.sem_inc(dve2act, 1)
                        dve.wait_ge(act2dve, 1).then_inc(act2dve, -1)
                        vec.tensor_tensor(AV, AV, GT[:, t, :], ALU.mult)
                        vec.memset(ACC[1], 0.0)
                        vec.memset(ACC[0], 0.0).then_inc(dve_own, 1)
                        vec.wait_ge(dve_own, 1).then_inc(dve_own, -1)
                        for seg in range(SEGS):
                            dve.sem_inc(dve_own, 1)
                            with dve.Fori(seg * PER, (seg + 1) * PER) as i:
                                for j in range(GR):
                                    dve.wait_ge(gathered[j], l * per_layer[j] + (i * 16 + (done + 16)))
                                    a = ACC[j % 2]
                                    vec.scalar_tensor_tensor(a, G_[j], AV[:, bass.ds(i * GR + j, 1)], a, ALU.mult, ALU.add).then_inc(dve_own, 1)
                                    dve.wait_ge(dve_own, 1).then_inc(dve_own, -1)
                                    dve.sem_inc(ring_free, 1)
                            dve.wait_ge(dve_own, 1).then_inc(dve_own, -1)
                            next(nxt, None)
                            next(nxt, None)
                        done += SLOTS // GR * 16
                        vec.tensor_tensor(ACC[0], ACC[0], ACC[1], ALU.add).then_inc(dve_own, 1)
                        vec.wait_ge(dve_own, 1).then_inc(dve_own, -1)
                        vec.tensor_tensor(ACC[0], ACC[0], GP, ALU.mult).then_inc(dve_own, 1)
                        vec.wait_ge(dve_own, 1).then_inc(dve_own, -1)
                        vec.tensor_tensor(X[:, t, :], X[:, t, :], ACC[0], ALU.add).then_inc(dve_own, 1)
                        vec.wait_ge(dve_own, 1).then_inc(dve_own, -1)
                        for _ in nxt:
                            pass
                    dve.sem_inc(ring_free, 1)
                    dve.wait_ge(pe2dve, 1).then_inc(pe2dve, -1)
                    for i in range(2):
                        vec.tensor_copy(XD[:, i * GBLK:(i + 1) * GBLK], ps[i][:, :])
                    sel = bc(cst("slot_of_row"), 1, PH)
                    for i in range(2):
                        v = JK[:, i * SLOTS:(i + 1) * SLOTS].rearrange("p (h k) -> p h k", h=PH)
                        vec.tensor_tensor(v, ps[2 + i][:, 0:SLOTS].rearrange("p (h k) -> p h k", h=PH), sel, ALU.mult).then_inc(dve_own, 1)
                        vec.wait_ge(dve_own, 1).then_inc(dve_own, -1)
                        vec.tensor_reduce(IW[:, i * PH:(i + 1) * PH], v, AX, ALU.add).then_inc(dve_own, 1)
                        vec.wait_ge(dve_own, 1).then_inc(dve_own, -1)
                    vec.tensor_copy(IWI, IW[:, 0:PH]).then_inc(dve2pool, 1)
                    for j in range(PH):
                        dve.wait_ge(gathered[j], l * per_layer[j] + (done + 16))
                        i_ = vec.tensor_tensor_reduce(G_[j], G_[j], XD, 1.0, 0.0, ALU.mult, ALU.add, A8[:, j:j + 1])
                    i_.then_inc(dve2act, 1)
                    dve.wait_ge(act2dve, 1).then_inc(act2dve, -1)
                    vec.tensor_tensor(A8[:, 0:PH], A8[:, 0:PH], IW[:, PH:2 * PH], ALU.mult).then_inc(dve_own, 1)
                    vec.wait_ge(dve_own, 1).then_inc(dve_own, -1)
                    vec.memset(ACC[0], 0.0).then_inc(dve_own, 1)
                    vec.wait_ge(dve_own, 1).then_inc(dve_own, -1)
                    for j in range(PH):
                        dve.wait_ge(gathered[PH + j], l * per_layer[PH + j] + (done + 16))
                        vec.scalar_tensor_tensor(ACC[0], G_[PH + j], A8[:, j:j + 1], ACC[0], ALU.mult, ALU.add).then_inc(dve_own, 1)
                        vec.wait_ge(dve_own, 1).then_inc(dve_own, -1)
                    dve.sem_inc(dve2pe, 1)
                    dve.wait_ge(pe2dve, 1).then_inc(pe2dve, -1)
                    for i in range(2):
                        c = slice(i * GBLK, (i + 1) * GBLK)
                        vec.tensor_tensor(TM[0:NB, :], ps[4 + i][0:NB, :], MOD9[0:NB, 5 * D + i * GBLK:5 * D + (i + 1) * GBLK], ALU.mult).then_inc(dve_own, 1)
                        vec.wait_ge(dve_own, 1).then_inc(dve_own, -1)
                        vec.tensor_tensor(X[0:NB, NT, c], X[0:NB, NT, c], TM[0:NB, :], ALU.add).then_inc(dve_own, 1)
                        vec.wait_ge(dve_own, 1).then_inc(dve_own, -1)
                    vec.tensor_scalar(LB, LB, float(EXPERTS), None, ALU.add)
            AR.at = mark

        nc_page_table = AR.room(NB * PAGES, rows=1).bitcast(I32)
        with nc.Block() as block:
            @block.sync
            def _(sp):
                sp.dma_start(nc_page_table, ins["page_table"].rearrange("b j -> (b j)").unsqueeze(0)).then_inc(loaded, 16)
                sp.wait_ge(loaded, 16).then_inc(loaded, -16)

        with nc.Fori(0, DEPTH) as l:
            mark = AR.at
            modulation(l)
            G = AR.room(2 * TILES, NH).rearrange("p (c t) h -> p c t h", c=2)
            PZ = AR.room(TILES, NH * DK)
            BA = AR.room(TILES, 8)
            of_b = AR.at
            BT = AR.room(CC, SEQ + 3)
            DB = AR.room(CONV_CH)
            inner = AR.at
            PC = AR.room(TILES, 3 * AW)
            inner3 = AR.at
            PA = AR.room(TILES, 3 * AW)
            inner2 = AR.at
            with nc.Block() as block:
                @block.gpsimd
                def _(pool):
                    for a in (PA, PC, PZ, BA, O):
                        nc.gpsimd.memset(a[:, NT, :], 0.0)
            HT = AR.room(KD, SEQ + NB)
            W = [AR.room(KD, GBLK) for _ in range(2)]

            def first_w_in(sp):
                for n in range(2):
                    sp.dma_start(*w_in_tile(l, W, n)).then_inc(w_landed[n], 16)

            norm(0, HT, first_w_in, of_b)
            project(l, HT, W, PA, PC, PZ, BA, BT, DB)
            AR.at = inner2
            heads_of_a_and_c(l, PA, PC)
            QT = AR.room(8, SEQ)
            transpose_heads(PA, PC, QT)
            attend_a(QT, PA)
            attend_c(QT, PC)
            AR.at = inner2
            windows_sample(l, PA, PC)
            AR.at = inner3
            sticks_sample(l, PC)
            AR.at = inner
            gates(l, BA, G)
            delta_sample(l, DB, G)
            delta_prompt(l, BT, G, PZ)
            W_OUT = AR.room(KD, D)
            gated_norm(l, PZ, W_OUT)
            AR.at = mark
            out_projection(W_OUT)
            peer(l)
            AR.at = mark

        with nc.Block() as block:
            @block.sync
            def _(sp):
                sp.dma_start(outs["y_prompt"][0].rearrange("(t p) d -> p t d", p=P), X[:, 0:NT, :]).then_inc(stored, 16)
                sp.dma_start(outs["y_sample"].rearrange("b s d -> (b s) d"), X[0:NB, NT, :]).then_inc(stored, 16)
                sp.wait_ge(stored, 32).then_inc(stored, -32)


_INS = ["x_prompt", "x_sample", "cache_win_k", "cache_win_v", "cache_sb_k", "cache_sb_v", "state_conv", "state_delta",
        "page_table", "c_prompt", "c_sample", "w_ada", "b_ada", "norm1_g", "norm2_g", "w_in", "b_q_c", "b_k_c",
        "qnorm_a", "knorm_a", "conv_w", "a_log", "dt_bias", "gnorm_b", "w_out", "peer_wq", "peer_keys", "peer_u", "peer_v"]
_OUTS = [("y_prompt", (1, SEQ, D)), ("y_sample", (NB, 1, D)),
         ("win_k_prompt", (DEPTH, 1, SEQ, NH, HD)), ("win_v_prompt", (DEPTH, 1, SEQ, NH, HD)),
         ("win_k_sample", (DEPTH, NB, 1, NH, HD)), ("win_v_sample", (DEPTH, NB, 1, NH, HD)),
         ("sb_k_prompt", (DEPTH, 1, SEQ, NH, HD)), ("sb_v_prompt", (DEPTH, 1, SEQ, NH, HD)),
         ("sb_k_sample", (DEPTH, NB, 1, NH, HD)), ("sb_v_sample", (DEPTH, NB, 1, NH, HD)),
         ("conv_prompt", (DEPTH, 1, KW - 1, CONV_CH)), ("conv_sample", (DEPTH, NB, KW - 1, CONV_CH)),
         ("delta_prompt", (DEPTH, 1, NH, DK, DK)), ("delta_sample", (DEPTH, NB, NH, DK, DK))]


def kernel(**inputs):
    import numpy as _np
    import concourse.bacc as _bacc
    from concourse import mybir as _mybir
    from concourse.bass_utils import run_bass_kernel_spmd as _run

    nc = _bacc.Bacc("TRN2", target_bir_lowering=False, num_devices=1)
    arrays, ins, outs = {}, {}, {}
    for name in _INS + ["consts"]:
        a = constants() if name == "consts" else _np.ascontiguousarray(inputs[name])
        arrays[f"in_{name}_dram"] = a
        ins[name] = nc.dram_tensor(f"in_{name}_dram", a.shape, _mybir.dt.from_np(a.dtype), kind="ExternalInput").ap()
    for name, shape in _OUTS:
        outs[name] = nc.dram_tensor(f"out_{name}_dram", shape, _mybir.dt.from_np(_np.dtype("float32")), kind="ExternalOutput").ap()
    build(nc, ins, outs)
    r = _run(nc, [arrays], core_ids=[0])
    return tuple(r.results[0][f"out_{name}_dram"] for name, _ in _OUTS)
```
